# Optimizing a Trainium2 kernel written in Bass

```python
import jax, jax.numpy as jnp
from jax import lax
import numpy as np

D_MODEL = 2048
BATCH = 1
SEQ = 256
DEPTH = 2

MIX = D_MODEL
HALF = MIX // 2
HEAD_DIM = 128
N_HEADS = HALF // HEAD_DIM
POOL_WINDOWS = (2, 4, 8, 16)
POOL_GROUPS = len(POOL_WINDOWS)
POOL_GW = HALF // POOL_GROUPS
MOBA_BLOCK = 256
MOBA_TOPK = 3
MOBA_Q_CHUNK = 64
DSA_TOPK_MAX = 256
DSA_IDX_HEADS = 8
DSA_IDX_DIM = 64
DSA_Q_CHUNK = 128
CONV_WIDTH = 31
N_EVEN = (DEPTH + 1) // 2
N_ODD = DEPTH // 2
EVEN_WIDTHS = (HALF, HALF, HALF, HALF, MIX)
EVEN_IN = 4 * HALF + MIX
ODD_WIDTHS = (HALF, HALF, HALF, DSA_IDX_HEADS * DSA_IDX_DIM, DSA_IDX_HEADS, DSA_IDX_DIM, HALF, HALF, MIX)
ODD_IN = 5 * HALF + DSA_IDX_HEADS * DSA_IDX_DIM + DSA_IDX_HEADS + DSA_IDX_DIM + MIX
EPS = 1e-6
NEG_INF = -1e30

kernel_name = 'hybrid_pool_moba_dsa_conformer_trunk'

def _offsets(widths):
    out, s = [], 0
    for w in widths[:-1]:
        s += w
        out.append(s)
    return out

def _rms(x, g):
    x32 = x.astype(jnp.float32)
    y = x32 * lax.rsqrt(jnp.mean(x32 * x32, axis=-1, keepdims=True) + EPS)
    return (y * g.astype(jnp.float32)).astype(x.dtype)

def _alibi_slopes(n):
    return jnp.exp2(-8.0 * jnp.arange(1, n + 1, dtype=jnp.float32) / n)

def _pool_mixer(u, pool_w, pool_scale):
    S = u.shape[1]
    u32 = u.astype(jnp.float32)
    cs = jnp.cumsum(u32, axis=1)
    t1 = jnp.arange(1, S + 1, dtype=jnp.float32)[None, :, None]
    outs = []
    for g, w in enumerate(POOL_WINDOWS):
        sl = slice(g * POOL_GW, (g + 1) * POOL_GW)
        csg = cs[:, :, sl]
        prev = jnp.pad(csg, ((0, 0), (w, 0), (0, 0)))[:, :S]
        mean = (csg - prev) / jnp.minimum(t1, float(w))
        outs.append(mean - u32[:, :, sl])
    d = jnp.stack(outs, axis=2).astype(u.dtype)
    y = jnp.einsum('bsgc,gcd->bsgd', d, pool_w).reshape(u.shape)
    return y * pool_scale

def _moba_attention(q, k, v):
    B_, S, H, Dh = q.shape
    nb = -(-S // MOBA_BLOCK)
    s_pad = nb * MOBA_BLOCK
    pad = ((0, 0), (0, s_pad - S), (0, 0), (0, 0))
    kb = jnp.pad(k, pad).reshape(B_, nb, MOBA_BLOCK, H, Dh).transpose(0, 3, 1, 2, 4)
    vb = jnp.pad(v, pad).reshape(B_, nb, MOBA_BLOCK, H, Dh).transpose(0, 3, 1, 2, 4)
    kmean = jnp.mean(kb.astype(jnp.float32), axis=3)
    n_sel = max(1, min(MOBA_TOPK, nb - 1))
    slopes = _alibi_slopes(H)[None, :, None, None]
    scale = Dh ** -0.5
    bi = jnp.arange(B_)[:, None, None, None]
    hi = jnp.arange(H)[None, :, None, None]
    blk_ids = jnp.arange(nb)
    in_blk = jnp.arange(MOBA_BLOCK)
    rank = jnp.arange(n_sel)

    def chunk(ci):
        t0 = ci * MOBA_Q_CHUNK
        tq = t0 + jnp.arange(MOBA_Q_CHUNK)
        qc = lax.dynamic_slice_in_dim(q, t0, MOBA_Q_CHUNK, axis=1).transpose(0, 2, 1, 3)
        qc32 = qc.astype(jnp.float32)
        own = t0 // MOBA_BLOCK
        k_own = lax.dynamic_index_in_dim(kb, own, axis=2, keepdims=False)
        v_own = lax.dynamic_index_in_dim(vb, own, axis=2, keepdims=False)
        dist_own = (tq[:, None] - (own * MOBA_BLOCK + in_blk)[None, :]).astype(jnp.float32)
        s_own = jnp.einsum('bhqd,bhkd->bhqk', qc32, k_own.astype(jnp.float32)) * scale - slopes * dist_own
        s_own = jnp.where(dist_own >= 0, s_own, NEG_INF)
        gsc = jnp.einsum('bhqd,bhnd->bhqn', qc32, kmean)
        gsc = jnp.where(blk_ids < own, gsc, NEG_INF)
        _, idx = lax.top_k(gsc, n_sel)
        valid = rank < own
        k_sel = kb[bi, hi, idx]
        v_sel = vb[bi, hi, idx]
        pos_sel = idx[..., None] * MOBA_BLOCK + in_blk
        dist_sel = (tq[None, None, :, None, None] - pos_sel).astype(jnp.float32)
        s_sel = jnp.einsum('bhqd,bhqrkd->bhqrk', qc32, k_sel.astype(jnp.float32)) * scale - slopes[..., None] * dist_sel
        s_sel = jnp.where(valid[:, None], s_sel, NEG_INF).reshape(B_, H, MOBA_Q_CHUNK, n_sel * MOBA_BLOCK)
        p = jax.nn.softmax(jnp.concatenate([s_own, s_sel], axis=-1), axis=-1)
        p_own = p[..., :MOBA_BLOCK]
        p_sel = p[..., MOBA_BLOCK:].reshape(B_, H, MOBA_Q_CHUNK, n_sel, MOBA_BLOCK)
        o = (jnp.einsum('bhqk,bhkd->bhqd', p_own, v_own.astype(jnp.float32))
             + jnp.einsum('bhqrk,bhqrkd->bhqd', p_sel, v_sel.astype(jnp.float32)))
        return o.astype(q.dtype).transpose(0, 2, 1, 3)

    out = lax.map(chunk, jnp.arange(S // MOBA_Q_CHUNK))
    return out.transpose(1, 0, 2, 3, 4).reshape(B_, S, H * Dh)

def _dsa_attention(q, k, v, qi, wi, ki):
    B_, S, H, Dh = q.shape
    n_sel = min(DSA_TOPK_MAX, S // 4)
    slopes = _alibi_slopes(H)[None, :, None, None]
    scale = Dh ** -0.5
    idx_scale = DSA_IDX_DIM ** -0.5
    bi = jnp.arange(B_)[:, None, None]
    pos = jnp.arange(S)

    def chunk(ci):
        t0 = ci * DSA_Q_CHUNK
        tq = t0 + jnp.arange(DSA_Q_CHUNK)
        qic = lax.dynamic_slice_in_dim(qi, t0, DSA_Q_CHUNK, axis=1).astype(jnp.float32)
        wic = lax.dynamic_slice_in_dim(wi, t0, DSA_Q_CHUNK, axis=1).astype(jnp.float32)
        logits = jax.nn.relu(jnp.einsum('bqhd,bsd->bqhs', qic, ki.astype(jnp.float32)) * idx_scale)
        score = jnp.einsum('bqh,bqhs->bqs', wic, logits)
        score = jnp.where(pos[None, None, :] <= tq[None, :, None], score, NEG_INF)
        _, idx = lax.top_k(score, n_sel)
        valid = idx <= tq[None, :, None]
        k_sel = k[bi, idx]
        v_sel = v[bi, idx]
        qc = lax.dynamic_slice_in_dim(q, t0, DSA_Q_CHUNK, axis=1).astype(jnp.float32)
        s = jnp.einsum('bqhd,bqkhd->bhqk', qc, k_sel.astype(jnp.float32)) * scale
        dist = (tq[None, :, None] - idx).astype(jnp.float32)[:, None]
        s = jnp.where(valid[:, None], s - slopes * dist, NEG_INF)
        p = jax.nn.softmax(s, axis=-1)
        o = jnp.einsum('bhqk,bqkhd->bqhd', p, v_sel.astype(jnp.float32))
        return o.astype(q.dtype)

    out = lax.map(chunk, jnp.arange(S // DSA_Q_CHUNK))
    return out.transpose(1, 0, 2, 3, 4).reshape(B_, S, H * Dh)

def _conv_module(a, b, conv_w, conv_b, ln_g, ln_b):
    u = a * jax.nn.sigmoid(b)
    y = lax.conv_general_dilated(u, conv_w[:, None, :].astype(u.dtype), window_strides=(1,),
                                 padding=[(CONV_WIDTH - 1, 0)],
                                 dimension_numbers=('NWC', 'WIO', 'NWC'),
                                 feature_group_count=HALF)
    y32 = (y + conv_b).astype(jnp.float32)
    mu = jnp.mean(y32, axis=-1, keepdims=True)
    var = jnp.mean(jnp.square(y32 - mu), axis=-1, keepdims=True)
    y32 = (y32 - mu) * lax.rsqrt(var + EPS) * ln_g.astype(jnp.float32) + ln_b.astype(jnp.float32)
    return jax.nn.silu(y32).astype(a.dtype)

def setup_inputs(seed: int = 0) -> dict:
    key = jax.random.key(seed)
    ks = jax.random.split(key, 18)
    f32 = jnp.float32

    def nrm(k, shape, s):
        return jax.random.normal(k, shape, f32) * s

    return {
        'x': nrm(ks[0], (BATCH, SEQ, D_MODEL), 1.0),
        'c': nrm(ks[1], (BATCH, D_MODEL), 1.0),
        'norm_g': 1.0 + nrm(ks[2], (DEPTH, D_MODEL), 0.02),
        'ada_w': nrm(ks[3], (DEPTH, D_MODEL, 3 * D_MODEL), 0.5 * D_MODEL ** -0.5),
        'ada_b': nrm(ks[4], (DEPTH, 3 * D_MODEL), 0.02),
        'w_out': nrm(ks[5], (DEPTH, MIX, D_MODEL), MIX ** -0.5),
        'ev_w_in': nrm(ks[6], (N_EVEN, D_MODEL, EVEN_IN), D_MODEL ** -0.5),
        'pool_w': nrm(ks[7], (N_EVEN, POOL_GROUPS, POOL_GW, POOL_GW), POOL_GW ** -0.5),
        'pool_scale': 1.0 + nrm(ks[8], (N_EVEN, HALF), 0.1),
        'moba_qn': 1.0 + nrm(ks[9], (N_EVEN, HEAD_DIM), 0.02),
        'moba_kn': 1.0 + nrm(ks[10], (N_EVEN, HEAD_DIM), 0.02),
        'od_w_in': nrm(ks[11], (N_ODD, D_MODEL, ODD_IN), D_MODEL ** -0.5),
        'dsa_qn': 1.0 + nrm(ks[12], (N_ODD, HEAD_DIM), 0.02),
        'dsa_kn': 1.0 + nrm(ks[13], (N_ODD, HEAD_DIM), 0.02),
        'conv_w': nrm(ks[14], (N_ODD, CONV_WIDTH, HALF), CONV_WIDTH ** -0.5),
        'conv_b': nrm(ks[15], (N_ODD, HALF), 0.02),
        'conv_ln_g': 1.0 + nrm(ks[16], (N_ODD, HALF), 0.02),
        'conv_ln_b': nrm(ks[17], (N_ODD, HALF), 0.02),
    }

def reference(x, c, norm_g, ada_w, ada_b, w_out, ev_w_in, pool_w, pool_scale, moba_qn, moba_kn,
              od_w_in, dsa_qn, dsa_kn, conv_w, conv_b, conv_ln_g, conv_ln_b):
    B_, S, _ = x.shape
    c_act = jax.nn.silu(c)
    for l in range(DEPTH):
        mod = c_act @ ada_w[l] + ada_b[l]
        shift, scl, gate_res = jnp.split(mod[:, None, :], 3, axis=-1)
        h = _rms(x, norm_g[l]) * (1.0 + scl) + shift
        if l % 2 == 0:
            e = l // 2
            z = h @ ev_w_in[e]
            u_a, q, k, v, g = jnp.split(z, _offsets(EVEN_WIDTHS), axis=-1)
            q = _rms(q.reshape(B_, S, N_HEADS, HEAD_DIM), moba_qn[e])
            k = _rms(k.reshape(B_, S, N_HEADS, HEAD_DIM), moba_kn[e])
            v = v.reshape(B_, S, N_HEADS, HEAD_DIM)
            y = jnp.concatenate([_pool_mixer(u_a, pool_w[e], pool_scale[e]),
                                 _moba_attention(q, k, v)], axis=-1)
        else:
            o = l // 2
            z = h @ od_w_in[o]
            q, k, v, qi, wi, ki, ga, gb, g = jnp.split(z, _offsets(ODD_WIDTHS), axis=-1)
            q = _rms(q.reshape(B_, S, N_HEADS, HEAD_DIM), dsa_qn[o])
            k = _rms(k.reshape(B_, S, N_HEADS, HEAD_DIM), dsa_kn[o])
            v = v.reshape(B_, S, N_HEADS, HEAD_DIM)
            qi = qi.reshape(B_, S, DSA_IDX_HEADS, DSA_IDX_DIM)
            wi = wi * (DSA_IDX_HEADS ** -0.5)
            y = jnp.concatenate([_dsa_attention(q, k, v, qi, wi, ki),
                                 _conv_module(ga, gb, conv_w[o], conv_b[o], conv_ln_g[o], conv_ln_b[o])], axis=-1)
        x = x + gate_res * ((y * jax.nn.silu(g)) @ w_out[l])
    return x


_drawn_inputs = setup_inputs


def setup_inputs(seed=0):
    import zlib

    import numpy as np

    out = dict(_drawn_inputs(seed))
    spreads = {}
    factors = {'norm_g': 5.089,
     'ada_b': 2.986,
     'pool_scale': 3.602,
     'moba_qn': 8.0,
     'moba_kn': 8.0,
     'dsa_qn': 8.0,
     'dsa_kn': 8.0,
     'conv_b': 8.0,
     'conv_ln_g': 8.0,
     'conv_ln_b': 8.0}
    for name, (base, spread) in spreads.items():
        noise = np.random.default_rng([zlib.crc32(name.encode()), seed]).standard_normal(out[name].shape)
        drawn = base * np.exp(spread * noise) if base else spread * noise
        out[name] = __import__('jax').numpy.asarray(drawn.astype(out[name].dtype))
    for name, factor in factors.items():
        out[name] = (out[name] * factor).astype(out[name].dtype)
    return out
```

```python
from contextlib import ExitStack

import concourse.bass as bass
from concourse import mybir

F32 = mybir.dt.float32
F32R = mybir.dt.float32r
ALU = mybir.AluOpType
ACT = mybir.ActivationFunctionType
AX_X = mybir.AxisListType.X

P = 128
D_MODEL = 2048
SEQ = 256
HALF = D_MODEL // 2
KC = D_MODEL // P
HC = HALF // P
QT = SEQ // P
EPS = 1e-6
BIG = 2.56e32
NEG_INF = -1e30
DSA_SEL = SEQ // 4
IDX_HEADS = 8
IDX_DIM = 64
CONV_WIDTH = 31
PAD = CONV_WIDTH - 1
KEYS = P + SEQ

U0, Q0, V0, G0, O0 = 0, 8, 24, 32, 48
AB1, QI1, KW1, Q1, V1, G1, O1 = 64, 80, 84, 85, 101, 109, 125
N_SLABS = 141
AHEAD = 2

PIECE = 1024
UNITS = D_MODEL // P
PIECES = [(0, 0), (0, 1), (0, 2), (0, 3), (1, 0), (1, 1), (1, 2), (0, 4), (0, 5), (1, 3), (1, 4), (1, 5)]
PIECE_STEP = {4: 0, 5: 8, 6: 16, 7: 40, 8: 48, 9: 56, 10: 117, 11: 125}
SHIFT = {0: (0, 1), 1: (4, 5)}
SCALE = {0: (2, 3), 1: (6, 9)}
GATE = {0: 7, 1: 10}

C_C = 0
C_NORM = C_C + KC
C_ADAB = C_NORM + 2 * KC
C_PSC = C_ADAB + len(PIECES) * HC
C_QK = C_PSC + HC
C_CW = C_QK + 4
C_CB = C_CW + HC * CONV_WIDTH
C_LG = C_CB + HC
C_LB = C_LG + HC
N_PAR = C_LB + HC


def units_at(w):
    for piece, w0 in PIECE_STEP.items():
        if w0 <= w < w0 + UNITS // 2:
            return UNITS * piece + 2 * (w - w0)
    return None


def conv_plan():
    ops = [(2 * m + s, k) for m in range(HC // 2) for k in range(CONV_WIDTH) for s in range(2)]
    plan, n = {}, 0
    for w in range(68, 111):
        take = 8 if w <= 84 else 5 if w <= 100 else 2 if w <= 108 else 8
        plan[w] = ops[n:n + take]
        for j, _ in plan[w]:
            assert w > AB1 + 2 * j + 1
        n += take
    assert n >= len(ops)
    return plan


def build(nc, xT, params, pool_w, w_slabs, ada_units, x1_dram, outT):
    ctx = ExitStack()
    with ctx:
        def sb(name, shape, dt=F32):
            return ctx.enter_context(nc.sbuf_tensor(name, shape, dt))

        def sem(name):
            return ctx.enter_context(nc.semaphore(name))

        raw = sb("raw", [P, 4, 8, P])
        whi = sb("whi", [P, 4, 8, P], F32R)
        wlo = sb("wlo", [P, 4, 8, P], F32R)
        ada = sb("ada", [P, 4, PIECE])
        acc = sb("acc", [P, 2, PIECE])
        hhi = sb("hhi", [P, KC, SEQ], F32R)
        hlo = sb("hlo", [P, KC, SEQ], F32R)
        ghi = sb("ghi", [P, KC, SEQ], F32R)
        glo = sb("glo", [P, KC, SEQ], F32R)
        X = sb("X", [P, KC, SEQ])
        V = sb("V", [P, QT, HALF])
        Y = sb("Y", [P, HC, SEQ])
        U = sb("U", [P, HC, PAD + SEQ])
        T = sb("T", [P, 2, SEQ])
        SG = sb("SG", [P, 2, SEQ])
        SP = sb("SP", [P, 2, KEYS])
        PTs = sb("PTs", [P, 2, KEYS])
        PD = sb("PD", [P, 2, QT, P])
        KD = sb("KD", [P, QT, P])
        D = sb("D", [P, KEYS])
        MK = sb("MK", [P, KEYS])
        DS = sb("DS", [P, 2, KEYS])
        ident = sb("ident", [P, P])
        ones = sb("ones", [P, P])
        QI = sb("QI", [P, IDX_HEADS // 2, SEQ])
        KW = sb("KW", [P, SEQ])
        KI = sb("KI", [P, SEQ])
        par = sb("par", [P, N_PAR])
        cact = sb("cact", [P, KC])
        ctmp = sb("ctmp", [P, KC])
        mod = sb("mod", [P, len(PIECES) * HC])
        hgain = sb("hgain", [P, KC])
        st = sb("st", [P, 5, 2 * KC])
        rr = sb("rr", [P, 2 * KC])
        nm = sb("nm", [P, 2, QT])
        ls = sb("ls", [P, 2, QT])
        rl = sb("rl", [P, 2, QT])
        m8 = sb("m8", [P, QT, 8])
        wi = sb("wi", [P, QT, IDX_HEADS])
        lnh = sb("lnh", [P, 2 * HC])
        qgain = sb("qgain", [P, 2])
        rc = sb("rc", [P, 16])
        psum = [ctx.enter_context(nc.psum_tensor(f"bank{i}", [P, 512], F32)) for i in range(8)]
        Z, S, PT, O, M, XB = psum[0:2], psum[2:4], psum[4], psum[5], psum[6], psum[7]
        PW = V[:].rearrange("p a (b c) -> p (a b) c", c=512).rearrange("p g (k n) -> p g k n", k=2)
        poolA, poolB = (t[:].rearrange("p a b -> p (a b)")[:, 0:2 * (SEQ + 16)].rearrange("p (c t) -> p c t", c=2)
                        for t in (SP, PTs))

        par_in, x_in, pw_in = sem("par_in"), sem("x_in"), sem("pw_in")
        raw_in = [sem(f"raw_in{i}") for i in range(4)]
        ada_in = [sem(f"ada_in{i}") for i in range(4)]
        hi_done = sem("hi_done")
        lo_done = sem("lo_done")
        pe_half = sem("pe_half")
        z_free = [sem(f"z_free{i}") for i in range(2)]
        ada_done = sem("ada_done")
        acc_zero = sem("acc_zero")
        mod_sum = sem("mod_sum")
        mod_done = sem("mod_done")
        cexp = sem("cexp")
        const = sem("const")
        pool_self = sem("pool_self")
        dve_seq = sem("dve_seq")
        act_seq = sem("act_seq")
        sq_done = sem("sq_done")
        stat_done = sem("stat_done")
        var_ready = sem("var_ready")
        root_done = sem("root_done")
        diag_ready = sem("diag_ready")
        spread = sem("spread")
        xr_done = sem("xr_done")
        h_done = sem("h_done")
        hhi_done = sem("hhi_done")
        hlo_done = sem("hlo_done")
        qk_stat = sem("qk_stat")
        tanh_done = sem("tanh_done")
        gated = sem("gated")
        ghi_done, glo_done = sem("ghi_done"), sem("glo_done")
        gain_ready = sem("gain_ready")
        xr_in = [sem(f"xr_in{i}") for i in range(2)]
        store = [sem(f"store{i}") for i in range(4)]
        d_ready, pool_mm, pool_out = sem("d_ready"), sem("pool_mm"), sem("pool_out")
        vt_done, v_copied = sem("vt_done"), sem("v_copied")
        kdiag, kb_done, kmul = sem("kdiag"), sem("kb_done"), sem("kmul")
        ds_ready, scored, s_added, max_done = sem("ds_ready"), sem("scored"), sem("s_added"), sem("max_done")
        exp_done, pdiag, pt_done, pt_copied = sem("exp_done"), sem("pdiag"), sem("pt_done"), sem("pt_copied")
        pv_done, o_copied = sem("pv_done"), sem("o_copied")
        u_done = sem("u_done")
        wt_done, wi_ready = sem("wt_done"), sem("wi_ready")
        ki_in, cm_ready = sem("ki_in"), sem("cm_ready")
        logit, relu, score, mask_ready = sem("logit"), sem("relu"), sem("score"), sem("mask_ready")
        conv_seq = sem("conv_seq")
        mean_mm, ln_sub, ln_sq, var_mm = sem("mean_mm"), sem("ln_sub"), sem("ln_sq"), sem("var_mm")
        ln_mul, ln_act, ln_out = sem("ln_mul"), sem("ln_act"), sem("ln_out")

        N_TAPS = HC * CONV_WIDTH
        block = ctx.enter_context(nc.Block())

        def run(eng, w0, w1, step):
            with eng.Fori(0, (w1 - w0) // 2) as t:
                step(w0, t)
                step(w0 + 1, t)
            if (w1 - w0) % 2:
                step(w1 - 1, None)

        def now(w, t):
            return w if t is None else w + 2 * t

        def half_slot(w, half):
            return (2 * w + half) % 4

        def half_uses(w, half, t):
            n = (2 * w + half) // 4 + 1
            return n if t is None else n + t

        def x_written(eng, layer, count):
            last = (O0, O1)[layer] + count - 1
            for w in (last - 1, last):
                eng.wait_ge(z_free[w % 2], w // 2 + 2)

        def bank_uses(w, t):
            return w // 2 if t is None else w // 2 + t

        @block.sync
        def _(sp):
            sp.sem_inc(lo_done, 4)
            sp.sem_inc(ada_done, 4)
            sp.dma_start(par[:], params).then_inc(par_in, 16)
            sp.dma_start(X[:], xT).then_inc(x_in, 16)

            def load_units(n, t):
                for u in range(2):
                    slot = (n + u) % 4
                    unit = n + u if t is None else n + u + 4 * t
                    sp.wait_ge(ada_done, unit + 1)
                    sp.dma_start(ada[:, slot, :], ada_units[bass.ds(unit, 1)].rearrange("a p n -> p (a n)"))\
                      .then_inc(ada_in[slot], 16)

            def load_slab(w, t):
                for half in range(2):
                    slot = half_slot(w, half)
                    sp.wait_ge(lo_done, 2 * now(w, t) + half + 1)
                    sp.dma_start(raw[:, slot], w_slabs[bass.ds(now(w, t), 1), :, 8 * half:8 * half + 8, :]
                                 .rearrange("a p k n -> p (a k) n")).then_inc(raw_in[slot], 16)

            load_units(0, None)
            load_units(2, None)
            with sp.Fori(0, 11) as t:
                load_units(4, t)
                load_units(6, t)
            load_slab(0, None)
            load_slab(1, None)
            with sp.Fori(0, 4) as t:
                load_units(48, t)
                load_units(50, t)

            def step(w, t):
                load_slab(w + 2, t)
                if units_at(w) is not None:
                    load_units(units_at(w), t)

            for w0, w1 in ((0, 24), (24, 40), (40, 64), (64, 117), (117, 133), (133, N_SLABS - 2)):
                run(sp, w0, w1, step)

        @block.gpsimd
        def _(pool):
            n = [0]

            def own(ins):
                n[0] += 1
                ins.then_inc(pool_self, 1)
                pool.wait_ge(pool_self, n[0])

            pool.dma_start(PW, pool_w).then_inc(pw_in, 16)
            pool.memset(acc[:, 0, :], 0.0).then_inc(acc_zero, 1)
            pool.memset(acc[:, 1, :], 0.0).then_inc(acc_zero, 1)
            pool.memset(ones[:], 1.0).then_inc(const, 1)
            own(pool.memset(ident[:], 0.0))
            pool.affine_select(out=ident[:], in_=ident[:], compare_op=ALU.not_equal, fill=1.0, base=0,
                               pattern=[[-1, P]], channel_multiplier=1).then_inc(const, 1)
            pool.memset(U[:, :, 0:PAD], 0.0).then_inc(const, 1)
            pool.iota(rc[:], pattern=[[1, 16]], base=1, channel_multiplier=0,
                      allow_small_or_imprecise_dtypes=True).then_inc(const, 1)
            for c0, c1, q0 in ((0, P, 0), (P, KEYS, P)):
                own(pool.iota(D[:, c0:c1], pattern=[[1, c1 - c0]], base=-q0, channel_multiplier=-1,
                              allow_small_or_imprecise_dtypes=True))
                own(pool.affine_select(out=D[:, c0:c1], in_=D[:, c0:c1], compare_op=ALU.is_ge, fill=-BIG,
                                       base=q0, pattern=[[-1, c1 - c0]], channel_multiplier=1))

            def clear(piece):
                pool.wait_ge(mod_sum, piece - 1)
                pool.memset(acc[:, piece % 2, :], 0.0).then_inc(acc_zero, 1)

            def slopes(layer):
                mask = D if layer == 0 else MK
                for h in range(HC):
                    a = HC * layer + h
                    if a >= 2:
                        pool.wait_ge(s_added, a - 1)
                    pool.tensor_scalar(DS[:, a % 2, :], mask[:], 2.0 ** -(h + 1), None, ALU.mult)\
                        .then_inc(ds_ready, 1)

            def load_x(layer, m):
                src = xT if layer == 0 else x1_dram
                if m < 2:
                    pool.wait_ge(glo_done, KC * (layer + 1))
                else:
                    x_written(pool, layer, 4 * (m - 1))
                pool.dma_start(Y[:, 4 * (m % 2):4 * (m % 2) + 4, :], src[:, 4 * m:4 * m + 4, :])\
                    .then_inc(xr_in[m % 2], 16)

            def store_x(layer, m):
                x_written(pool, layer, 4 * (m + 1))
                pool.dma_start((x1_dram if layer == 0 else outT)[:, 4 * m:4 * m + 4, :],
                               X[:, 4 * m:4 * m + 4, :]).then_inc(store[m], 16)

            clear(2)
            clear(3)
            clear(4)
            clear(5)
            clear(6)
            slopes(0)
            pool.wait_ge(pv_done, HC)
            own(pool.memset(PTs[:, 0, :], 0.0))
            for c0, c1, q0 in ((0, P, 0), (P, KEYS, P)):
                pool.affine_select(out=PTs[:, 0, c0:c1], in_=PTs[:, 0, c0:c1], compare_op=ALU.is_ge,
                                   fill=NEG_INF, base=q0, pattern=[[-1, c1 - c0]],
                                   channel_multiplier=1).then_inc(cm_ready, 1)
            clear(7)
            load_x(0, 0)
            load_x(0, 1)
            clear(8)
            store_x(0, 0)
            load_x(0, 2)
            clear(9)
            store_x(0, 1)
            load_x(0, 3)
            store_x(0, 2)
            store_x(0, 3)
            clear(10)
            clear(11)
            pool.wait_ge(z_free[KW1 % 2], KW1 // 2 + 2)
            pool.dma_start(KI[IDX_DIM:2 * IDX_DIM, :], KW[0:IDX_DIM, :]).then_inc(ki_in, 16)
            pool.wait_ge(mask_ready, 1)
            slopes(1)
            for m in range(4):
                pool.wait_ge(store[m], 16)
            load_x(1, 0)
            load_x(1, 1)
            store_x(1, 0)
            load_x(1, 2)
            store_x(1, 1)
            load_x(1, 3)
            store_x(1, 2)
            store_x(1, 3)
            for m in range(4):
                pool.wait_ge(store[m], 32)

        @block.scalar
        def _(act):
            act.sem_inc(pe_half, 4)
            n = [0]

            def own(ins):
                n[0] += 1
                ins.then_inc(act_seq, 1)
                act.wait_ge(act_seq, n[0])

            def hi(w, t):
                for half in range(2):
                    slot = half_slot(w, half)
                    act.wait_ge(raw_in[slot], 16 * half_uses(w, half, t))
                    act.wait_ge(pe_half, 2 * now(w, t) + half + 1)
                    act.activation(whi[:, slot], raw[:, slot], ACT.Copy).then_inc(hi_done, 1)

            def product(w, t):
                act.wait_ge(pe_half, 2 * now(w, t) + 2 + 4)

            def root(i, cols):
                act.wait_ge(var_ready, i + 1)
                act.activation(st[:, 1, 0:cols], st[:, 0, 0:cols], ACT.Sqrt).then_inc(root_done, 1)

            def square_x(i, j):
                if i >= 2:
                    act.wait_ge(stat_done, i - 1)
                act.activation(T[:, i % 2, :], X[:, j, :], ACT.Square).then_inc(sq_done, 1)

            def make_h(layer):
                act.wait_ge(gain_ready, 2 * (layer + 1))
                for j in range(KC):
                    sh = SHIFT[layer][j // HC] * HC + j % HC
                    act.wait_ge(xr_done, KC * layer + j + 1)
                    act.activation(X[:, j, :], X[:, j, :], ACT.Identity, bias=mod[:, sh:sh + 1],
                                   scale=hgain[:, j:j + 1]).then_inc(h_done, 1)
                    act.wait_ge(h_done, KC * layer + j + 1)
                    act.activation(hhi[:, j, :], X[:, j, :], ACT.Copy).then_inc(hhi_done, 1)

            def step_u(w, t):
                hi(w + AHEAD, t)
                product(w, t)
                act.activation(U[:, bass.ds(now(w, t) - U0, 1), PAD:PAD + SEQ].rearrange("p a t -> p (a t)"),
                               Z[w % 2][:, 0:SEQ], ACT.Copy).then_inc(z_free[w % 2], 1)

            def step_qk(w, t, q0, kind, layer):
                hi(w + AHEAD, t)
                product(w, t)
                gain = qgain[:, layer:layer + 1] if kind == "q" else 1.0
                act.activation(X[:, bass.ds(now(w, t) - q0, 1), :].rearrange("p a t -> p (a t)"),
                               Z[w % 2][:, 0:SEQ], ACT.Copy, scale=gain)
                act.activation(T[:, w % 2, :], Z[w % 2][:, 0:SEQ], ACT.Square).then_inc(z_free[w % 2], 1)

            def evict_v(w):
                product(w, None)
                act.activation(T[:, w % 2, :], Z[w % 2][:, 0:SEQ], ACT.Copy).then_inc(z_free[w % 2], 1)

            def tanh_gate(w, t, g0, layer):
                product(w, t)
                i = KC * layer + now(w, t) - g0
                if t is not None or i >= 2:
                    act.wait_ge(gated, i - 1)
                act.activation(T[:, w % 2, :], Z[w % 2][:, 0:SEQ], ACT.Tanh, scale=0.5).then_inc(tanh_done, 1)

            def round_gated(w, t, g0, layer):
                c = now(w, t) - g0
                act.wait_ge(gated, KC * layer + c + 1)
                act.activation(ghi[:, bass.ds(c, 1), :].rearrange("p a t -> p (a t)"), SG[:, w % 2, :],
                               ACT.Copy).then_inc(ghi_done, 1)

            def step_g(w, t, g0, layer):
                hi(w + AHEAD, t)
                tanh_gate(w, t, g0, layer)
                round_gated(w - 1, t, g0, layer)

            def attend(layer, i):
                if 0 <= i < HC:
                    a = HC * layer + i
                    act.wait_ge(max_done, a + 1)
                    for q, (c0, c1) in enumerate(((0, P), (P, KEYS))):
                        e = act.activation(SP[:, a % 2, c0:c1], SP[:, a % 2, c0:c1], ACT.Exp,
                                           bias=nm[:, a % 2, q:q + 1], accum_out=ls[:, a % 2, q:q + 1])
                        e.then_inc(exp_done, 1)
                if 0 <= i - 1 < HC:
                    a = HC * layer + i - 1
                    act.wait_ge(pt_done, a + 1)
                    if a >= 2:
                        act.wait_ge(pv_done, a - 1)
                    act.activation(PTs[:, a % 2, :], PT[:, 0:KEYS], ACT.Copy).then_inc(pt_copied, 1)
                if 0 <= i - 2 < HC:
                    a = HC * layer + i - 2
                    act.wait_ge(pv_done, a + 1)
                    act.activation(X[:, i - 2, :], O[:, 0:SEQ], ACT.Copy).then_inc(o_copied, 1)

            def pool_evict(g):
                act.wait_ge(pool_mm, g + 1)
                for o in range(2):
                    j = 2 * g + o
                    act.activation(Y[:, j, :], PT[:, o * SEQ:(o + 1) * SEQ], ACT.Copy,
                                   scale=par[:, C_PSC + j:C_PSC + j + 1]).then_inc(pool_out, 1)

            act.wait_ge(par_in, 16)
            act.activation(ctmp[:], par[:, C_C:C_C + KC], ACT.Exp, scale=-1.0).then_inc(cexp, 1)
            for l in range(2):
                own(act.activation(qgain[:, l:l + 1], par[:, C_QK + 2 * l:C_QK + 2 * l + 1], ACT.Copy,
                                   scale=float(P) ** -0.5))
            act.activation(lnh[:], par[:, C_LG:C_LG + 2 * HC], ACT.Copy, scale=0.5).then_inc(act_seq, 1)
            n[0] += 1
            act.wait_ge(x_in, 16)
            for j in range(KC):
                square_x(j, j)
            root(0, QT)
            hi(0, None)
            hi(1, None)
            make_h(0)
            run(act, U0, Q0, step_u)
            step_qk(8, None, Q0, "q", 0)
            step_qk(9, None, Q0, "q", 0)
            pool_evict(0)
            run(act, 10, 16, lambda w, t: step_qk(w, t, Q0, "q", 0))
            step_qk(16, None, Q0, "k", 0)
            pool_evict(1)
            step_qk(17, None, Q0, "k", 0)
            pool_evict(2)
            run(act, 18, V0, lambda w, t: step_qk(w, t, Q0, "k", 0))
            for w in range(V0, G0 + 5):
                hi(w + AHEAD, None)
                if w < G0:
                    evict_v(w)
                else:
                    tanh_gate(w, None, G0, 0)
                if w == V0:
                    pool_evict(3)
                    root(1, 2 * KC)
                attend(0, w - V0 - 3)
                if w > G0:
                    round_gated(w - 1, None, G0, 0)
            step_g(37, None, G0, 0)
            run(act, 38, O0, lambda w, t: step_g(w, t, G0, 0))

            def step_o0(w, t):
                hi(w + AHEAD, t)
                j = now(w, t) - O0 - 1
                act.wait_ge(z_free[(w - 1) % 2], bank_uses(w - 1, t) + 2)
                act.wait_ge(stat_done, KC + j - 1)
                act.activation(T[:, (w - 1) % 2, :], X[:, bass.ds(j, 1), :].rearrange("p a t -> p (a t)"),
                               ACT.Square).then_inc(sq_done, 1)

            round_gated(O0 - 1, None, G0, 0)
            hi(O0 + AHEAD, None)
            step_o0(49, None)
            run(act, 50, AB1, step_o0)
            act.wait_ge(z_free[(AB1 - 1) % 2], (AB1 - 1) // 2 + 2)
            act.wait_ge(stat_done, 2 * KC - 2)
            act.activation(T[:, 1, :], X[:, KC - 1, :], ACT.Square).then_inc(sq_done, 1)
            root(2, QT)
            make_h(1)

            def step_ab(w, t):
                hi(w + AHEAD, t)
                product(w, t)
                pair = (w - AB1) // 2
                if w % 2 == 0:
                    if t is not None or pair > 0:
                        act.wait_ge(u_done, pair if t is None else pair + t)
                    act.activation(T[:, 0, :], Z[0][:, 0:SEQ], ACT.Copy, scale=0.5).then_inc(z_free[0], 1)
                else:
                    act.activation(T[:, 1, :], Z[1][:, 0:SEQ], ACT.Tanh, scale=0.5).then_inc(z_free[1], 1)

            step_ab(64, None)
            step_ab(65, None)
            run(act, 66, QI1, step_ab)

            def step_qi(w, t):
                hi(w + AHEAD, t)
                product(w, t)
                act.activation(QI[:, bass.ds(now(w, t) - QI1, 1), :].rearrange("p a t -> p (a t)"),
                               Z[w % 2][:, 0:SEQ], ACT.Copy).then_inc(z_free[w % 2], 1)

            run(act, QI1, KW1, step_qi)
            hi(KW1 + AHEAD, None)
            product(KW1, None)
            act.activation(KW[:], Z[KW1 % 2][:, 0:SEQ], ACT.Copy).then_inc(z_free[KW1 % 2], 1)
            step_qk(85, None, Q1, "q", 1)
            for w in range(86, 94):
                step_qk(w, None, Q1, "q" if w < 93 else "k", 1)
                hh = w - 86
                act.wait_ge(logit, hh + 1)
                if hh >= 2:
                    act.wait_ge(score, 2 * (hh - 1))
                act.activation(SP[:, hh % 2, :], S[hh % 2][:, 0:KEYS], ACT.Relu,
                               scale=float(IDX_DIM) ** -0.5).then_inc(relu, 1)
            run(act, 94, V1, lambda w, t: step_qk(w, t, Q1, "k", 1))
            for w in range(V1, 117):
                hi(w + AHEAD, None)
                if w < G1:
                    evict_v(w)
                else:
                    tanh_gate(w, None, G1, 1)
                if w == V1:
                    root(3, 2 * KC)
                attend(1, w - V1 - 3)
                if w > G1:
                    round_gated(w - 1, None, G1, 1)
                if w == 112:
                    act.wait_ge(ln_sub, 1)
                    act.activation(U[:, :, 0:SEQ], Y[:], ACT.Square).then_inc(ln_sq, 1)
                if w == 113:
                    root(4, QT)
                for j in {114: (0, 1, 2), 115: (3, 4, 5), 116: (6, 7)}.get(w, ()):
                    act.wait_ge(ln_mul, 1)
                    act.activation(U[:, j, 0:SEQ], Y[:, j, :], ACT.Tanh, bias=lnh[:, HC + j:HC + j + 1],
                                   scale=lnh[:, j:j + 1])
                    act.activation(Y[:, j, :], Y[:, j, :], ACT.Identity,
                                   bias=par[:, C_LB + j:C_LB + j + 1],
                                   scale=par[:, C_LG + j:C_LG + j + 1]).then_inc(ln_act, 1)
            run(act, 117, O1, lambda w, t: step_g(w, t, G1, 1))
            round_gated(O1 - 1, None, G1, 1)
            hi(O1 + AHEAD, None)
            run(act, O1 + 1, N_SLABS - AHEAD, lambda w, t: hi(w + AHEAD, t))

        @block.tensor
        def _(pe):
            for b in range(2):
                pe.sem_inc(z_free[b], 1)
            mm = nc.tensor.matmul

            def slab(w, t, ahi, alo, each=None):
                out = Z[w % 2][:, 0:SEQ]
                pe.wait_ge(z_free[w % 2], bank_uses(w, t) + 1)
                for half in range(2):
                    s = half_slot(w, half)
                    pe.wait_ge(lo_done, 2 * now(w, t) + half + 1 + 4)
                    for k in range(8):
                        c = 8 * half + k
                        if each is not None:
                            pe.wait_ge(hlo_done, each + c + 1)
                        mm(out, whi[:, s, k, :], ahi[:, c, :], start=(c == 0), stop=False)
                        mm(out, whi[:, s, k, :], alo[:, c, :], start=False, stop=False)
                        last = mm(out, wlo[:, s, k, :], ahi[:, c, :], start=False, stop=(c == KC - 1))
                    last.then_inc(pe_half, 1)

            def slab_h(w, t):
                slab(w, t, hhi, hlo)

            def slab_g(w, t):
                slab(w, t, ghi, glo)

            def sum_squares(slot, first, last):
                for q in range(QT):
                    ins = mm(M[:, q:q + 1], T[:, slot, q * P:(q + 1) * P], ones[:, 0:1],
                             start=(first and q == 0), stop=last, skip_group_check=True)
                return ins

            def x_stat(i, slot=None, runtime=None):
                pe.wait_ge(sq_done, (i if runtime is None else runtime) + 1)
                sum_squares(i % 2, i % KC == 0, i % KC == KC - 1).then_inc(stat_done, 1)

            def spread_token(i):
                pe.wait_ge(diag_ready, i + 1)
                for q in range(QT):
                    ins = mm(XB[:, q * P:(q + 1) * P], ones[:], KD[:, q, :], start=True, stop=True)
                ins.then_inc(spread, 1)

            def reduce_piece(p):
                pe.wait_ge(ada_done, UNITS * (p + 1) + 4)
                if p >= 1:
                    pe.wait_ge(mod_done, p)
                if p >= 7:
                    pe.wait_ge(o_copied, HC if p < 10 else 2 * HC)
                for j in range(HC):
                    ins = mm(O[:, j:j + 1], acc[:, p % 2, j * P:(j + 1) * P], ones[:, 0:1],
                             start=True, stop=True)
                ins.then_inc(mod_sum, 1)

            def qk_stats(w, t, q0):
                pe.wait_ge(z_free[w % 2], bank_uses(w, t) + 2)
                for q in range(QT):
                    ins = mm(M[:, bass.ds(q * KC + now(w, t) - q0, 1)], T[:, w % 2, q * P:(q + 1) * P],
                             ones[:, 0:1], start=True, stop=True)
                ins.then_inc(qk_stat, 1)

            def pool_product(g):
                pe.wait_ge(d_ready, g + 1)
                if g:
                    pe.wait_ge(pool_out, 2 * g)
                for o in range(2):
                    for k in range(2):
                        ins = mm(PT[:, o * SEQ:(o + 1) * SEQ], PW[:, g, k, o * P:(o + 1) * P],
                                 Y[:, 2 * g + k, :], start=(k == 0), stop=(k == 1))
                ins.then_inc(pool_mm, 1)

            def turn_v(w, layer, v0):
                pe.wait_ge(z_free[w % 2], w // 2 + 2)
                n = HC * layer + w - v0
                if n:
                    pe.wait_ge(v_copied, n)
                for q in range(QT):
                    ins = nc.tensor.transpose(XB[:, q * P:(q + 1) * P], T[:, w % 2, q * P:(q + 1) * P], ident[:])
                ins.then_inc(vt_done, 1)

            def attend(layer, i):
                if 0 <= i + 1 < HC:
                    a = HC * layer + i + 1
                    pe.wait_ge(kdiag, a + 1)
                    if a:
                        pe.wait_ge(kmul, a)
                    for q in range(QT):
                        ins = mm(M[:, q * P:(q + 1) * P], ones[:], KD[:, q, :], start=True, stop=True)
                    ins.then_inc(kb_done, 1)
                if 0 <= i < HC:
                    a = HC * layer + i
                    pe.wait_ge(kmul, a + 1)
                    if a >= 2:
                        pe.wait_ge(s_added, a - 1)
                    mm(S[a % 2][:, 0:P], X[:, i, 0:P], X[:, HC + i, 0:P], start=True, stop=True)
                    mm(S[a % 2][:, P:KEYS], X[:, i, P:SEQ], X[:, HC + i, :], start=True, stop=True)\
                        .then_inc(scored, 1)
                if 0 <= i - 1 < HC:
                    a = HC * layer + i - 1
                    pe.wait_ge(pdiag, a + 1)
                    if a:
                        pe.wait_ge(pt_copied, a)
                    else:
                        pe.wait_ge(pool_out, HC)
                    for out, keys, q in ((0, 0, 0), (P, P, 1), (2 * P, 2 * P, 1)):
                        ins = mm(PT[:, out:out + P], SP[:, a % 2, keys:keys + P], PD[:, a % 2, q, :],
                                 start=True, stop=True)
                    ins.then_inc(pt_done, 1)
                if 0 <= i - 2 < HC:
                    a, h = HC * layer + i - 2, i - 2
                    pe.wait_ge(pt_copied, a + 1)
                    pe.wait_ge(v_copied, a + 1)
                    pe.wait_ge(mod_done, 7 if layer == 0 else 10)
                    if a:
                        pe.wait_ge(o_copied, a)
                    mm(O[:, 0:SEQ], V[:, 0, h * P:(h + 1) * P], PTs[:, a % 2, 0:SEQ], start=True, stop=False)
                    mm(O[:, P:SEQ], V[:, 1, h * P:(h + 1) * P], PTs[:, a % 2, SEQ:KEYS],
                       start=False, stop=True).then_inc(pv_done, 1)

            def logits(hh):
                c, p0 = hh // 2, IDX_DIM * (hh % 2)
                keys = KW if p0 == 0 else KI
                if hh == 0:
                    pe.wait_ge(z_free[KW1 % 2], KW1 // 2 + 2)
                    pe.wait_ge(s_added, HC)
                if hh == 1:
                    pe.wait_ge(ki_in, 16)
                if hh >= 2:
                    pe.wait_ge(relu, hh - 1)
                mm(S[hh % 2][:, 0:P], QI[p0:p0 + IDX_DIM, c, 0:P], keys[p0:p0 + IDX_DIM, 0:P],
                   start=True, stop=True)
                mm(S[hh % 2][:, P:KEYS], QI[p0:p0 + IDX_DIM, c, P:SEQ], keys[p0:p0 + IDX_DIM, :],
                   start=True, stop=True).then_inc(logit, 1)

            pe.wait_ge(const, 2)
            for i in range(KC):
                x_stat(i)
            spread_token(0)
            for p in range(4):
                reduce_piece(p)
            slab(0, None, hhi, hlo, each=0)
            slab_h(1, None)
            run(pe, 2, Q0, slab_h)

            def slab_stat(q0):
                def step(w, t):
                    slab_h(w, t)
                    qk_stats(w - 1, t, q0)
                return step

            slab_h(8, None)
            reduce_piece(4)
            slab_h(9, None)
            qk_stats(8, None, Q0)
            pe.wait_ge(pw_in, 16)
            pool_product(0)
            run(pe, 10, 16, slab_stat(Q0))
            slab_stat(Q0)(16, None)
            reduce_piece(5)
            pool_product(1)
            slab_stat(Q0)(17, None)
            pool_product(2)
            run(pe, 18, V0, slab_stat(Q0))
            for w in range(V0, G0 + 5):
                slab_h(w, None)
                if w == V0:
                    qk_stats(w - 1, None, Q0)
                    reduce_piece(6)
                    pool_product(3)
                elif w <= G0:
                    turn_v(w - 1, 0, V0)
                attend(0, w - V0 - 3)
            slab_h(37, None)
            run(pe, 38, O0, slab_h)

            pe.wait_ge(glo_done, KC)
            slab_g(48, None)
            reduce_piece(7)
            slab_g(49, None)
            slab_g(50, None)
            x_stat(KC)
            slab_g(51, None)
            x_stat(KC + 1)

            def slab_x(w, t):
                slab_g(w, t)
                x_stat(KC + w - O0 - 2, runtime=KC + now(w, t) - O0 - 2)

            run(pe, 52, 56, slab_x)
            slab_x(56, None)
            reduce_piece(8)
            slab_x(57, None)
            run(pe, 58, AB1, slab_x)
            reduce_piece(9)
            x_stat(2 * KC - 2)
            x_stat(2 * KC - 1)
            spread_token(1)

            slab(64, None, hhi, hlo, each=KC)
            slab_h(65, None)
            run(pe, 66, KW1, slab_h)
            slab_h(KW1, None)
            slab_h(85, None)
            pe.wait_ge(z_free[KW1 % 2], KW1 // 2 + 2)
            for q in range(QT):
                ins = nc.tensor.transpose(XB[:, q * P:(q + 1) * P], KW[:, q * P:(q + 1) * P], ident[:])
            ins.then_inc(wt_done, 1)
            for w in range(86, 94):
                slab_stat(Q1)(w, None)
                logits(w - 86)
            run(pe, 94, V1, slab_stat(Q1))
            for w in range(V1, 117):
                slab_h(w, None)
                if w == V1:
                    qk_stats(w - 1, None, Q1)
                elif w <= G1:
                    turn_v(w - 1, 1, V1)
                attend(1, w - V1 - 3)
                if w == 111:
                    pe.wait_ge(conv_seq, N_TAPS)
                    for j in range(HC):
                        for q in range(QT):
                            ins = mm(M[:, q:q + 1], Y[:, j, q * P:(q + 1) * P], ones[:, 0:1],
                                     start=(j == 0 and q == 0), stop=(j == HC - 1), skip_group_check=True)
                    ins.then_inc(mean_mm, 1)
                if w == 112:
                    spread_token(2)
                if w == 113:
                    pe.wait_ge(ln_sq, 1)
                    for j in range(HC):
                        for q in range(QT):
                            ins = mm(M[:, q:q + 1], U[:, j, q * P:(q + 1) * P], ones[:, 0:1],
                                     start=(j == 0 and q == 0), stop=(j == HC - 1), skip_group_check=True)
                    ins.then_inc(var_mm, 1)
                if w == 114:
                    spread_token(3)
            run(pe, 117, O1, slab_h)
            pe.wait_ge(glo_done, 2 * KC)
            slab_g(125, None)
            reduce_piece(10)
            run(pe, 126, 133, slab_g)
            slab_g(133, None)
            reduce_piece(11)
            run(pe, 134, N_SLABS, slab_g)

        @block.vector
        def _(dve):
            n = [0]

            def seq(ins):
                n[0] += 1
                ins.then_inc(dve_seq, 1)

            def settle():
                dve.wait_ge(dve_seq, n[0])

            def lo(w, t):
                for half in range(2):
                    s = half_slot(w, half)
                    dve.wait_ge(hi_done, 2 * now(w, t) + half + 1)
                    dve.tensor_tensor(wlo[:, s], raw[:, s], whi[:, s].bitcast(F32), ALU.subtract)\
                        .then_inc(lo_done, 1)

            def add_units(first, count, t):
                for u in range(count):
                    unit = first + u if t is None else first + u + 4 * t
                    slot, p = (first + u) % 4, first // UNITS
                    uses = (first + u) // 4 + 1
                    k = unit - UNITS * p
                    dve.wait_ge(ada_in[slot], 16 * (uses if t is None else uses + t))
                    dve.wait_ge(ada_done, unit + 4)
                    dve.scalar_tensor_tensor(acc[:, p % 2, :], ada[:, slot, :], cact[:, bass.ds(k, 1)],
                                             acc[:, p % 2, :], ALU.mult, ALU.add).then_inc(ada_done, 1)

            def units(w, t):
                if units_at(w) is not None:
                    if t is None and units_at(w) % UNITS == 0:
                        dve.wait_ge(acc_zero, units_at(w) // UNITS + 1)
                    add_units(units_at(w), 2, t)

            def keep_piece(p):
                dve.wait_ge(mod_sum, p + 1)
                dve.tensor_tensor(mod[:, p * HC:(p + 1) * HC], O[:, 0:HC],
                                  par[:, C_ADAB + p * HC:C_ADAB + (p + 1) * HC], ALU.add).then_inc(mod_done, 1)

            def make_gain(layer):
                for half, p in enumerate(SCALE[layer]):
                    dve.wait_ge(mod_done, p + 1)
                    g = C_NORM + KC * layer + HC * half
                    dve.scalar_tensor_tensor(hgain[:, HC * half:HC * (half + 1)],
                                             mod[:, p * HC:(p + 1) * HC], 1.0, par[:, g:g + HC],
                                             ALU.add, ALU.mult).then_inc(gain_ready, 1)

            def rsqrt(i, cols, src, count):
                a, s, r, y = (st[:, k, 0:cols] for k in (0, 1, 2, 3))
                dve.tensor_scalar(a, src, 1.0 / count, EPS, ALU.mult, ALU.add).then_inc(var_ready, 1)
                dve.wait_ge(root_done, i + 1)
                seq(dve.reciprocal(r, s))
                settle()
                seq(dve.tensor_tensor(y, r, r, ALU.mult))
                settle()
                seq(dve.scalar_tensor_tensor(st[:, 4, 0:cols], y, -0.5, a, ALU.mult, ALU.mult))
                settle()
                seq(dve.scalar_tensor_tensor(rr[:, 0:cols], st[:, 4, 0:cols], 1.5, r, ALU.add, ALU.mult))
                settle()

            def token_diag(src):
                for q in range(QT):
                    ins = dve.tensor_scalar(KD[:, q, :], ident[:], src[:, q:q + 1], None, ALU.mult)
                ins.then_inc(diag_ready, 1)

            def scale_x(layer):
                dve.wait_ge(spread, layer + 1)
                if layer:
                    x_written(dve, 0, KC)
                for j in range(KC):
                    if layer and j % 4 == 0:
                        dve.wait_ge(store[j // 4], 16)
                    dve.tensor_tensor(X[:, j, :], X[:, j, :], XB[:, 0:SEQ], ALU.mult).then_inc(xr_done, 1)

            def split_h(layer):
                for j in range(KC):
                    dve.wait_ge(hhi_done, KC * layer + j + 1)
                    dve.tensor_tensor(hlo[:, j, :], X[:, j, :], hhi[:, j, :].bitcast(F32), ALU.subtract)\
                        .then_inc(hlo_done, 1)

            def flat(ap):
                return ap.rearrange("p a t -> p (a t)")

            def gate(w, t, g0, layer):
                i = KC * layer + now(w, t) - g0
                half, j = (w - g0) // HC, now(w, t) - g0 - HC * ((w - g0) // HC)
                src = (Y, X)[half] if layer == 0 else (X, Y)[half]
                factor = 0.25 if (layer == 1 and half == 1) else 0.5
                dve.wait_ge(tanh_done, i + 1)
                dve.scalar_tensor_tensor(SG[:, w % 2, :], T[:, w % 2, :], 1.0, Z[w % 2][:, 0:SEQ],
                                         ALU.add, ALU.mult).then_inc(z_free[w % 2], 1)
                if src is X and t is None:
                    dve.wait_ge(o_copied, i + 1 - HC * (1 + layer) if layer == 0 else HC + (w - g0) + 1)
                dve.wait_ge(z_free[w % 2], bank_uses(w, t) + 2)
                dve.scalar_tensor_tensor(SG[:, w % 2, :], flat(src[:, bass.ds(j, 1), :]), factor,
                                         SG[:, w % 2, :], ALU.mult, ALU.mult).then_inc(gated, 1)

            def split_gated(w, t, g0, layer):
                c = now(w, t) - g0
                dve.wait_ge(ghi_done, KC * layer + c + 1)
                dve.tensor_tensor(flat(glo[:, bass.ds(c, 1), :]), SG[:, w % 2, :],
                                  flat(ghi[:, bass.ds(c, 1), :]).bitcast(F32), ALU.subtract)\
                    .then_inc(glo_done, 1)

            def add_x(w, t, o0, layer):
                j = now(w, t) - o0
                in_seg = (w - o0) % HC
                dve.wait_ge(pe_half, 2 * now(w, t) + 2 + 4)
                gcol = GATE[layer] * HC
                y = in_seg if t is None else in_seg + 2 * t
                dve.scalar_tensor_tensor(flat(X[:, bass.ds(j, 1), :]), Z[w % 2][:, 0:SEQ],
                                         mod[:, bass.ds(gcol + j, 1)], flat(Y[:, bass.ds(y, 1), :]),
                                         ALU.mult, ALU.add).then_inc(z_free[w % 2], 1)

            def pool_branch(g):
                win = 2 ** (g + 1)
                u = U[:, 2 * g:2 * g + 2, PAD - 16:PAD + SEQ]
                src, s, bufs = u, 1, (poolA, poolB)
                for lev in range(g + 1):
                    dst = bufs[lev % 2]
                    seq(dve.tensor_tensor(dst[:, :, s:SEQ + 16] if lev == 0 else dst[:, :, 2 * s - 1:SEQ + 16],
                                          src[:, :, s:SEQ + 16] if lev == 0 else src[:, :, 2 * s - 1:SEQ + 16],
                                          src[:, :, 0:SEQ + 16 - s] if lev == 0 else
                                          src[:, :, s - 1:SEQ + 16 - s], ALU.add))
                    settle()
                    src, s = dst, 2 * s
                d = Y[:, 2 * g:2 * g + 2, :]
                seq(dve.scalar_tensor_tensor(d, src[:, :, 16:], 1.0 / win, u[:, :, 16:], ALU.mult, ALU.subtract))
                settle()
                for c in range(2):
                    seq(dve.tensor_tensor(src[:, c, 16:16 + win], src[:, c, 16:16 + win], rc[:, 0:win], ALU.mult))
                settle()
                for c in range(2):
                    ins = dve.tensor_tensor(d[:, c, 0:win], src[:, c, 16:16 + win], u[:, c, 16:16 + win],
                                            ALU.subtract)
                    if c:
                        ins.then_inc(d_ready, 1)
                    else:
                        seq(ins)

            def copy_v(nv, layer):
                h = nv - HC * layer
                dve.wait_ge(vt_done, nv + 1)
                dve.tensor_copy(V[:, :, h * P:(h + 1) * P], XB[:, 0:SEQ].rearrange("p (a b) -> p a b", a=QT))\
                    .then_inc(v_copied, 1)

            def attend(layer, i, filler=None):
                if 0 <= i + 1 < HC:
                    a = HC * layer + i + 1
                    dve.wait_ge(kb_done, a + 1)
                    dve.scalar_tensor_tensor(X[:, HC + i + 1, :], X[:, HC + i + 1, :],
                                             par[:, C_QK + 2 * layer + 1:C_QK + 2 * layer + 2], M[:, 0:SEQ],
                                             ALU.mult, ALU.mult).then_inc(kmul, 1)
                if 0 <= i < HC:
                    a = HC * layer + i
                    dve.wait_ge(scored, a + 1)
                    dve.wait_ge(ds_ready, a + 1)
                    if a >= 2:
                        dve.wait_ge(pt_done, a - 1)
                    for q, (c0, c1) in enumerate(((0, P), (P, KEYS))):
                        ins = dve.scalar_tensor_tensor(SP[:, a % 2, c0:c1], S[a % 2][:, c0:c1],
                                                       rr[:, KC * q + i:KC * q + i + 1], DS[:, a % 2, c0:c1],
                                                       ALU.mult, ALU.add)
                        if q:
                            ins.then_inc(s_added, 1)
                        else:
                            seq(ins)
                if 0 <= i + 2 < HC:
                    a = HC * layer + i + 2
                    if a:
                        dve.wait_ge(kb_done, a)
                    for q in range(QT):
                        col = KC * q + HC + i + 2
                        ins = dve.tensor_scalar(KD[:, q, :], ident[:], rr[:, col:col + 1], None, ALU.mult)
                    ins.then_inc(kdiag, 1)
                if 0 <= i < HC:
                    settle()
                    dve.wait_ge(s_added, a0(layer, i) + 1)
                    for q, (c0, c1) in enumerate(((0, P), (P, KEYS))):
                        ins = dve.tensor_reduce(nm[:, i % 2, q:q + 1], SP[:, i % 2, c0:c1], AX_X, ALU.max,
                                                negate=True)
                        if q:
                            ins.then_inc(max_done, 1)
                        else:
                            seq(ins)

            def a0(layer, i):
                return HC * layer + i

            def divide(layer, i):
                if 0 <= i < HC:
                    a = HC * layer + i
                    dve.wait_ge(exp_done, 2 * (a + 1))
                    seq(dve.reciprocal(rl[:, i % 2, :], ls[:, i % 2, :]))
                    settle()
                    for q in range(QT):
                        ins = dve.tensor_scalar(PD[:, i % 2, q, :], ident[:], rl[:, i % 2, q:q + 1], None, ALU.mult)
                    ins.then_inc(pdiag, 1)

            plan = conv_plan()
            taps = [0]

            def conv(w):
                for j, k in plan.get(w, ()):
                    wcol = C_CW + j * CONV_WIDTH + k
                    if k == 0:
                        dve.wait_ge(u_done, j + 1)
                        ins = dve.tensor_scalar(Y[:, j, :], U[:, j, 0:SEQ], par[:, wcol:wcol + 1],
                                                par[:, C_CB + j:C_CB + j + 1], ALU.mult, ALU.add)
                    else:
                        dve.wait_ge(conv_seq, taps[0] - 1)
                        ins = dve.scalar_tensor_tensor(Y[:, j, :], U[:, j, k:k + SEQ], par[:, wcol:wcol + 1],
                                                       Y[:, j, :], ALU.mult, ALU.add)
                    ins.then_inc(conv_seq, 1)
                    taps[0] += 1

            dve.wait_ge(cexp, 1)
            seq(dve.tensor_scalar(ctmp[:], ctmp[:], 1.0, None, ALU.add))
            settle()
            seq(dve.reciprocal(ctmp[:], ctmp[:]))
            settle()
            seq(dve.tensor_tensor(cact[:], ctmp[:], par[:, C_C:C_C + KC], ALU.mult))
            dve.wait_ge(const, 4)
            seq(dve.reciprocal(rc[:], rc[:]))
            settle()
            for p in range(4):
                dve.wait_ge(acc_zero, p + 1)
                if p == 3:
                    lo(0, None)
                    lo(1, None)
                with dve.Fori(0, UNITS // 4) as t:
                    add_units(UNITS * p, 4, t)
                if p:
                    keep_piece(p - 1)
                if p == 0:
                    dve.wait_ge(stat_done, KC)
                    rsqrt(0, QT, M[:, 0:QT], D_MODEL)
                    token_diag(rr)
                    scale_x(0)
            keep_piece(3)
            make_gain(0)
            split_h(0)

            def plain(w, t):
                lo(w + AHEAD, t)
                units(w, t)

            plain(0, None)
            plain(1, None)
            run(dve, 2, Q0, plain)
            plain(8, None)
            keep_piece(4)
            dve.wait_ge(z_free[1], 7 // 2 + 2)
            dve.wait_ge(z_free[0], 6 // 2 + 2)
            pool_branch(0)
            plain(9, None)
            pool_branch(1)
            run(dve, 10, 16, plain)
            plain(16, None)
            keep_piece(5)
            pool_branch(2)
            plain(17, None)
            pool_branch(3)
            run(dve, 18, V0, plain)
            for w in range(V0, G0 + 5):
                plain(w, None)
                if w == V0:
                    keep_piece(6)
                    dve.wait_ge(qk_stat, 2 * HC)
                    rsqrt(1, 2 * KC, M[:, 0:2 * KC], P)
                if V0 < w <= G0:
                    copy_v(w - 1 - V0, 0)
                attend(0, w - V0 - 3)
                if w > G0:
                    split_gated(w - 1, None, G0, 0)
                if w >= G0:
                    gate(w, None, G0, 0)
                divide(0, w - V0 - 3)

            def step_g(g0, layer):
                def step(w, t):
                    plain(w, t)
                    split_gated(w - 1, t, g0, layer)
                    gate(w, t, g0, layer)
                return step

            for w in range(37, 42):
                step_g(G0, 0)(w, None)
            run(dve, 42, O0, step_g(G0, 0))

            def step_o(o0, layer):
                def step(w, t):
                    plain(w, t)
                    add_x(w, t, o0, layer)
                return step

            def output(layer, o0, g0, p):
                last = N_SLABS - AHEAD
                def head(w):
                    if w < last:
                        lo(w + AHEAD, None)
                    units(w, None)
                split_gated(o0 - 1, None, g0, layer)
                head(o0)
                keep_piece(p)
                dve.wait_ge(mod_done, p + 1)
                dve.wait_ge(xr_in[0], 32 * layer + 16)
                add_x(o0, None, o0, layer)
                for half in range(2):
                    w0 = o0 + HC * half
                    if half:
                        head(w0)
                        keep_piece(p + 1)
                        dve.wait_ge(mod_done, p + 2)
                        dve.wait_ge(xr_in[0], 32 * layer + 32)
                        add_x(w0, None, o0, layer)
                    for w in (w0 + 1, w0 + 2, w0 + 3):
                        head(w)
                        add_x(w, None, o0, layer)
                    dve.wait_ge(xr_in[1], 32 * layer + 16 * (half + 1))
                    if w0 + HC <= last:
                        run(dve, w0 + 4, w0 + HC, step_o(o0, layer))
                    else:
                        for w in range(w0 + 4, w0 + HC):
                            head(w)
                            add_x(w, None, o0, layer)

            output(0, O0, G0, 7)
            keep_piece(9)
            make_gain(1)
            dve.wait_ge(stat_done, 2 * KC)
            rsqrt(2, QT, M[:, 0:QT], D_MODEL)
            token_diag(rr)
            scale_x(1)
            split_h(1)

            for w in range(AB1, 117):
                plain(w, None)
                if w < QI1 and w % 2:
                    j = (w - AB1) // 2
                    dve.wait_ge(z_free[1], w // 2 + 2)
                    dve.wait_ge(z_free[0], w // 2 + 2)
                    dve.scalar_tensor_tensor(U[:, j, PAD:PAD + SEQ], T[:, 1, :], 1.0, T[:, 0, :],
                                             ALU.add, ALU.mult).then_inc(u_done, 1)
                conv(w)
                if w == 85:
                    dve.wait_ge(wt_done, 1)
                    seq(dve.tensor_scalar(wi[:], XB[:, 0:SEQ].rearrange("p (a b) -> p a b", a=QT)
                                          [:, :, IDX_DIM:IDX_DIM + IDX_HEADS],
                                          float(IDX_HEADS) ** -0.5, None, ALU.mult))
                    settle()
                if 86 <= w < 94:
                    hh = w - 86
                    dve.wait_ge(relu, hh + 1)
                    if hh == 0:
                        dve.wait_ge(cm_ready, 2)
                    else:
                        dve.wait_ge(score, 2 * hh)
                    for q, (c0, c1) in enumerate(((0, P), (P, KEYS))):
                        dve.scalar_tensor_tensor(PTs[:, 0, c0:c1], SP[:, hh % 2, c0:c1], wi[:, q, hh:hh + 1],
                                                 PTs[:, 0, c0:c1], ALU.mult, ALU.add).then_inc(score, 1)
                if 94 <= w < 98:
                    if w == 94:
                        dve.wait_ge(score, 2 * IDX_HEADS)
                    for r in range(2):
                        for q, (c0, c1) in enumerate(((0, P), (P, KEYS))):
                            seq(dve.max(m8[:, q, :], PTs[:, r, c0:c1]))
                        settle()
                        for q, (c0, c1) in enumerate(((0, P), (P, KEYS))):
                            seq(dve.match_replace(PTs[:, 1 - r, c0:c1], m8[:, q, :], PTs[:, r, c0:c1], -3e38))
                        settle()
                if w == 98:
                    seq(dve.tensor_scalar(MK[:], PTs[:, 0, :], -2e38, -BIG, ALU.is_ge, ALU.mult))
                    settle()
                    dve.tensor_tensor(MK[:], MK[:], D[:], ALU.add).then_inc(mask_ready, 1)
                if w == V1:
                    dve.wait_ge(qk_stat, 4 * HC)
                    rsqrt(3, 2 * KC, M[:, 0:2 * KC], P)
                if V1 < w <= G1:
                    copy_v(HC + w - 1 - V1, 1)
                attend(1, w - V1 - 3)
                if w > G1:
                    split_gated(w - 1, None, G1, 1)
                if w >= G1:
                    gate(w, None, G1, 1)
                divide(1, w - V1 - 3)
                if w == 111:
                    dve.wait_ge(mean_mm, 1)
                    seq(dve.tensor_scalar(st[:, 0, 0:QT], M[:, 0:QT], 1.0 / HALF, None, ALU.mult))
                    settle()
                    token_diag(st[:, 0, :])
                if w == 112:
                    dve.wait_ge(spread, 3)
                    for j in range(HC):
                        seq(dve.tensor_tensor(Y[:, j, :], Y[:, j, :], XB[:, 0:SEQ], ALU.subtract))
                    settle()
                    dve.sem_inc(ln_sub, 1)
                if w == 113:
                    dve.wait_ge(var_mm, 1)
                    rsqrt(4, QT, M[:, 0:QT], HALF)
                    token_diag(rr)
                if w == 114:
                    dve.wait_ge(spread, 4)
                    for j in range(HC):
                        ins = dve.tensor_tensor(Y[:, j, :], Y[:, j, :], XB[:, 0:SEQ], ALU.mult)
                        if j == HC - 1:
                            ins.then_inc(ln_mul, 1)
            for w in range(117, 119):
                plain(w, None)
                if w == 117:
                    for j in range(HC):
                        dve.wait_ge(ln_act, j + 1)
                        ins = dve.scalar_tensor_tensor(Y[:, j, :], U[:, j, 0:SEQ], 1.0, Y[:, j, :],
                                                       ALU.add, ALU.mult)
                        seq(ins)
                    settle()
                split_gated(w - 1, None, G1, 1)
                gate(w, None, G1, 1)
            run(dve, 119, O1, step_g(G1, 1))
            output(1, O1, G1, 10)


def kernel(**inputs):
    import numpy as np
    import concourse.bacc as bacc
    from concourse.bass_utils import run_bass_kernel_spmd

    def slabs(w):
        k, n = w.shape
        return w.reshape(k // P, P, n // P, P).transpose(2, 1, 0, 3)

    def cols(v):
        return v.reshape(-1, P).T

    od = inputs["od_w_in"][0]
    q, k, v = od[:, 0:HALF], od[:, HALF:2 * HALF], od[:, 2 * HALF:3 * HALF]
    at = 3 * HALF
    qi = od[:, at:at + IDX_HEADS * IDX_DIM]
    at += IDX_HEADS * IDX_DIM
    wi, ki = od[:, at:at + IDX_HEADS], od[:, at + IDX_HEADS:at + IDX_HEADS + IDX_DIM]
    at += IDX_HEADS + IDX_DIM
    ga, gb, g = od[:, at:at + HALF], od[:, at + HALF:at + 2 * HALF], od[:, at + 2 * HALF:]
    ab = np.stack([slabs(ga), slabs(gb)], axis=1).reshape(2 * HC, P, KC, P)
    kw = np.concatenate([ki] + [wi] * (IDX_DIM // IDX_HEADS), axis=1)
    w_slabs = np.concatenate([slabs(inputs["ev_w_in"][0]), slabs(inputs["w_out"][0]), ab, slabs(qi), slabs(kw),
                              slabs(q), slabs(k), slabs(v), slabs(g), slabs(inputs["w_out"][1])])
    ada = inputs["ada_w"].reshape(2, UNITS, P, 6, PIECE).transpose(0, 3, 1, 2, 4)
    ada_units = np.stack([ada[l, p] for l, p in PIECES]).reshape(len(PIECES) * UNITS, P, PIECE)
    ada_b = inputs["ada_b"].reshape(2, 6, HC, P)
    params = np.concatenate(
        [cols(inputs["c"]), cols(inputs["norm_g"])] + [ada_b[l, p].T for l, p in PIECES]
        + [cols(inputs["pool_scale"]), cols(inputs["moba_qn"]), cols(inputs["moba_kn"]),
           cols(inputs["dsa_qn"]), cols(inputs["dsa_kn"]),
           inputs["conv_w"][0].reshape(CONV_WIDTH, HC, P).transpose(2, 1, 0).reshape(P, HC * CONV_WIDTH),
           cols(inputs["conv_b"]), cols(inputs["conv_ln_g"]), cols(inputs["conv_ln_b"])], axis=1)
    arrays = {
        "xT": inputs["x"][0].T.reshape(KC, P, SEQ).transpose(1, 0, 2),
        "params": params,
        "pool_w": inputs["pool_w"][0].reshape(4, 2, P, 2 * P).transpose(2, 0, 1, 3),
        "w_slabs": w_slabs,
        "ada_units": ada_units,
    }
    arrays = {name: np.ascontiguousarray(a) for name, a in arrays.items()}

    nc = bacc.Bacc("TRN2", target_bir_lowering=False, num_devices=1)
    args = [nc.dram_tensor(name, a.shape, F32, kind="ExternalInput").ap() for name, a in arrays.items()]
    args.append(nc.dram_tensor("x1_dram", (P, KC, SEQ), F32, kind="Internal").ap())
    args.append(nc.dram_tensor("outT", (P, KC, SEQ), F32, kind="ExternalOutput").ap())
    build(nc, *args)
    r = run_bass_kernel_spmd(nc, [arrays], core_ids=[0])
    outT = r.results[0]["outT"]
    return np.ascontiguousarray(outT.transpose(1, 0, 2).reshape(D_MODEL, SEQ).T)[None]
```

```python
from contextlib import ExitStack

import concourse.bass as bass
from concourse import mybir

F32 = mybir.dt.float32
F32R = mybir.dt.float32r
ALU = mybir.AluOpType
ACT = mybir.ActivationFunctionType
AX_X = mybir.AxisListType.X

P = 128
D_MODEL = 2048
SEQ = 256
HALF = D_MODEL // 2
KC = D_MODEL // P
HC = HALF // P
QT = SEQ // P
EPS = 1e-6
BIG = 2.56e32
NEG_INF = -1e30
DSA_SEL = SEQ // 4
IDX_HEADS = 8
IDX_DIM = 64
CONV_WIDTH = 31
PAD = CONV_WIDTH - 1
KEYS = P + SEQ

U0, Q0, V0, G0, O0 = 0, 8, 24, 32, 48
AB1, QI1, KW1, Q1, V1, G1, O1 = 64, 80, 84, 85, 101, 109, 125
N_SLABS = 141
AHEAD = 2

PIECE = 1024
UNITS = D_MODEL // P
GROUP = 4
PIECES = [("h", 0, 0), ("h", 0, 1), ("h", 0, 2), ("h", 0, 3), ("h", 1, 0), ("h", 1, 1), ("gate", 0, 0),
          ("gate", 0, 1), ("h", 1, 2), ("h", 1, 3), ("gate", 1, 0), ("gate", 1, 1)]
UNIT_RATES = ((8, 32, 2), (32, 48, 1), (48, 62, 2), (62, 70, 1), (70, 72, 2),
              (110, 111, 2), (112, 113, 2), (115, 117, 1), (121, 125, 1), (125, 132, 2))
H_PIECE = {0: (0, 1, 2, 3), 1: (4, 5, 8, 9)}
GATE = {0: 6, 1: 10}
WIDE = 8

C_C = 0
C_NORM = C_C + KC
C_ADAB = C_NORM + 2 * KC
C_PSC = C_ADAB + len(PIECES) * HC
C_QK = C_PSC + HC
C_CW = C_QK + 4
C_CB = C_CW + HC * CONV_WIDTH
C_LG = C_CB + HC
C_LB = C_LG + HC
N_PAR = C_LB + HC


def units_at(w):
    first = 4 * UNITS
    for w0, w1, rate in UNIT_RATES:
        if w0 <= w < w1:
            return first + rate * (w - w0), rate
        first += rate * (w1 - w0)
    return None, 0


def conv_plan():
    ops = [(2 * m + s, k) for m in range(HC // 2) for k in range(CONV_WIDTH) for s in range(2)]
    plan, n = {}, 0
    for w0, w1, taps in ((72, 86, 7), (86, 94, 8), (94, 98, 3), (98, 101, 8), (101, 102, 4), (102, 104, 7),
                         (104, 106, 4), (106, 110, 6)):
        for w in range(w0, w1):
            plan[w] = ops[n:n + taps]
            assert all(w > max(AB1 + 2 * j + 1, AB1 + WIDE - 1) for j, _ in plan[w])
            n += taps
    assert n >= len(ops)
    return plan


def build(nc, xT, params, pool_w, w_slabs, ada_units, x1_dram, outT):
    ctx = ExitStack()
    with ctx:
        def sb(name, shape, dt=F32):
            return ctx.enter_context(nc.sbuf_tensor(name, shape, dt))

        def sem(name):
            return ctx.enter_context(nc.semaphore(name))

        raw = sb("raw", [P, 4, 8, P])
        whi = sb("whi", [P, 4, 8, P], F32R)
        wlo = sb("wlo", [P, 4, 8, P], F32R)
        ada = sb("ada", [P, 4, PIECE])
        acc = sb("acc", [P, 2, PIECE])
        hhi = sb("hhi", [P, KC, SEQ], F32R)
        hlo = sb("hlo", [P, KC, SEQ], F32R)
        ghi = sb("ghi", [P, KC, SEQ], F32R)
        glo = sb("glo", [P, KC, SEQ], F32R)
        X = sb("X", [P, KC, SEQ])
        V = sb("V", [P, QT, HALF])
        Y = sb("Y", [P, HC, SEQ])
        U = sb("U", [P, HC, PAD + SEQ])
        T = sb("T", [P, 2, SEQ])
        SG = sb("SG", [P, 2, SEQ])
        SP = sb("SP", [P, 2, KEYS])
        PTs = sb("PTs", [P, 2, KEYS])
        PD = sb("PD", [P, 2, QT, P])
        KD = sb("KD", [P, QT, P])
        D = sb("D", [P, KEYS])
        MK = sb("MK", [P, KEYS])
        DS = sb("DS", [P, 2, KEYS])
        ident = sb("ident", [P, P])
        ones = sb("ones", [P, P])
        QI = sb("QI", [P, IDX_HEADS // 2, SEQ])
        KW = sb("KW", [P, SEQ])
        KI = sb("KI", [P, SEQ])
        par = sb("par", [P, N_PAR])
        cact = sb("cact", [P, KC])
        tab = sb("tab", [P, 1])
        ctmp = sb("ctmp", [P, KC])
        mod = sb("mod", [P, len(PIECES) * HC])
        hgain = sb("hgain", [P, KC])
        st = sb("st", [P, 5, 2 * KC])
        rr = sb("rr", [P, 2 * KC])
        nm = sb("nm", [P, 2, QT])
        ls = sb("ls", [P, 2, QT])
        rl = sb("rl", [P, 2, QT])
        m8 = sb("m8", [P, QT, 8])
        wi = sb("wi", [P, QT, IDX_HEADS])
        lnh = sb("lnh", [P, 2 * HC])
        qgain = sb("qgain", [P, 2])
        rc = sb("rc", [P, 16])
        psum = [ctx.enter_context(nc.psum_tensor(f"bank{i}", [P, 512], F32)) for i in range(8)]
        Z, S, PT, O, M, XB = psum[0:2], psum[2:4], psum[4], psum[5], psum[6], psum[7]
        VX = V[:].rearrange("p a (b t) -> p (a b) t", t=SEQ)
        PW = V[:].rearrange("p a (b c) -> p (a b) c", c=512).rearrange("p g (k n) -> p g k n", k=2)
        poolA, poolB = (t[:].rearrange("p a b -> p (a b)")[:, 0:2 * (SEQ + 16)].rearrange("p (c t) -> p c t", c=2)
                        for t in (SP, PTs))

        par_in, x_in, pw_in = sem("par_in"), sem("x_in"), sem("pw_in")
        raw_in = [sem(f"raw_in{i}") for i in range(4)]
        ada_in = [sem(f"ada_in{i}") for i in range(4)]
        hi_done = sem("hi_done")
        lo_done = sem("lo_done")
        pe_half = sem("pe_half")
        z_free = [sem(f"z_free{i}") for i in range(2)]
        ada_done = sem("ada_done")
        acc_zero = sem("acc_zero")
        mod_sum = sem("mod_sum")
        mod_done = sem("mod_done")
        cexp = sem("cexp")
        const = sem("const")
        pool_self = sem("pool_self")
        dve_seq = sem("dve_seq")
        act_seq = sem("act_seq")
        sq_done = sem("sq_done")
        stat_done = sem("stat_done")
        var_ready = sem("var_ready")
        root_done = sem("root_done")
        diag_ready = sem("diag_ready")
        spread = sem("spread")
        rr_ready = sem("rr_ready")
        s_read = sem("s_read")
        xr_done = sem("xr_done")
        hhi_done = sem("hhi_done")
        hlo_done = sem("hlo_done")
        qk_stat = sem("qk_stat")
        tanh_done = sem("tanh_done")
        gated = sem("gated")
        ghi_done, glo_done = sem("ghi_done"), sem("glo_done")
        gain_ready = sem("gain_ready")
        xr_in = [sem(f"xr_in{i}") for i in range(4)]
        store = [sem(f"store{i}") for i in range(4)]
        d_ready, pool_mm, pool_out = sem("d_ready"), sem("pool_mm"), sem("pool_out")
        kdiag, kb_done, kmul = sem("kdiag"), sem("kb_done"), sem("kmul")
        ds_ready, scored, s_added, max_done = sem("ds_ready"), sem("scored"), sem("s_added"), sem("max_done")
        exp_done, pdiag, pt_done, pt_copied = sem("exp_done"), sem("pdiag"), sem("pt_done"), sem("pt_copied")
        pv_done, o_copied = sem("pv_done"), sem("o_copied")
        u_done = sem("u_done")
        wt_done, wi_ready = sem("wt_done"), sem("wi_ready")
        ki_in, cm_ready = sem("ki_in"), sem("cm_ready")
        logit, relu, score, mask_ready = sem("logit"), sem("relu"), sem("score"), sem("mask_ready")
        conv_seq = sem("conv_seq")
        mean_mm, ln_sub, ln_sq, var_mm = sem("mean_mm"), sem("ln_sub"), sem("ln_sq"), sem("var_mm")
        ln_mul, ln_act, ln_out = sem("ln_mul"), sem("ln_act"), sem("ln_out")

        N_TAPS = HC * CONV_WIDTH
        block = ctx.enter_context(nc.Block())

        def run(eng, w0, w1, step):
            with eng.Fori(0, (w1 - w0) // 2) as t:
                step(w0, t)
                step(w0 + 1, t)
            if (w1 - w0) % 2:
                step(w1 - 1, None)

        def now(w, t):
            return w if t is None else w + 2 * t

        def half_slot(w, half):
            return (2 * w + half) % 4

        def half_uses(w, half, t):
            n = (2 * w + half) // 4 + 1
            return n if t is None else n + t

        def x_written(eng, layer, count):
            last = (O0, O1)[layer] + count - 1
            for w in (last - 1, last):
                eng.wait_ge(z_free[w % 2], w // 2 + 2)

        def wide(s):
            return (Z[0], Z[1], S[0], S[1])[s // 2][:, s % 2 * SEQ:(s % 2 + 1) * SEQ]

        def flat(ap):
            return ap.rearrange("p a t -> p (a t)")

        def bank_uses(w, t):
            return w // 2 if t is None else w // 2 + t

        @block.sync
        def _(sp):
            sp.sem_inc(lo_done, 4)
            sp.sem_inc(ada_done, 4)
            sp.dma_start(par[:], params).then_inc(par_in, 16)
            sp.dma_start(X[:], xT).then_inc(x_in, 16)

            def load_units(n, count, t):
                for u in range(count):
                    slot = (n + u) % 4
                    unit = n + u if t is None else n + u + 4 * t
                    sp.wait_ge(ada_done, unit + 1)
                    sp.dma_start(ada[:, slot, :], ada_units[bass.ds(unit, 1)].rearrange("a p n -> p (a n)"))\
                      .then_inc(ada_in[slot], 16)

            def load_slab(w, t):
                for half in range(2):
                    slot = half_slot(w, half)
                    sp.wait_ge(lo_done, 2 * now(w, t) + half + 1)
                    sp.dma_start(raw[:, slot], w_slabs[bass.ds(now(w, t), 1), :, 8 * half:8 * half + 8, :]
                                 .rearrange("a p k n -> p (a k) n")).then_inc(raw_in[slot], 16)

            for p in range(4):
                with sp.Fori(0, 2) as t:
                    load_units(UNITS * p, 4, t)
                load_slab(2 * p, None)
                load_slab(2 * p + 1, None)
                with sp.Fori(0, 2) as t:
                    load_units(UNITS * p + 8, 4, t)

            def step(w, t):
                load_slab(w + AHEAD, t)
                load_units(*units_at(w), t)

            for w0, w1 in ((6, 8), (8, 32), (32, 48), (48, 62), (62, 72), (72, 110), (110, 125), (125, 131),
                           (131, 132), (132, N_SLABS - AHEAD)):
                if w0 in (32, 62, 110, 131):
                    for w in range(w0, w1):
                        step(w, None)
                else:
                    run(sp, w0, w1, step)

        @block.gpsimd
        def _(pool):
            n = [0]

            def own(ins):
                n[0] += 1
                ins.then_inc(pool_self, 1)
                pool.wait_ge(pool_self, n[0])

            pool.memset(acc[:, 0, :], 0.0).then_inc(acc_zero, 1)
            pool.memset(acc[:, 1, :], 0.0).then_inc(acc_zero, 1)
            pool.memset(tab[:], 1.0).then_inc(const, 1)
            pool.memset(ones[:], 1.0).then_inc(const, 1)
            own(pool.memset(ident[:], 0.0))
            pool.affine_select(out=ident[:], in_=ident[:], compare_op=ALU.not_equal, fill=1.0, base=0,
                               pattern=[[-1, P]], channel_multiplier=1).then_inc(const, 1)
            pool.memset(U[:, :, 0:PAD], 0.0).then_inc(const, 1)
            pool.iota(rc[:], pattern=[[1, 16]], base=1, channel_multiplier=0,
                      allow_small_or_imprecise_dtypes=True).then_inc(const, 1)
            for c0, c1, q0 in ((0, P, 0), (P, KEYS, P)):
                own(pool.iota(D[:, c0:c1], pattern=[[1, c1 - c0]], base=-q0, channel_multiplier=-1,
                              allow_small_or_imprecise_dtypes=True))
                own(pool.affine_select(out=D[:, c0:c1], in_=D[:, c0:c1], compare_op=ALU.is_ge, fill=-BIG,
                                       base=q0, pattern=[[-1, c1 - c0]], channel_multiplier=1))

            def clear(piece):
                pool.wait_ge(mod_sum, piece - 1)
                pool.memset(acc[:, piece % 2, :], 0.0).then_inc(acc_zero, 1)

            def slopes(layer, heads=range(HC)):
                mask = D if layer == 0 else MK
                for h in heads:
                    a = HC * layer + h
                    if a >= 2:
                        pool.wait_ge(s_added, a - 1)
                    pool.tensor_scalar(DS[:, a % 2, :], mask[:], 2.0 ** -(h + 1), None, ALU.mult)\
                        .then_inc(ds_ready, 1)

            def load_x(layer, m):
                src = xT if layer == 0 else x1_dram
                if m >= 2:
                    pool.wait_ge(pv_done, HC * (layer + 1))
                    out = VX[:, 4 * (m - 2):4 * (m - 1), :]
                elif layer == 0:
                    pool.wait_ge(d_ready, 4)
                    out = U[:, 4 * m:4 * (m + 1), PAD:PAD + SEQ]
                else:
                    pool.wait_ge(ln_out, HC)
                    out = U[:, 4 * m:4 * (m + 1), PAD:PAD + SEQ]
                pool.dma_start(out, src[:, 4 * m:4 * m + 4, :]).then_inc(xr_in[m], 16)

            def store_x(layer, m):
                x_written(pool, layer, 4 * (m + 1))
                pool.dma_start((x1_dram if layer == 0 else outT)[:, 4 * m:4 * m + 4, :],
                               X[:, 4 * m:4 * m + 4, :]).then_inc(store[m], 16)

            clear(2)
            clear(3)
            clear(4)
            clear(5)
            pool.dma_start(PW, pool_w).then_inc(pw_in, 16)
            clear(6)
            load_x(0, 0)
            load_x(0, 1)
            slopes(0, range(0, 2))
            clear(7)
            slopes(0, range(2, HC))
            load_x(0, 2)
            load_x(0, 3)
            own(pool.memset(PTs[:, 0, :], 0.0))
            for c0, c1, q0 in ((0, P, 0), (P, KEYS, P)):
                pool.affine_select(out=PTs[:, 0, c0:c1], in_=PTs[:, 0, c0:c1], compare_op=ALU.is_ge,
                                   fill=NEG_INF, base=q0, pattern=[[-1, c1 - c0]],
                                   channel_multiplier=1).then_inc(cm_ready, 1)
            clear(8)
            clear(9)
            store_x(0, 0)
            store_x(0, 1)
            clear(10)
            store_x(0, 2)
            store_x(0, 3)
            clear(11)
            pool.wait_ge(z_free[KW1 % 2], KW1 // 2 + 2)
            pool.dma_start(KI[IDX_DIM:2 * IDX_DIM, :], KW[0:IDX_DIM, :]).then_inc(ki_in, 16)
            pool.wait_ge(mask_ready, 1)
            slopes(1)
            for m in range(4):
                pool.wait_ge(store[m], 16)
            load_x(1, 2)
            load_x(1, 3)
            load_x(1, 0)
            load_x(1, 1)
            for m in range(4):
                store_x(1, m)
            for m in range(4):
                pool.wait_ge(store[m], 32)

        @block.scalar
        def _(act):
            act.sem_inc(pe_half, 4)
            n = [0]

            def own(ins):
                n[0] += 1
                ins.then_inc(act_seq, 1)
                act.wait_ge(act_seq, n[0])

            def hi(w, t, halves=(0, 1)):
                for half in halves:
                    slot = half_slot(w, half)
                    act.wait_ge(raw_in[slot], 16 * half_uses(w, half, t))
                    act.wait_ge(pe_half, 2 * now(w, t) + half + 1)
                    act.activation(whi[:, slot], raw[:, slot], ACT.Copy).then_inc(hi_done, 1)

            def product(w, t):
                act.wait_ge(pe_half, 2 * now(w, t) + 2 + 4)

            def root(i, cols):
                act.wait_ge(var_ready, i + 1)
                act.activation(st[:, 1, 0:cols], st[:, 0, 0:cols], ACT.Sqrt).then_inc(root_done, 1)

            def square_x(i, j):
                if i >= 2:
                    act.wait_ge(stat_done, i - 1)
                act.activation(T[:, i % 2, :], X[:, j, :], ACT.Square).then_inc(sq_done, 1)

            def upper_h(layer, chunks):
                for j in chunks:
                    col = HC * H_PIECE[layer][j // GROUP] + GROUP + j % GROUP
                    act.wait_ge(xr_done, KC * layer + j + 1)
                    act.activation(hhi[:, j, :], X[:, j, :], ACT.Identity, bias=mod[:, col:col + 1])\
                        .then_inc(hhi_done, 1)

            def step_qk(w, t, q0, kind, layer):
                hi(w + AHEAD, t)
                product(w, t)
                gain = qgain[:, layer:layer + 1] if kind == "q" else 1.0
                act.activation(X[:, bass.ds(now(w, t) - q0, 1), :].rearrange("p a t -> p (a t)"),
                               Z[w % 2][:, 0:SEQ], ACT.Copy, scale=gain)
                act.activation(T[:, w % 2, :], Z[w % 2][:, 0:SEQ], ACT.Square).then_inc(z_free[w % 2], 1)

            def evict_v(w, v0, layer):
                pair = (w - v0) // 2
                if (w - v0) % 2:
                    product(w, None)
                    act.activation(V[:, :, 2 * P * pair:2 * P * (pair + 1)],
                                   Z[(v0 + pair) % 2][:].rearrange("p (a b) -> p a b", a=QT), ACT.Copy)\
                       .then_inc(z_free[(v0 + pair) % 2], 2)

            def tanh_gate(w, t, g0, layer):
                product(w, t)
                i = KC * layer + now(w, t) - g0
                if t is not None or i >= 2:
                    act.wait_ge(gated, i - 1)
                act.activation(T[:, w % 2, :], Z[w % 2][:, 0:SEQ], ACT.Tanh, scale=0.5).then_inc(tanh_done, 1)

            def round_gated(w, t, g0, layer):
                c = now(w, t) - g0
                act.wait_ge(gated, KC * layer + c + 1)
                act.activation(ghi[:, bass.ds(c, 1), :].rearrange("p a t -> p (a t)"), SG[:, w % 2, :],
                               ACT.Copy).then_inc(ghi_done, 1)

            def step_g(w, t, g0, layer):
                hi(w + AHEAD, t)
                tanh_gate(w, t, g0, layer)
                round_gated(w - 1, t, g0, layer)

            def attend(layer, i):
                if 0 <= i + 2 < HC:
                    a = HC * layer + i + 2
                    if i + 2 == 0:
                        act.wait_ge(rr_ready, layer + 1)
                    if a:
                        act.wait_ge(kb_done, a)
                    for q in range(QT):
                        col = KC * q + HC + i + 2
                        e = act.activation(KD[:, q, :], ident[:], ACT.Copy, scale=rr[:, col:col + 1])
                    e.then_inc(kdiag, 1)
                if 0 <= i - 1 < HC:
                    a = HC * layer + i - 1
                    act.wait_ge(pt_done, a + 1)
                    if a >= 2:
                        act.wait_ge(pv_done, a - 1)
                    act.activation(PTs[:, a % 2, :], PT[:, 0:KEYS], ACT.Copy).then_inc(pt_copied, 1)
                if 0 <= i - 2 < HC:
                    a = HC * layer + i - 2
                    act.wait_ge(pv_done, a + 1)
                    act.activation(X[:, i - 2, :], O[:, 0:SEQ], ACT.Copy).then_inc(o_copied, 1)
                if 0 <= i < HC:
                    a = HC * layer + i
                    act.wait_ge(max_done, a + 1)
                    for q, (c0, c1) in enumerate(((0, P), (P, KEYS))):
                        e = act.activation(SP[:, a % 2, c0:c1], SP[:, a % 2, c0:c1], ACT.Exp,
                                           bias=nm[:, a % 2, q:q + 1], accum_out=ls[:, a % 2, q:q + 1])
                        e.then_inc(exp_done, 1)

            def pool_evict(g):
                act.wait_ge(pool_mm, g + 1)
                for o in range(2):
                    j = 2 * g + o
                    act.activation(Y[:, j, :], PT[:, o * SEQ:(o + 1) * SEQ], ACT.Copy,
                                   scale=par[:, C_PSC + j:C_PSC + j + 1]).then_inc(pool_out, 1)

            def warm(func):
                act.activation(tab[:], tab[:], func)

            act.wait_ge(par_in, 16)
            act.activation(ctmp[:], par[:, C_C:C_C + KC], ACT.Exp, scale=-1.0).then_inc(cexp, 1)
            for l in range(2):
                own(act.activation(qgain[:, l:l + 1], par[:, C_QK + 2 * l:C_QK + 2 * l + 1], ACT.Copy,
                                   scale=float(P) ** -0.5))
            act.activation(lnh[:], par[:, C_LG:C_LG + 2 * HC], ACT.Copy, scale=0.5).then_inc(act_seq, 1)
            n[0] += 1
            act.wait_ge(x_in, 16)
            for j in range(KC):
                square_x(j, j)
            hi(0, None)
            hi(1, None)
            root(0, QT)
            for g in range(KC // GROUP):
                upper_h(0, range(GROUP * g, GROUP * (g + 1)))
                hi(2 * g + 2, None)
                if g == 3:
                    act.wait_ge(pe_half, 2 * WIDE + 4)
                    for s in range(WIDE):
                        read = act.activation(U[:, s, PAD:PAD + SEQ], wide(s), ACT.Copy)
                        if s < 4:
                            read.then_inc(z_free[s // 2], 2)
                        else:
                            read.then_inc(s_read, 1)
                hi(2 * g + 3, None)
            step_qk(8, None, Q0, "q", 0)
            step_qk(9, None, Q0, "q", 0)
            pool_evict(0)
            run(act, 10, 16, lambda w, t: step_qk(w, t, Q0, "q", 0))
            step_qk(16, None, Q0, "k", 0)
            pool_evict(1)
            step_qk(17, None, Q0, "k", 0)
            pool_evict(2)
            run(act, 18, V0, lambda w, t: step_qk(w, t, Q0, "k", 0))
            for w in range(V0, G0 + 5):
                hi(w + AHEAD, None)
                if w < G0:
                    evict_v(w, V0, 0)
                else:
                    tanh_gate(w, None, G0, 0)
                if w == V0:
                    pool_evict(3)
                    root(1, 2 * KC)
                attend(0, w - V0 - 3)
                if w > G0:
                    round_gated(w - 1, None, G0, 0)
            step_g(37, None, G0, 0)
            run(act, 38, O0, lambda w, t: step_g(w, t, G0, 0))

            def square_new(j, t):
                w = O0 + j
                act.wait_ge(z_free[w % 2], bank_uses(w, t) + 2)
                act.wait_ge(stat_done, KC + now(j, t) - 1)
                act.activation(T[:, j % 2, :], flat(X[:, bass.ds(now(j, t), 1), :]), ACT.Square)\
                   .then_inc(sq_done, 1)

            def step_o0(w, t):
                hi(w + AHEAD, t, (0,))
                square_new(w - O0 - 1, t)
                hi(w + AHEAD, t, (1,))

            round_gated(O0 - 1, None, G0, 0)
            hi(O0 + AHEAD, None)
            step_o0(49, None)
            run(act, 50, AB1 - 2, step_o0)
            step_o0(AB1 - 2, None)
            hi(AB1 + 1, None, (0,))
            square_new(KC - 2, None)
            warm(ACT.Sqrt)
            square_new(KC - 1, None)
            root(2, QT)
            hi(AB1 + 1, None, (1,))
            upper_h(1, range(0, 8))
            for w in (66, 67):
                hi(w, None)
            upper_h(1, range(8, 12))
            for w in (68, 69):
                hi(w, None)
            upper_h(1, range(12, 14))
            hi(70, None)
            upper_h(1, range(14, 16))

            def step_ab(w, t):
                hi(w + AHEAD, t)
                product(w, t)
                pair = (w - AB1) // 2
                if w % 2 == 0:
                    if t is not None or pair > 0:
                        act.wait_ge(u_done, pair if t is None else pair + t)
                    act.activation(T[:, 0, :], Z[0][:, 0:SEQ], ACT.Copy, scale=0.5).then_inc(z_free[0], 1)
                else:
                    act.activation(T[:, 1, :], Z[1][:, 0:SEQ], ACT.Tanh, scale=0.5).then_inc(z_free[1], 1)

            warm(ACT.Tanh)
            for w in (71, 72):
                hi(w, None)
            act.wait_ge(pe_half, 2 * (AB1 + WIDE) + 4)
            for pair in range(4):
                half_a, tanh_b = (T, SG)[pair % 2][:, 0, :], (T, SG)[pair % 2][:, 1, :]
                if pair >= 2:
                    act.wait_ge(u_done, pair - 1)
                for out, s, func in ((half_a, 2 * pair, ACT.Copy), (tanh_b, 2 * pair + 1, ACT.Tanh)):
                    read = act.activation(out, wide(s), func, scale=0.5)
                    if pair < 2:
                        read.then_inc(z_free[pair], 2)
                    else:
                        read.then_inc(s_read, 1)
            hi(73, None)
            step_ab(72, None)
            step_ab(73, None)
            run(act, 74, QI1, step_ab)

            def step_qi(w, t):
                hi(w + AHEAD, t)
                product(w, t)
                act.activation(QI[:, bass.ds(now(w, t) - QI1, 1), :].rearrange("p a t -> p (a t)"),
                               Z[w % 2][:, 0:SEQ], ACT.Copy).then_inc(z_free[w % 2], 1)

            run(act, QI1, KW1, step_qi)
            hi(KW1 + AHEAD, None)
            product(KW1, None)
            act.activation(KW[:], Z[KW1 % 2][:, 0:SEQ], ACT.Copy).then_inc(z_free[KW1 % 2], 1)
            step_qk(85, None, Q1, "q", 1)
            for w in range(86, 94):
                step_qk(w, None, Q1, "q" if w < 93 else "k", 1)
                hh = w - 86
                act.wait_ge(logit, hh + 1)
                if hh >= 2:
                    act.wait_ge(score, 2 * (hh - 1))
                act.activation(SP[:, hh % 2, :], S[hh % 2][:, 0:KEYS], ACT.Relu,
                               scale=float(IDX_DIM) ** -0.5).then_inc(relu, 1)
            run(act, 94, V1, lambda w, t: step_qk(w, t, Q1, "k", 1))
            def normed(chunks):
                for j in chunks:
                    act.wait_ge(ln_mul, j + 1)
                    act.activation(U[:, j, 0:SEQ], Y[:, j, :], ACT.Tanh, bias=lnh[:, HC + j:HC + j + 1],
                                   scale=lnh[:, j:j + 1])
                    act.activation(Y[:, j, :], Y[:, j, :], ACT.Identity,
                                   bias=par[:, C_LB + j:C_LB + j + 1],
                                   scale=par[:, C_LG + j:C_LG + j + 1]).then_inc(ln_act, 1)

            for w in range(V1, 117):
                if w == 114:
                    root(4, QT)
                hi(w + AHEAD, None)
                if w < G1:
                    evict_v(w, V1, 1)
                else:
                    tanh_gate(w, None, G1, 1)
                if w == V1:
                    root(3, 2 * KC)
                attend(1, w - V1 - 3)
                if w > G1:
                    round_gated(w - 1, None, G1, 1)
                if w == 111:
                    act.wait_ge(ln_sub, 1)
                    act.activation(U[:, :, 0:SEQ], Y[:], ACT.Square).then_inc(ln_sq, 1)
                if w in (115, 116):
                    normed(range(2 * (w - 115), 2 * (w - 114)))
            for w in (117, 118):
                step_g(w, None, G1, 1)
                normed(range(2 * (w - 115), 2 * (w - 114)))
            run(act, 119, O1, lambda w, t: step_g(w, t, G1, 1))
            round_gated(O1 - 1, None, G1, 1)
            hi(O1 + AHEAD, None)
            run(act, O1 + 1, N_SLABS - AHEAD, lambda w, t: hi(w + AHEAD, t))

        @block.tensor
        def _(pe):
            for b in range(2):
                pe.sem_inc(z_free[b], 1)
            mm = nc.tensor.matmul

            def keep_warm(count):
                for _ in range(count):
                    mm(PT[:, 0:P], ones[:], ident[:], start=True, stop=True)

            def slab(w, t, ahi, alo, gated_last=None, between=None):
                out = Z[w % 2][:, 0:SEQ]
                pe.wait_ge(z_free[w % 2], bank_uses(w, t) + 1)
                for half in range(2):
                    s = half_slot(w, half)
                    pe.wait_ge(lo_done, 2 * now(w, t) + half + 1 + 4)
                    for k in range(8):
                        c = 8 * half + k
                        if gated_last is not None and c >= KC - 2:
                            pe.wait_ge(glo_done, gated_last - KC + c + 1)
                        mm(out, whi[:, s, k, :], ahi[:, c, :], start=(c == 0), stop=False)
                        mm(out, whi[:, s, k, :], alo[:, c, :], start=False, stop=False)
                        last = mm(out, wlo[:, s, k, :], ahi[:, c, :], start=False, stop=(c == KC - 1))
                        if between is not None and c < KC - 1:
                            between(c)
                    last.then_inc(pe_half, 1)

            def wide_chunk(layer, w0, c):
                w, half = w0 + c // 2, c % 2
                slot = half_slot(w, half)
                pe.wait_ge(lo_done, 2 * w + half + 1 + 4)
                pe.wait_ge(hlo_done, KC * layer + c + 1)
                for s in range(WIDE):
                    mm(wide(s), whi[:, slot, s, :], hhi[:, c, :], start=(c == 0 and s % 2 == 0), stop=False,
                       skip_group_check=True)
                    mm(wide(s), whi[:, slot, s, :], hlo[:, c, :], start=False, stop=False, skip_group_check=True)
                    last = mm(wide(s), wlo[:, slot, s, :], hhi[:, c, :], start=False, stop=(c == KC - 1),
                              skip_group_check=True)
                last.then_inc(pe_half, 1)

            def slab_h(w, t):
                slab(w, t, hhi, hlo)

            def slab_g(w, t):
                slab(w, t, ghi, glo)

            def by_token(bank, chunk, first, last):
                for q in range(QT):
                    ins = mm(bank[:, q:q + 1], chunk[:, q * P:(q + 1) * P], ones[:, 0:1],
                             start=(first and q == 0), stop=last, skip_group_check=True)
                return ins

            def x_stat(i, runtime=None):
                pe.wait_ge(sq_done, (i if runtime is None else runtime) + 1)
                by_token(M, T[:, i % 2, :], i % KC == 0, i % KC == KC - 1).then_inc(stat_done, 1)

            def spread_token(i):
                pe.wait_ge(diag_ready, i + 1)
                for q in range(QT):
                    ins = mm(XB[:, q * P:(q + 1) * P], ones[:], KD[:, q, :], start=True, stop=True)
                ins.then_inc(spread, 1)

            def reduce_piece(p):
                pe.wait_ge(ada_done, UNITS * (p + 1) + 4)
                if p >= 1:
                    pe.wait_ge(mod_done, p)
                if p >= 6:
                    pe.wait_ge(o_copied, HC if p < 10 else 2 * HC)
                for j in range(HC):
                    ins = mm(O[:, j:j + 1], acc[:, p % 2, j * P:(j + 1) * P], ones[:, 0:1],
                             start=True, stop=True)
                ins.then_inc(mod_sum, 1)

            def qk_stats(w, t, q0):
                pe.wait_ge(z_free[w % 2], bank_uses(w, t) + 2)
                for q in range(QT):
                    ins = mm(M[:, bass.ds(q * KC + now(w, t) - q0, 1)], T[:, w % 2, q * P:(q + 1) * P],
                             ones[:, 0:1], start=True, stop=True)
                ins.then_inc(qk_stat, 1)

            def pool_product(g):
                pe.wait_ge(d_ready, g + 1)
                if g:
                    pe.wait_ge(pool_out, 2 * g)
                for o in range(2):
                    for k in range(2):
                        ins = mm(PT[:, o * SEQ:(o + 1) * SEQ], PW[:, g, k, o * P:(o + 1) * P],
                                 Y[:, 2 * g + k, :], start=(k == 0), stop=(k == 1))
                ins.then_inc(pool_mm, 1)

            def slab_v(w, v0):
                pair, second = (w - v0) // 2, (w - v0) % 2
                b = (v0 + pair) % 2
                bank = Z[b]
                if not second:
                    pe.wait_ge(z_free[b], (v0 + 1 - b) // 2 + 1 + 2 * (pair // 2))
                for half in range(2):
                    s = half_slot(w, half)
                    pe.wait_ge(lo_done, 2 * w + half + 1 + 4)
                    for k in range(4):
                        c = 8 * second + 4 * half + k
                        upper, lower = flat(whi[:, s, 2 * k:2 * k + 2, :]), flat(wlo[:, s, 2 * k:2 * k + 2, :])
                        for q in range(QT):
                            out, tokens = bank[:, q * SEQ:(q + 1) * SEQ], slice(q * P, (q + 1) * P)
                            mm(out, hhi[:, c, tokens], upper, start=(c == 0 and q == 0), stop=False,
                               skip_group_check=True)
                            mm(out, hlo[:, c, tokens], upper, start=False, stop=False, skip_group_check=True)
                            last = mm(out, hhi[:, c, tokens], lower, start=False, stop=(c == KC - 1),
                                      skip_group_check=True)
                    last.then_inc(pe_half, 1)

            def attend(layer, v0, w):
                i = w - v0 - 3
                if 0 <= i + 1 < HC:
                    a = HC * layer + i + 1
                    pe.wait_ge(kdiag, a + 1)
                    if a:
                        pe.wait_ge(kmul, a)
                    for q in range(QT):
                        ins = mm(M[:, q * P:(q + 1) * P], ones[:], KD[:, q, :], start=True, stop=True)
                    ins.then_inc(kb_done, 1)
                if 0 <= i < HC:
                    a = HC * layer + i
                    pe.wait_ge(kmul, a + 1)
                    if i == 0:
                        pe.wait_ge(s_read, 4 * (layer + 1))
                    if a >= 2:
                        pe.wait_ge(s_added, a - 1)
                    mm(S[a % 2][:, 0:P], X[:, i, 0:P], X[:, HC + i, 0:P], start=True, stop=True)
                    mm(S[a % 2][:, P:KEYS], X[:, i, P:SEQ], X[:, HC + i, :], start=True, stop=True)\
                        .then_inc(scored, 1)
                if 0 <= i - 1 < HC:
                    a = HC * layer + i - 1
                    pe.wait_ge(pdiag, a + 1)
                    if a:
                        pe.wait_ge(pt_copied, a)
                    else:
                        pe.wait_ge(pool_out, HC)
                    for out, keys, q in ((0, 0, 0), (P, P, 1), (2 * P, 2 * P, 1)):
                        ins = mm(PT[:, out:out + P], SP[:, a % 2, keys:keys + P], PD[:, a % 2, q, :],
                                 start=True, stop=True)
                    ins.then_inc(pt_done, 1)
                if 0 <= i - 2 < HC:
                    a, h = HC * layer + i - 2, i - 2
                    pe.wait_ge(pt_copied, a + 1)
                    b = (v0 + h // 2) % 2
                    pe.wait_ge(z_free[b], (v0 + 1 - b) // 2 + 1 + 2 * (h // 4 + 1))
                    pe.wait_ge(mod_done, 6 if layer == 0 else 10)
                    if a:
                        pe.wait_ge(o_copied, a)
                    mm(O[:, 0:SEQ], V[:, 0, h * P:(h + 1) * P], PTs[:, a % 2, 0:SEQ], start=True, stop=False)
                    mm(O[:, P:SEQ], V[:, 1, h * P:(h + 1) * P], PTs[:, a % 2, SEQ:KEYS],
                       start=False, stop=True).then_inc(pv_done, 1)

            def logits(hh):
                c, p0 = hh // 2, IDX_DIM * (hh % 2)
                keys = KW if p0 == 0 else KI
                if hh == 0:
                    pe.wait_ge(z_free[KW1 % 2], KW1 // 2 + 2)
                    pe.wait_ge(s_read, 8)
                if hh == 1:
                    pe.wait_ge(ki_in, 16)
                if hh >= 2:
                    pe.wait_ge(relu, hh - 1)
                mm(S[hh % 2][:, 0:P], QI[p0:p0 + IDX_DIM, c, 0:P], keys[p0:p0 + IDX_DIM, 0:P],
                   start=True, stop=True)
                mm(S[hh % 2][:, P:KEYS], QI[p0:p0 + IDX_DIM, c, P:SEQ], keys[p0:p0 + IDX_DIM, :],
                   start=True, stop=True).then_inc(logit, 1)

            pe.wait_ge(const, 3)
            for i in range(KC):
                x_stat(i)
            spread_token(0)
            for p in range(4):
                if p == 3:
                    pe.wait_ge(ada_done, UNITS * p + 13 + 4)
                    keep_warm(24)
                reduce_piece(p)
                keep_warm(9 if p == 3 else 0)
                for c in range(GROUP * p, GROUP * (p + 1)):
                    wide_chunk(0, U0, c)

            def slab_stat(q0):
                def step(w, t):
                    slab_h(w, t)
                    qk_stats(w - 1, t, q0)
                return step

            slab_h(8, None)
            slab_h(9, None)
            qk_stats(8, None, Q0)
            pe.wait_ge(pw_in, 16)
            pool_product(0)
            run(pe, 10, 16, slab_stat(Q0))
            slab_stat(Q0)(16, None)
            pool_product(1)
            slab_stat(Q0)(17, None)
            pool_product(2)
            reduce_piece(4)
            run(pe, 18, V0, slab_stat(Q0))
            for w in range(V0, G0 + 5):
                if w == V0 + 2:
                    reduce_piece(5)
                if w < G0:
                    slab_v(w, V0)
                else:
                    slab_h(w, None)
                if w == V0:
                    qk_stats(w - 1, None, Q0)
                    pool_product(3)
                attend(0, V0, w)
            run(pe, 37, 42, slab_h)
            reduce_piece(6)
            run(pe, 42, O0, slab_h)

            pe.wait_ge(glo_done, KC - 2)
            slab(48, None, ghi, glo, KC)
            slab_g(49, None)
            reduce_piece(7)
            slab_g(50, None)
            x_stat(KC)
            slab_g(51, None)
            x_stat(KC + 1)

            def slab_x(w, t):
                slab_g(w, t)
                x_stat(KC + w - O0 - 2, runtime=KC + now(w, t) - O0 - 2)

            run(pe, 52, 56, slab_x)
            slab_x(56, None)
            slab_x(57, None)
            reduce_piece(8)
            run(pe, 58, AB1, slab_x)
            x_stat(2 * KC - 2)
            keep_warm(7)
            x_stat(2 * KC - 1)
            keep_warm(9)
            spread_token(1)
            keep_warm(9)

            pe.wait_ge(s_added, HC)
            for c in range(KC):
                if c == 2 * GROUP:
                    reduce_piece(9)
                wide_chunk(1, AB1, c)
            run(pe, AB1 + WIDE, KW1, slab_h)
            slab_h(KW1, None)
            slab_h(85, None)
            pe.wait_ge(z_free[KW1 % 2], KW1 // 2 + 2)
            for q in range(QT):
                ins = nc.tensor.transpose(XB[:, q * P:(q + 1) * P], KW[:, q * P:(q + 1) * P], ident[:])
            ins.then_inc(wt_done, 1)
            for w in range(86, 94):
                slab_stat(Q1)(w, None)
                logits(w - 86)
            run(pe, 94, V1, slab_stat(Q1))
            for w in range(V1, 117):
                if w < G1:
                    slab_v(w, V1)
                elif w == 113:
                    pe.wait_ge(ln_sq, 1)
                    slab(w, None, hhi, hlo, between=lambda c: c < HC and
                         by_token(XB, U[:, c, 0:SEQ], c == 0, c == HC - 1))
                    pe.sem_inc(var_mm, 1)
                else:
                    slab_h(w, None)
                if w == V1:
                    qk_stats(w - 1, None, Q1)
                attend(1, V1, w)
                if w == 110:
                    pe.wait_ge(conv_seq, N_TAPS)
                    for j in range(HC):
                        ins = mm(XB[:, 0:SEQ], ones[:], Y[:, j, :], start=(j == 0), stop=(j == HC - 1))
                    ins.then_inc(mean_mm, 1)
                if w == 114:
                    spread_token(2)
            run(pe, 117, 124, slab_h)
            reduce_piece(10)
            slab_h(124, None)
            pe.wait_ge(glo_done, 2 * KC - 2)
            slab(125, None, ghi, glo, 2 * KC)
            run(pe, 126, 134, slab_g)
            reduce_piece(11)
            run(pe, 134, N_SLABS, slab_g)

        @block.vector
        def _(dve):
            n = [0]

            def seq(ins):
                n[0] += 1
                ins.then_inc(dve_seq, 1)

            def settle():
                dve.wait_ge(dve_seq, n[0])

            def lo(w, t, halves=(0, 1)):
                for half in halves:
                    s = half_slot(w, half)
                    dve.wait_ge(hi_done, 2 * now(w, t) + half + 1)
                    dve.tensor_tensor(wlo[:, s], raw[:, s], whi[:, s].bitcast(F32), ALU.subtract)\
                        .then_inc(lo_done, 1)

            def add_units(first, count, t):
                for u in range(count):
                    unit = first + u if t is None else first + u + 4 * t
                    slot, p = (first + u) % 4, first // UNITS
                    uses = (first + u) // 4 + 1
                    k = unit - UNITS * p
                    dve.wait_ge(ada_in[slot], 16 * (uses if t is None else uses + t))
                    dve.wait_ge(ada_done, unit + 4)
                    dve.scalar_tensor_tensor(acc[:, p % 2, :], ada[:, slot, :], cact[:, bass.ds(k, 1)],
                                             acc[:, p % 2, :], ALU.mult, ALU.add).then_inc(ada_done, 1)

            def units(w, t):
                first, count = units_at(w)
                if count:
                    if t is None and first % UNITS == 0:
                        dve.wait_ge(acc_zero, first // UNITS + 1)
                    add_units(first, count, t)

            def keep_piece(p):
                dve.wait_ge(mod_sum, p + 1)
                dve.tensor_tensor(mod[:, p * HC:(p + 1) * HC], O[:, 0:HC],
                                  par[:, C_ADAB + p * HC:C_ADAB + (p + 1) * HC], ALU.add).then_inc(mod_done, 1)

            def make_gain(layer, g):
                p, col = H_PIECE[layer][g], C_NORM + KC * layer + GROUP * g
                dve.wait_ge(mod_done, p + 1)
                dve.scalar_tensor_tensor(hgain[:, GROUP * g:GROUP * (g + 1)], mod[:, p * HC:p * HC + GROUP], 1.0,
                                         par[:, col:col + GROUP], ALU.add, ALU.mult).then_inc(gain_ready, 1)

            def rsqrt(i, cols, src, count):
                a, s, r, y = (st[:, k, 0:cols] for k in (0, 1, 2, 3))
                dve.tensor_scalar(a, src, 1.0 / count, EPS, ALU.mult, ALU.add).then_inc(var_ready, 1)
                dve.wait_ge(root_done, i + 1)
                seq(dve.reciprocal(r, s))
                settle()
                seq(dve.tensor_tensor(y, r, r, ALU.mult))
                settle()
                seq(dve.scalar_tensor_tensor(st[:, 4, 0:cols], y, -0.5, a, ALU.mult, ALU.mult))
                settle()
                seq(dve.scalar_tensor_tensor(rr[:, 0:cols], st[:, 4, 0:cols], 1.5, r, ALU.add, ALU.mult))
                settle()

            def token_diag():
                for q in range(QT):
                    ins = dve.tensor_scalar(KD[:, q, :], ident[:], rr[:, q:q + 1], None, ALU.mult)
                ins.then_inc(diag_ready, 1)

            def norm_x(layer, j):
                dve.wait_ge(gain_ready, 4 * layer + j // GROUP + 1)
                if layer and j % 4 == 0:
                    dve.wait_ge(store[j // 4], 16)
                dve.scalar_tensor_tensor(X[:, j, :], X[:, j, :], hgain[:, j:j + 1], XB[:, 0:SEQ],
                                         ALU.mult, ALU.mult).then_inc(xr_done, 1)

            def lower_h(layer, j):
                col = HC * H_PIECE[layer][j // GROUP] + GROUP + j % GROUP
                dve.wait_ge(xr_done, KC * layer + j + 1)
                dve.wait_ge(hhi_done, KC * layer + j + 1)
                dve.scalar_tensor_tensor(hlo[:, j, :], X[:, j, :], mod[:, col:col + 1],
                                         hhi[:, j, :].bitcast(F32), ALU.add, ALU.subtract).then_inc(hlo_done, 1)

            def make_h(layer, chunks, lead=2):
                for i in range(len(chunks) + lead):
                    if i < len(chunks):
                        norm_x(layer, chunks[i])
                    if i >= lead:
                        lower_h(layer, chunks[i - lead])

            def gate(w, t, g0, layer):
                i = KC * layer + now(w, t) - g0
                half, j = (w - g0) // HC, now(w, t) - g0 - HC * ((w - g0) // HC)
                src = (Y, X)[half] if layer == 0 else (X, Y)[half]
                factor = 0.25 if (layer == 1 and half == 1) else 0.5
                dve.wait_ge(tanh_done, i + 1)
                dve.scalar_tensor_tensor(SG[:, w % 2, :], T[:, w % 2, :], 1.0, Z[w % 2][:, 0:SEQ],
                                         ALU.add, ALU.mult).then_inc(z_free[w % 2], 1)
                if src is X and t is None:
                    dve.wait_ge(o_copied, i + 1 - HC * (1 + layer) if layer == 0 else HC + (w - g0) + 1)
                dve.wait_ge(z_free[w % 2], bank_uses(w, t) + 2)
                dve.scalar_tensor_tensor(SG[:, w % 2, :], flat(src[:, bass.ds(j, 1), :]), factor,
                                         SG[:, w % 2, :], ALU.mult, ALU.mult).then_inc(gated, 1)

            def split_gated(w, t, g0, layer):
                c = now(w, t) - g0
                dve.wait_ge(ghi_done, KC * layer + c + 1)
                dve.tensor_tensor(flat(glo[:, bass.ds(c, 1), :]), SG[:, w % 2, :],
                                  flat(ghi[:, bass.ds(c, 1), :]).bitcast(F32), ALU.subtract)\
                    .then_inc(glo_done, 1)

            def add_x(w, t, o0, layer):
                j = now(w, t) - o0
                second, seg = (w - o0) // HC, (w - o0) % HC
                dve.wait_ge(pe_half, 2 * now(w, t) + 2 + 4)
                gcol = GATE[layer] * HC
                seg = seg if t is None else seg + 2 * t
                x = VX[:, bass.ds(seg, 1), :] if second else U[:, bass.ds(seg, 1), PAD:PAD + SEQ]
                dve.scalar_tensor_tensor(flat(X[:, bass.ds(j, 1), :]), Z[w % 2][:, 0:SEQ],
                                         mod[:, bass.ds(gcol + j, 1)], flat(x),
                                         ALU.mult, ALU.add).then_inc(z_free[w % 2], 1)

            def pool_branch(g):
                win = 2 ** (g + 1)
                u = U[:, 2 * g:2 * g + 2, PAD - 16:PAD + SEQ]
                src, s, bufs = u, 1, (poolA, poolB)
                for lev in range(g + 1):
                    dst = bufs[lev % 2]
                    seq(dve.tensor_tensor(dst[:, :, s:SEQ + 16] if lev == 0 else dst[:, :, 2 * s - 1:SEQ + 16],
                                          src[:, :, s:SEQ + 16] if lev == 0 else src[:, :, 2 * s - 1:SEQ + 16],
                                          src[:, :, 0:SEQ + 16 - s] if lev == 0 else
                                          src[:, :, s - 1:SEQ + 16 - s], ALU.add))
                    settle()
                    src, s = dst, 2 * s
                d = Y[:, 2 * g:2 * g + 2, :]
                seq(dve.scalar_tensor_tensor(d, src[:, :, 16:], 1.0 / win, u[:, :, 16:], ALU.mult, ALU.subtract))
                settle()
                for c in range(2):
                    seq(dve.tensor_tensor(src[:, c, 16:16 + win], src[:, c, 16:16 + win], rc[:, 0:win], ALU.mult))
                settle()
                for c in range(2):
                    ins = dve.tensor_tensor(d[:, c, 0:win], src[:, c, 16:16 + win], u[:, c, 16:16 + win],
                                            ALU.subtract)
                    if c:
                        ins.then_inc(d_ready, 1)
                    else:
                        seq(ins)

            def attend(layer, i):
                if 0 <= i + 1 < HC:
                    a = HC * layer + i + 1
                    dve.wait_ge(kb_done, a + 1)
                    dve.scalar_tensor_tensor(X[:, HC + i + 1, :], X[:, HC + i + 1, :],
                                             par[:, C_QK + 2 * layer + 1:C_QK + 2 * layer + 2], M[:, 0:SEQ],
                                             ALU.mult, ALU.mult).then_inc(kmul, 1)
                if 0 <= i < HC:
                    a = HC * layer + i
                    dve.wait_ge(scored, a + 1)
                    dve.wait_ge(ds_ready, a + 1)
                    if a >= 2:
                        dve.wait_ge(pt_done, a - 1)
                    for q, (c0, c1) in enumerate(((0, P), (P, KEYS))):
                        ins = dve.scalar_tensor_tensor(SP[:, a % 2, c0:c1], S[a % 2][:, c0:c1],
                                                       rr[:, KC * q + i:KC * q + i + 1], DS[:, a % 2, c0:c1],
                                                       ALU.mult, ALU.add)
                        if q:
                            ins.then_inc(s_added, 1)
                        else:
                            seq(ins)
                if 0 <= i < HC:
                    settle()
                    dve.wait_ge(s_added, a0(layer, i) + 1)
                    for q, (c0, c1) in enumerate(((0, P), (P, KEYS))):
                        ins = dve.tensor_reduce(nm[:, i % 2, q:q + 1], SP[:, i % 2, c0:c1], AX_X, ALU.max,
                                                negate=True)
                        if q:
                            ins.then_inc(max_done, 1)
                        else:
                            seq(ins)

            def a0(layer, i):
                return HC * layer + i

            def divide(layer, i):
                if 0 <= i < HC:
                    a = HC * layer + i
                    dve.wait_ge(exp_done, 2 * (a + 1))
                    seq(dve.reciprocal(rl[:, i % 2, :], ls[:, i % 2, :]))
                    settle()
                    for q in range(QT):
                        ins = dve.tensor_scalar(PD[:, i % 2, q, :], ident[:], rl[:, i % 2, q:q + 1], None, ALU.mult)
                    ins.then_inc(pdiag, 1)

            plan = conv_plan()
            taps = [0]

            def conv(w):
                for j, k in plan.get(w, ()):
                    wcol = C_CW + j * CONV_WIDTH + k
                    if k == 0:
                        dve.wait_ge(u_done, max(4, j + 1))
                        ins = dve.tensor_scalar(Y[:, j, :], U[:, j, 0:SEQ], par[:, wcol:wcol + 1],
                                                par[:, C_CB + j:C_CB + j + 1], ALU.mult, ALU.add)
                    else:
                        dve.wait_ge(conv_seq, taps[0] - 1)
                        ins = dve.scalar_tensor_tensor(Y[:, j, :], U[:, j, k:k + SEQ], par[:, wcol:wcol + 1],
                                                       Y[:, j, :], ALU.mult, ALU.add)
                    ins.then_inc(conv_seq, 1)
                    taps[0] += 1

            dve.wait_ge(cexp, 1)
            seq(dve.tensor_scalar(ctmp[:], ctmp[:], 1.0, None, ALU.add))
            settle()
            seq(dve.reciprocal(ctmp[:], ctmp[:]))
            settle()
            seq(dve.tensor_tensor(cact[:], ctmp[:], par[:, C_C:C_C + KC], ALU.mult))
            dve.wait_ge(const, 5)
            seq(dve.reciprocal(rc[:], rc[:]))
            settle()
            def group_of_h(g):
                keep_piece(g)
                make_gain(0, g)
                make_h(0, range(GROUP * g, GROUP * (g + 1)))

            for p in range(4):
                dve.wait_ge(acc_zero, p + 1)
                add_units(UNITS * p, 4, None)
                if p:
                    group_of_h(p - 1)
                add_units(UNITS * p + 4, 4, None)
                lo(2 * p, None)
                add_units(UNITS * p + 8, 4, None)
                lo(2 * p + 1, None)
                add_units(UNITS * p + 12, 4, None)
                if p == 0:
                    dve.wait_ge(stat_done, KC)
                    rsqrt(0, QT, M[:, 0:QT], D_MODEL)
                    token_diag()
                    dve.wait_ge(spread, 1)
            group_of_h(3)
            lo(8, None)
            lo(9, None)

            def plain(w, t):
                lo(w + AHEAD, t, (0,))
                units(w, t)
                lo(w + AHEAD, t, (1,))

            plain(8, None)
            dve.wait_ge(z_free[0], WIDE // 2 + 1)
            pool_branch(0)
            plain(9, None)
            dve.wait_ge(z_free[1], WIDE // 2 + 1)
            pool_branch(1)
            run(dve, 10, 16, plain)
            plain(16, None)
            dve.wait_ge(s_read, 4)
            pool_branch(2)
            plain(17, None)
            pool_branch(3)
            keep_piece(4)
            run(dve, 18, V0, plain)
            def attention_step(w, v0, g0, layer, more=None):
                i = w - v0 - 3
                lo(w + AHEAD, None, (0,))
                divide(layer, i - 1)
                if w == v0:
                    dve.wait_ge(qk_stat, 2 * HC * (layer + 1))
                    rsqrt(2 * layer + 1, 2 * KC, M[:, 0:2 * KC], P)
                    dve.sem_inc(rr_ready, 1)
                attend(layer, i)
                units(w, None)
                lo(w + AHEAD, None, (1,))
                if w > g0:
                    split_gated(w - 1, None, g0, layer)
                if w >= g0:
                    gate(w, None, g0, layer)

            for w in range(V0, G0 + 5):
                if w == V0 + 2:
                    keep_piece(5)
                attention_step(w, V0, G0, 0)

            def step_g(g0, layer):
                def step(w, t):
                    plain(w, t)
                    split_gated(w - 1, t, g0, layer)
                    gate(w, t, g0, layer)
                return step

            for w in range(37, O0):
                if w == 42:
                    keep_piece(6)
                step_g(G0, 0)(w, None)

            def step_o(o0, layer):
                def step(w, t):
                    last = w + AHEAD >= N_SLABS
                    if not last:
                        lo(w + AHEAD, t, (0,))
                    units(w, t)
                    add_x(w, t, o0, layer)
                    if not last:
                        lo(w + AHEAD, t, (1,))
                return step

            split_gated(O0 - 1, None, G0, 0)
            dve.wait_ge(mod_done, GATE[0] + 1)
            dve.wait_ge(xr_in[0], 16)
            step_o(O0, 0)(48, None)
            step_o(O0, 0)(49, None)
            keep_piece(7)
            step_o(O0, 0)(50, None)
            step_o(O0, 0)(51, None)
            dve.wait_ge(xr_in[1], 16)
            run(dve, 52, 56, step_o(O0, 0))
            dve.wait_ge(mod_done, GATE[0] + 2)
            dve.wait_ge(xr_in[2], 16)
            step_o(O0, 0)(56, None)
            step_o(O0, 0)(57, None)
            keep_piece(8)
            step_o(O0, 0)(58, None)
            step_o(O0, 0)(59, None)
            dve.wait_ge(xr_in[3], 16)
            run(dve, 60, 62, step_o(O0, 0))
            step_o(O0, 0)(62, None)
            lo(65, None, (0,))
            for g in range(3):
                make_gain(1, g)
            add_x(63, None, O0, 0)
            dve.wait_ge(stat_done, 2 * KC)
            rsqrt(2, QT, M[:, 0:QT], D_MODEL)
            token_diag()
            dve.wait_ge(spread, 2)
            make_h(1, range(0, 4))
            lo(65, None, (1,))
            units(63, None)
            units(64, None)
            make_h(1, range(4, 8))
            lo(66, None)
            units(65, None)
            lo(67, None)
            units(66, None)
            make_h(1, range(8, 12))
            lo(68, None)
            keep_piece(9)
            make_gain(1, 3)
            units(67, None)
            lo(69, None)
            make_h(1, range(12, 14))
            lo(70, None)
            units(68, None)
            make_h(1, range(14, 16))
            units(69, None)

            def conv_silu(w):
                for j in range(2 * (w - 116), 2 * (w - 115)):
                    dve.wait_ge(ln_act, j + 1)
                    dve.scalar_tensor_tensor(Y[:, j, :], U[:, j, 0:SEQ], 1.0, Y[:, j, :],
                                             ALU.add, ALU.mult).then_inc(ln_out, 1)

            for w in (71, 72):
                lo(w, None)
                units(w - 1, None)
            for pair in range(4):
                half_a, tanh_b = (T, SG)[pair % 2][:, 0, :], (T, SG)[pair % 2][:, 1, :]
                if pair < 2:
                    dve.wait_ge(z_free[pair], (AB1 + WIDE) // 2 + 1)
                else:
                    dve.wait_ge(s_read, 4 + 2 * (pair - 1))
                dve.scalar_tensor_tensor(U[:, pair, PAD:PAD + SEQ], tanh_b, 1.0, half_a,
                                         ALU.add, ALU.mult).then_inc(u_done, 1)
            lo(73, None)

            def second_layer_step(w):
                if w < V1:
                    plain(w, None)
                else:
                    attention_step(w, V1, G1, 1)

            for w in range(AB1 + WIDE, 117):
                if w == 111:
                    dve.wait_ge(mean_mm, 1)
                    for j in range(HC):
                        seq(dve.scalar_tensor_tensor(Y[:, j, :], XB[:, 0:SEQ], -1.0 / HALF, Y[:, j, :],
                                                     ALU.mult, ALU.add))
                    settle()
                    dve.sem_inc(ln_sub, 1)
                if w == 114:
                    dve.wait_ge(var_mm, 1)
                    rsqrt(4, QT, XB[:, 0:QT], HALF)
                    token_diag()
                if w == 115:
                    dve.wait_ge(spread, 3)
                    for j in range(HC):
                        dve.tensor_tensor(Y[:, j, :], Y[:, j, :], XB[:, 0:SEQ], ALU.mult).then_inc(ln_mul, 1)
                second_layer_step(w)
                if w == 116:
                    conv_silu(w)
                if w < QI1 and w % 2:
                    j = (w - AB1) // 2
                    dve.wait_ge(z_free[1], w // 2 + 2)
                    dve.wait_ge(z_free[0], w // 2 + 2)
                    dve.scalar_tensor_tensor(U[:, j, PAD:PAD + SEQ], T[:, 1, :], 1.0, T[:, 0, :],
                                             ALU.add, ALU.mult).then_inc(u_done, 1)
                conv(w)
                if w == 85:
                    dve.wait_ge(wt_done, 1)
                    seq(dve.tensor_scalar(wi[:], XB[:, 0:SEQ].rearrange("p (a b) -> p a b", a=QT)
                                          [:, :, IDX_DIM:IDX_DIM + IDX_HEADS],
                                          float(IDX_HEADS) ** -0.5, None, ALU.mult))
                    settle()
                if 86 <= w < 94:
                    hh = w - 86
                    dve.wait_ge(relu, hh + 1)
                    if hh == 0:
                        dve.wait_ge(cm_ready, 2)
                    else:
                        dve.wait_ge(score, 2 * hh)
                    for q, (c0, c1) in enumerate(((0, P), (P, KEYS))):
                        dve.scalar_tensor_tensor(PTs[:, 0, c0:c1], SP[:, hh % 2, c0:c1], wi[:, q, hh:hh + 1],
                                                 PTs[:, 0, c0:c1], ALU.mult, ALU.add).then_inc(score, 1)
                if 94 <= w < 98:
                    if w == 94:
                        dve.wait_ge(score, 2 * IDX_HEADS)
                    for r in range(2):
                        for q, (c0, c1) in enumerate(((0, P), (P, KEYS))):
                            seq(dve.max(m8[:, q, :], PTs[:, r, c0:c1]))
                        settle()
                        for q, (c0, c1) in enumerate(((0, P), (P, KEYS))):
                            seq(dve.match_replace(PTs[:, 1 - r, c0:c1], m8[:, q, :], PTs[:, r, c0:c1], -3e38))
                        settle()
                if w == 98:
                    seq(dve.tensor_scalar(MK[:], PTs[:, 0, :], -2e38, -BIG, ALU.is_ge, ALU.mult))
                    settle()
                    dve.tensor_tensor(MK[:], MK[:], D[:], ALU.add).then_inc(mask_ready, 1)

            for w in range(117, O1):
                if w == 124:
                    keep_piece(10)
                plain(w, None)
                if w < 120:
                    conv_silu(w)
                split_gated(w - 1, None, G1, 1)
                gate(w, None, G1, 1)
            split_gated(O1 - 1, None, G1, 1)
            for half in range(2):
                w0 = O1 + HC * half
                dve.wait_ge(xr_in[2 * half], 32)
                if half:
                    lo(w0 + AHEAD, None)
                    keep_piece(11)
                dve.wait_ge(mod_done, GATE[1] + half + 1)
                if half:
                    add_x(w0, None, O1, 1)
                else:
                    step_o(O1, 1)(w0, None)
                for w in range(w0 + 1, w0 + 4):
                    step_o(O1, 1)(w, None)
                dve.wait_ge(xr_in[2 * half + 1], 32)
                for w in range(w0 + 4, w0 + HC):
                    step_o(O1, 1)(w, None)


def kernel(**inputs):
    import numpy as np
    import concourse.bacc as bacc
    from concourse.bass_utils import run_bass_kernel_spmd

    def slabs(w):
        k, n = w.shape
        return w.reshape(k // P, P, n // P, P).transpose(2, 1, 0, 3)

    def cols(v):
        return v.reshape(-1, P).T

    od = inputs["od_w_in"][0]
    q, k, v = od[:, 0:HALF], od[:, HALF:2 * HALF], od[:, 2 * HALF:3 * HALF]
    at = 3 * HALF
    qi = od[:, at:at + IDX_HEADS * IDX_DIM]
    at += IDX_HEADS * IDX_DIM
    wi, ki = od[:, at:at + IDX_HEADS], od[:, at + IDX_HEADS:at + IDX_HEADS + IDX_DIM]
    at += IDX_HEADS + IDX_DIM
    ga, gb, g = od[:, at:at + HALF], od[:, at + HALF:at + 2 * HALF], od[:, at + 2 * HALF:]
    ab = np.stack([slabs(ga), slabs(gb)], axis=1).reshape(2 * HC, P, KC, P)
    kw = np.concatenate([ki] + [wi] * (IDX_DIM // IDX_HEADS), axis=1)
    w_slabs = np.concatenate([slabs(inputs["ev_w_in"][0]), slabs(inputs["w_out"][0]), ab, slabs(qi), slabs(kw),
                              slabs(q), slabs(k), slabs(v), slabs(g), slabs(inputs["w_out"][1])])
    def by_token(v):
        return v.reshape(HC // 2, 2, P, KC, P).transpose(0, 2, 3, 1, 4).reshape(HC // 2, P, 2, KC, P)\
            .transpose(0, 2, 1, 3, 4).reshape(HC, P, KC, P)

    def wide(first):
        return first.transpose(2, 1, 0, 3).reshape(WIDE, 2, P, WIDE, P).transpose(0, 2, 1, 3, 4)\
            .reshape(WIDE, P, KC, P)

    w_slabs = np.concatenate([wide(w_slabs[:WIDE]), w_slabs[WIDE:V0], by_token(w_slabs[V0:G0]), w_slabs[G0:AB1],
                              wide(w_slabs[AB1:AB1 + WIDE]), w_slabs[AB1 + WIDE:V1], by_token(w_slabs[V1:G1]),
                              w_slabs[G1:]])

    def piece(a, kind, layer, n):
        if kind == "gate":
            return a[layer][..., 2 * D_MODEL + PIECE * n:2 * D_MODEL + PIECE * (n + 1)]
        at, width = GROUP * P * n, GROUP * P
        return np.concatenate([a[layer][..., D_MODEL + at:D_MODEL + at + width],
                               a[layer][..., at:at + width]], axis=-1)

    ada_units = np.concatenate([piece(inputs["ada_w"], *which).reshape(UNITS, P, PIECE) for which in PIECES])
    params = np.concatenate(
        [cols(inputs["c"]), cols(inputs["norm_g"])] + [cols(piece(inputs["ada_b"], *which)) for which in PIECES]
        + [cols(inputs["pool_scale"]), cols(inputs["moba_qn"]), cols(inputs["moba_kn"]),
           cols(inputs["dsa_qn"]), cols(inputs["dsa_kn"]),
           inputs["conv_w"][0].reshape(CONV_WIDTH, HC, P).transpose(2, 1, 0).reshape(P, HC * CONV_WIDTH),
           cols(inputs["conv_b"]), cols(inputs["conv_ln_g"]), cols(inputs["conv_ln_b"])], axis=1)
    arrays = {
        "xT": inputs["x"][0].T.reshape(KC, P, SEQ).transpose(1, 0, 2),
        "params": params,
        "pool_w": inputs["pool_w"][0].reshape(4, 2, P, 2 * P).transpose(2, 0, 1, 3),
        "w_slabs": w_slabs,
        "ada_units": ada_units,
    }
    arrays = {name: np.ascontiguousarray(a) for name, a in arrays.items()}

    nc = bacc.Bacc("TRN2", target_bir_lowering=False, num_devices=1)
    args = [nc.dram_tensor(name, a.shape, F32, kind="ExternalInput").ap() for name, a in arrays.items()]
    args.append(nc.dram_tensor("x1_dram", (P, KC, SEQ), F32, kind="Internal").ap())
    args.append(nc.dram_tensor("outT", (P, KC, SEQ), F32, kind="ExternalOutput").ap())
    build(nc, *args)
    r = run_bass_kernel_spmd(nc, [arrays], core_ids=[0])
    outT = r.results[0]["outT"]
    return np.ascontiguousarray(outT.transpose(1, 0, 2).reshape(D_MODEL, SEQ).T)[None]
```

```python
from contextlib import ExitStack

import concourse.bass as bass
from concourse import mybir

F32 = mybir.dt.float32
F32R = mybir.dt.float32r
ALU = mybir.AluOpType
ACT = mybir.ActivationFunctionType
AX_X = mybir.AxisListType.X

P = 128
D_MODEL = 2048
SEQ = 256
HALF = D_MODEL // 2
KC = D_MODEL // P
HC = HALF // P
QT = SEQ // P
EPS = 1e-6
BIG = 2.56e32
NEG_INF = -1e30
DSA_SEL = SEQ // 4
IDX_HEADS = 8
IDX_DIM = 64
CONV_WIDTH = 31
PAD = CONV_WIDTH - 1
KEYS = P + SEQ

U0, Q0, V0, G0, O0 = 0, 8, 24, 32, 48
AB1, QI1, KW1, Q1, V1, G1, O1 = 64, 80, 84, 85, 101, 109, 125
N_SLABS = 141
AHEAD = 2

PIECE = 1024
UNITS = D_MODEL // P
GROUP = 4
PIECES = [("h", 0, 0), ("h", 0, 1), ("h", 0, 2), ("h", 0, 3), ("h", 1, 0), ("h", 1, 1), ("gate", 0, 0),
          ("gate", 0, 1), ("h", 1, 2), ("h", 1, 3), ("gate", 1, 0), ("gate", 1, 1)]
UNIT_RATES = ((10, 34, 2), (34, 45, 1), (45, 47, 2), (47, 48, 1), (48, 62, 2),
              (62, 70, 1), (70, 72, 2), (110, 111, 2), (112, 113, 2), (115, 117, 1), (121, 125, 1), (125, 132, 2))
H_PIECE = {0: (0, 1, 2, 3), 1: (4, 5, 8, 9)}
GATE = {0: 6, 1: 10}
WIDE = (12, 8)

C_C = 0
C_NORM = C_C + KC
C_ADAB = C_NORM + 2 * KC
C_PSC = C_ADAB + len(PIECES) * HC
C_QK = C_PSC + HC
C_CW = C_QK + 4
C_CB = C_CW + HC * CONV_WIDTH
C_LG = C_CB + HC
C_LB = C_LG + HC
N_PAR = C_LB + HC


def shift_col(layer, j):
    return HC * H_PIECE[layer][j // GROUP] + 4 * (j % GROUP // 2) + 2 + j % 2


def units_at(w):
    first = 4 * UNITS
    for w0, w1, rate in UNIT_RATES:
        if w0 <= w < w1:
            return first + rate * (w - w0), rate
        first += rate * (w1 - w0)
    return None, 0


def conv_plan():
    ops = [(2 * m + s, k) for m in range(HC // 2) for k in range(CONV_WIDTH) for s in range(2)]
    plan, n = {}, 0
    for w0, w1, taps in ((72, 86, 7), (86, 94, 8), (94, 98, 3), (98, 101, 8), (101, 102, 4), (102, 104, 7),
                         (104, 106, 4), (106, 110, 6)):
        for w in range(w0, w1):
            plan[w] = ops[n:n + taps]
            assert all(w > max(AB1 + 2 * j + 1, AB1 + WIDE[1] - 1) for j, _ in plan[w])
            n += taps
    assert n >= len(ops)
    return plan


def build(nc, xT, params, pool_w, w_slabs, ada_units, x1_dram, outT):
    ctx = ExitStack()
    with ctx:
        def sb(name, shape, dt=F32):
            return ctx.enter_context(nc.sbuf_tensor(name, shape, dt))

        def sem(name):
            return ctx.enter_context(nc.semaphore(name))

        raw = sb("raw", [P, 4, 8, P])
        whi = sb("whi", [P, 4, 8, P], F32R)
        wlo = sb("wlo", [P, 4, 8, P], F32R)
        ada = sb("ada", [P, 4, PIECE])
        acc = sb("acc", [P, 2, PIECE])
        hhi = sb("hhi", [P, KC, SEQ], F32R)
        hlo = sb("hlo", [P, KC, SEQ], F32R)
        ghi = sb("ghi", [P, KC, SEQ], F32R)
        glo = sb("glo", [P, KC, SEQ], F32R)
        X = sb("X", [P, KC, SEQ])
        V = sb("V", [P, QT, HALF])
        Y = sb("Y", [P, HC, SEQ])
        U = sb("U", [P, HC, PAD + SEQ])
        T = sb("T", [P, 2, SEQ])
        SG = sb("SG", [P, 2, SEQ])
        SP = sb("SP", [P, 2, KEYS])
        PTs = sb("PTs", [P, 2, KEYS])
        PD = sb("PD", [P, 2, QT, P])
        KD = sb("KD", [P, QT, P])
        D = sb("D", [P, KEYS])
        MK = sb("MK", [P, KEYS])
        DS = sb("DS", [P, 2, KEYS])
        ident = sb("ident", [P, P])
        ones = sb("ones", [P, P])
        QI = sb("QI", [P, IDX_HEADS // 2, SEQ])
        KW = sb("KW", [P, SEQ])
        KI = sb("KI", [P, SEQ])
        par = sb("par", [P, N_PAR])
        cact = sb("cact", [P, KC])
        tab = sb("tab", [P, 1])
        ctmp = sb("ctmp", [P, KC])
        mod = sb("mod", [P, len(PIECES) * HC])
        hgain = sb("hgain", [P, KC])
        st = sb("st", [P, 5, 2 * KC])
        rr = sb("rr", [P, 2 * KC])
        nm = sb("nm", [P, 2, QT])
        ls = sb("ls", [P, 2, QT])
        rl = sb("rl", [P, 2, QT])
        m8 = sb("m8", [P, QT, 8])
        wi = sb("wi", [P, QT, IDX_HEADS])
        lnh = sb("lnh", [P, 2 * HC])
        qgain = sb("qgain", [P, 2])
        rc = sb("rc", [P, 16])
        psum = [ctx.enter_context(nc.psum_tensor(f"bank{i}", [P, 512], F32)) for i in range(8)]
        Z, S, PT, O, M, XB = psum[0:2], psum[2:4], psum[4], psum[5], psum[6], psum[7]
        VX = V[:].rearrange("p a (b t) -> p (a b) t", t=SEQ)
        PW = V[:].rearrange("p a (b c) -> p (a b) c", c=512).rearrange("p g (k n) -> p g k n", k=2)
        poolA, poolB = (t[:].rearrange("p a b -> p (a b)")[:, 0:2 * (SEQ + 16)].rearrange("p (c t) -> p c t", c=2)
                        for t in (SP, PTs))

        par_in, x_in, pw_in = sem("par_in"), sem("x_in"), sem("pw_in")
        raw_in = [sem(f"raw_in{i}") for i in range(4)]
        ada_in = [sem(f"ada_in{i}") for i in range(4)]
        hi_done = sem("hi_done")
        lo_done = sem("lo_done")
        pe_half = sem("pe_half")
        z_free = [sem(f"z_free{i}") for i in range(2)]
        ada_done = sem("ada_done")
        acc_zero = sem("acc_zero")
        mod_sum = sem("mod_sum")
        half_sum = sem("half_sum")
        mod_done = sem("mod_done")
        cexp = sem("cexp")
        const = sem("const")
        pool_self = sem("pool_self")
        dve_seq = sem("dve_seq")
        act_seq = sem("act_seq")
        sq_done = sem("sq_done")
        stat_done = sem("stat_done")
        var_ready = sem("var_ready")
        root_done = sem("root_done")
        diag_ready = sem("diag_ready")
        spread = sem("spread")
        rr_ready = sem("rr_ready")
        r_copied = sem("r_copied")
        q_read = sem("q_read")
        s_read = sem("s_read")
        xr_done = sem("xr_done")
        hhi_done = sem("hhi_done")
        hlo_done = sem("hlo_done")
        qk_stat = sem("qk_stat")
        tanh_done = sem("tanh_done")
        gated = sem("gated")
        ghi_done, glo_done = sem("ghi_done"), sem("glo_done")
        gain_ready = sem("gain_ready")
        xr_in = [sem(f"xr_in{i}") for i in range(4)]
        store = [sem(f"store{i}") for i in range(4)]
        d_ready, pool_mm, pool_out = sem("d_ready"), sem("pool_mm"), sem("pool_out")
        kdiag, kb_done, kmul = sem("kdiag"), sem("kb_done"), sem("kmul")
        ds_ready, scored, s_added, max_done = sem("ds_ready"), sem("scored"), sem("s_added"), sem("max_done")
        exp_done, pdiag, pt_done, pt_copied = sem("exp_done"), sem("pdiag"), sem("pt_done"), sem("pt_copied")
        pv_done, o_copied = sem("pv_done"), sem("o_copied")
        u_done = sem("u_done")
        wt_done, wi_ready = sem("wt_done"), sem("wi_ready")
        ki_in, cm_ready = sem("ki_in"), sem("cm_ready")
        logit, relu, score, mask_ready = sem("logit"), sem("relu"), sem("score"), sem("mask_ready")
        conv_seq = sem("conv_seq")
        mean_mm, ln_sub, ln_sq, var_mm = sem("mean_mm"), sem("ln_sub"), sem("ln_sq"), sem("var_mm")
        ln_mul, ln_act, ln_out = sem("ln_mul"), sem("ln_act"), sem("ln_out")

        N_TAPS = HC * CONV_WIDTH
        block = ctx.enter_context(nc.Block())

        def run(eng, w0, w1, step):
            with eng.Fori(0, (w1 - w0) // 2) as t:
                step(w0, t)
                step(w0 + 1, t)
            if (w1 - w0) % 2:
                step(w1 - 1, None)

        def now(w, t):
            return w if t is None else w + 2 * t

        def half_slot(w, half):
            return (2 * w + half) % 4

        def half_uses(w, half, t):
            n = (2 * w + half) // 4 + 1
            return n if t is None else n + t

        def x_written(eng, layer, count):
            last = (O0, O1)[layer] + count - 1
            for w in (last - 1, last):
                eng.wait_ge(z_free[w % 2], w // 2 + 2)

        def wide(s):
            return (Z[0], Z[1], S[0], S[1], PT, XB)[s // 2][:, s % 2 * SEQ:(s % 2 + 1) * SEQ]

        def flat(ap):
            return ap.rearrange("p a t -> p (a t)")

        def bank_uses(w, t):
            return w // 2 if t is None else w // 2 + t

        @block.sync
        def _(sp):
            sp.sem_inc(lo_done, 4)
            sp.sem_inc(ada_done, 4)
            sp.dma_start(par[:], params).then_inc(par_in, 16)
            sp.dma_start(X[:], xT).then_inc(x_in, 16)

            def load_units(n, count, t):
                for u in range(count):
                    slot = (n + u) % 4
                    unit = n + u if t is None else n + u + 4 * t
                    sp.wait_ge(ada_done, unit + 1)
                    sp.dma_start(ada[:, slot, :], ada_units[bass.ds(unit, 1)].rearrange("a p n -> p (a n)"))\
                      .then_inc(ada_in[slot], 16)

            def load_slab(w, t):
                for half in range(2):
                    slot = half_slot(w, half)
                    sp.wait_ge(lo_done, 2 * now(w, t) + half + 1)
                    sp.dma_start(raw[:, slot], w_slabs[bass.ds(now(w, t), 1), :, 8 * half:8 * half + 8, :]
                                 .rearrange("a p k n -> p (a k) n")).then_inc(raw_in[slot], 16)

            for p in range(4):
                for part in range(4):
                    load_units(UNITS * p + 4 * part, 4, None)
                    if part < 3 and 3 * p - 1 + part >= 0:
                        load_slab(3 * p - 1 + part, None)
            load_slab(WIDE[0] - 1, None)

            def step(w, t):
                load_slab(w + AHEAD, t)
                load_units(*units_at(w), t)

            for w0, w1 in ((10, 34), (34, 48), (48, 62), (62, 72), (72, 110), (110, 125), (125, 131),
                           (131, 132), (132, N_SLABS - AHEAD)):
                if w0 in (34, 62, 110, 131):
                    for w in range(w0, w1):
                        step(w, None)
                else:
                    run(sp, w0, w1, step)

        @block.gpsimd
        def _(pool):
            n = [0]

            def own(ins):
                n[0] += 1
                ins.then_inc(pool_self, 1)
                pool.wait_ge(pool_self, n[0])

            pool.memset(acc[:, 0, :], 0.0).then_inc(acc_zero, 1)
            pool.memset(acc[:, 1, :], 0.0).then_inc(acc_zero, 1)
            pool.memset(tab[:], 1.0).then_inc(const, 1)
            pool.memset(ones[:], 1.0).then_inc(const, 1)
            own(pool.memset(ident[:], 0.0))
            pool.affine_select(out=ident[:], in_=ident[:], compare_op=ALU.not_equal, fill=1.0, base=0,
                               pattern=[[-1, P]], channel_multiplier=1).then_inc(const, 1)
            pool.memset(U[:, :, 0:PAD], 0.0).then_inc(const, 1)
            pool.iota(rc[:], pattern=[[1, 16]], base=1, channel_multiplier=0,
                      allow_small_or_imprecise_dtypes=True).then_inc(const, 1)
            for c0, c1, q0 in ((0, P, 0), (P, KEYS, P)):
                own(pool.iota(D[:, c0:c1], pattern=[[1, c1 - c0]], base=-q0, channel_multiplier=-1,
                              allow_small_or_imprecise_dtypes=True))
                own(pool.affine_select(out=D[:, c0:c1], in_=D[:, c0:c1], compare_op=ALU.is_ge, fill=-BIG,
                                       base=q0, pattern=[[-1, c1 - c0]], channel_multiplier=1))

            def clear(piece):
                pool.wait_ge(mod_sum, piece - 1)
                pool.memset(acc[:, piece % 2, :], 0.0).then_inc(acc_zero, 1)

            def slopes(layer, heads=range(HC)):
                mask = D if layer == 0 else MK
                for h in heads:
                    a = HC * layer + h
                    if a >= 2:
                        pool.wait_ge(s_added, a - 1)
                    pool.tensor_scalar(DS[:, a % 2, :], mask[:], 2.0 ** -(h + 1), None, ALU.mult)\
                        .then_inc(ds_ready, 1)

            def load_x(layer, m):
                src = xT if layer == 0 else x1_dram
                if m >= 2:
                    pool.wait_ge(pv_done, HC * (layer + 1))
                    out = VX[:, 4 * (m - 2):4 * (m - 1), :]
                elif layer == 0:
                    pool.wait_ge(d_ready, 4)
                    out = U[:, 4 * m:4 * (m + 1), PAD:PAD + SEQ]
                else:
                    pool.wait_ge(ln_out, HC)
                    out = U[:, 4 * m:4 * (m + 1), PAD:PAD + SEQ]
                pool.dma_start(out, src[:, 4 * m:4 * m + 4, :]).then_inc(xr_in[m], 16)

            def store_x(layer, m):
                x_written(pool, layer, 4 * (m + 1))
                pool.dma_start((x1_dram if layer == 0 else outT)[:, 4 * m:4 * m + 4, :],
                               X[:, 4 * m:4 * m + 4, :]).then_inc(store[m], 16)

            clear(2)
            clear(3)
            clear(4)
            clear(5)
            pool.dma_start(PW, pool_w).then_inc(pw_in, 16)
            clear(6)
            load_x(0, 0)
            load_x(0, 1)
            slopes(0, range(0, 2))
            clear(7)
            slopes(0, range(2, HC))
            load_x(0, 2)
            load_x(0, 3)
            own(pool.memset(PTs[:, 0, :], 0.0))
            for c0, c1, q0 in ((0, P, 0), (P, KEYS, P)):
                pool.affine_select(out=PTs[:, 0, c0:c1], in_=PTs[:, 0, c0:c1], compare_op=ALU.is_ge,
                                   fill=NEG_INF, base=q0, pattern=[[-1, c1 - c0]],
                                   channel_multiplier=1).then_inc(cm_ready, 1)
            clear(8)
            clear(9)
            store_x(0, 0)
            store_x(0, 1)
            clear(10)
            store_x(0, 2)
            store_x(0, 3)
            clear(11)
            pool.wait_ge(z_free[KW1 % 2], KW1 // 2 + 2)
            pool.dma_start(KI[IDX_DIM:2 * IDX_DIM, :], KW[0:IDX_DIM, :]).then_inc(ki_in, 16)
            pool.wait_ge(mask_ready, 1)
            slopes(1)
            for m in range(4):
                pool.wait_ge(store[m], 16)
            load_x(1, 2)
            load_x(1, 3)
            load_x(1, 0)
            load_x(1, 1)
            for m in range(4):
                store_x(1, m)
            for m in range(4):
                pool.wait_ge(store[m], 32)

        @block.scalar
        def _(act):
            act.sem_inc(pe_half, 4)
            n = [0]

            def own(ins):
                n[0] += 1
                ins.then_inc(act_seq, 1)
                act.wait_ge(act_seq, n[0])

            def hi(w, t, halves=(0, 1)):
                for half in halves:
                    slot = half_slot(w, half)
                    act.wait_ge(raw_in[slot], 16 * half_uses(w, half, t))
                    act.wait_ge(pe_half, 2 * now(w, t) + half + 1)
                    act.activation(whi[:, slot], raw[:, slot], ACT.Copy).then_inc(hi_done, 1)

            def product(w, t):
                act.wait_ge(pe_half, 2 * now(w, t) + 2 + 4)

            def root(i, cols):
                act.wait_ge(var_ready, i + 1)
                act.activation(st[:, 1, 0:cols], st[:, 0, 0:cols], ACT.Sqrt).then_inc(root_done, 1)

            def square_x(i, j):
                if i >= 2:
                    act.wait_ge(stat_done, i - 1)
                act.activation(T[:, i % 2, :], X[:, j, :], ACT.Square).then_inc(sq_done, 1)

            def upper_h(layer, chunks):
                for j in chunks:
                    col = shift_col(layer, j)
                    act.wait_ge(xr_done, KC * layer + j + 1)
                    act.activation(hhi[:, j, :], X[:, j, :], ACT.Identity, bias=mod[:, col:col + 1])\
                        .then_inc(hhi_done, 1)

            def step_qk(w, t, q0, kind, layer):
                hi(w + AHEAD, t)
                evict_qk(w, t, q0, kind, layer)

            def evict_qk(w, t, q0, kind, layer):
                product(w, t)
                gain = qgain[:, layer:layer + 1] if kind == "q" else 1.0
                act.activation(X[:, bass.ds(now(w, t) - q0, 1), :].rearrange("p a t -> p (a t)"),
                               Z[w % 2][:, 0:SEQ], ACT.Copy, scale=gain)
                act.activation(T[:, w % 2, :], Z[w % 2][:, 0:SEQ], ACT.Square).then_inc(z_free[w % 2], 1)

            def evict_v(w, v0, layer):
                pair = (w - v0) // 2
                if (w - v0) % 2:
                    product(w, None)
                    act.activation(V[:, :, 2 * P * pair:2 * P * (pair + 1)],
                                   Z[(v0 + pair) % 2][:].rearrange("p (a b) -> p a b", a=QT), ACT.Copy)\
                       .then_inc(z_free[(v0 + pair) % 2], 2)

            def tanh_gate(w, t, g0, layer):
                product(w, t)
                i = KC * layer + now(w, t) - g0
                if t is not None or i >= 2:
                    act.wait_ge(gated, i - 1)
                act.activation(T[:, w % 2, :], Z[w % 2][:, 0:SEQ], ACT.Tanh, scale=0.5).then_inc(tanh_done, 1)

            def round_gated(w, t, g0, layer):
                c = now(w, t) - g0
                act.wait_ge(gated, KC * layer + c + 1)
                act.activation(ghi[:, bass.ds(c, 1), :].rearrange("p a t -> p (a t)"), SG[:, w % 2, :],
                               ACT.Copy).then_inc(ghi_done, 1)

            def step_g(w, t, g0, layer):
                hi(w + AHEAD, t)
                tanh_gate(w, t, g0, layer)
                round_gated(w - 1, t, g0, layer)

            def attend(layer, i):
                if 0 <= i + 2 < HC:
                    a = HC * layer + i + 2
                    if i + 2 == 0:
                        act.wait_ge(rr_ready, layer + 1)
                    if a:
                        act.wait_ge(kb_done, a)
                    for q in range(QT):
                        col = KC * q + HC + i + 2
                        e = act.activation(KD[:, q, :], ident[:], ACT.Copy, scale=rr[:, col:col + 1])
                    e.then_inc(kdiag, 1)
                if 0 <= i - 1 < HC:
                    a = HC * layer + i - 1
                    act.wait_ge(pt_done, a + 1)
                    if a >= 2:
                        act.wait_ge(pv_done, a - 1)
                    act.activation(PTs[:, a % 2, :], PT[:, 0:KEYS], ACT.Copy).then_inc(pt_copied, 1)
                if 0 <= i - 2 < HC:
                    a = HC * layer + i - 2
                    act.wait_ge(pv_done, a + 1)
                    act.activation(X[:, i - 2, :], O[:, 0:SEQ], ACT.Copy).then_inc(o_copied, 1)
                if 0 <= i < HC:
                    a = HC * layer + i
                    act.wait_ge(max_done, a + 1)
                    for q, (c0, c1) in enumerate(((0, P), (P, KEYS))):
                        e = act.activation(SP[:, a % 2, c0:c1], SP[:, a % 2, c0:c1], ACT.Exp,
                                           bias=nm[:, a % 2, q:q + 1], accum_out=ls[:, a % 2, q:q + 1])
                        e.then_inc(exp_done, 1)

            def pool_evict(g):
                act.wait_ge(pool_mm, g + 1)
                for o in range(2):
                    j = 2 * g + o
                    act.activation(Y[:, j, :], PT[:, o * SEQ:(o + 1) * SEQ], ACT.Copy,
                                   scale=par[:, C_PSC + j:C_PSC + j + 1]).then_inc(pool_out, 1)

            def warm(func):
                act.activation(tab[:], tab[:], func)

            act.wait_ge(par_in, 16)
            act.activation(ctmp[:], par[:, C_C:C_C + KC], ACT.Exp, scale=-1.0).then_inc(cexp, 1)
            for l in range(2):
                own(act.activation(qgain[:, l:l + 1], par[:, C_QK + 2 * l:C_QK + 2 * l + 1], ACT.Copy,
                                   scale=float(P) ** -0.5))
            act.activation(lnh[:], par[:, C_LG:C_LG + 2 * HC], ACT.Copy, scale=0.5).then_inc(act_seq, 1)
            n[0] += 1
            act.wait_ge(x_in, 16)
            for j in range(KC):
                square_x(j, j)
            hi(0, None)
            hi(1, None)
            root(0, QT)
            act.wait_ge(spread, 1)
            act.activation(DS[:, 0, 0:SEQ], XB[:, 0:SEQ], ACT.Copy).then_inc(r_copied, 1)
            for g in range(3):
                upper_h(0, range(GROUP * g, GROUP * (g + 1)))
                hi(3 * g + 2, None)
                hi(3 * g + 3, None)
                if g < 2:
                    hi(3 * g + 4, None)
            upper_h(0, range(12, 14))
            hi(10, None)
            upper_h(0, range(14, 16))
            hi(11, None)
            hi(12, None)
            act.wait_ge(pe_half, 2 * WIDE[0] + 4)
            for s in range(8):
                read = act.activation(U[:, s, PAD:PAD + SEQ], wide(s), ACT.Copy)
                if s < 4:
                    read.then_inc(z_free[s // 2], 3)
                else:
                    read.then_inc(s_read, 1)
                if s == 1:
                    hi(13, None)
            for i in range(4):
                act.activation(X[:, i, :], wide(8 + i), ACT.Copy, scale=qgain[:, 0:1])
                act.activation((T, SG)[i // 2][:, i % 2, :], wide(8 + i), ACT.Square).then_inc(q_read, 1)
            hi(14, None)
            act.wait_ge(qk_stat, 4)
            evict_qk(12, None, Q0, "q", 0)
            step_qk(13, None, Q0, "q", 0)
            step_qk(14, None, Q0, "q", 0)
            pool_evict(0)
            step_qk(15, None, Q0, "q", 0)
            step_qk(16, None, Q0, "k", 0)
            pool_evict(1)
            step_qk(17, None, Q0, "k", 0)
            pool_evict(2)
            run(act, 18, V0, lambda w, t: step_qk(w, t, Q0, "k", 0))
            for w in range(V0, G0 + 5):
                hi(w + AHEAD, None)
                if w < G0:
                    evict_v(w, V0, 0)
                else:
                    tanh_gate(w, None, G0, 0)
                if w == V0:
                    pool_evict(3)
                    root(1, 2 * KC)
                attend(0, w - V0 - 3)
                if w > G0:
                    round_gated(w - 1, None, G0, 0)
            step_g(37, None, G0, 0)
            run(act, 38, O0, lambda w, t: step_g(w, t, G0, 0))

            def square_new(j, t):
                w = O0 + j
                act.wait_ge(z_free[w % 2], bank_uses(w, t) + 2)
                act.wait_ge(stat_done, KC + now(j, t) - 1)
                act.activation(T[:, j % 2, :], flat(X[:, bass.ds(now(j, t), 1), :]), ACT.Square)\
                   .then_inc(sq_done, 1)

            def step_o0(w, t):
                hi(w + AHEAD, t, (0,))
                square_new(w - O0 - 1, t)
                hi(w + AHEAD, t, (1,))

            round_gated(O0 - 1, None, G0, 0)
            hi(O0 + AHEAD, None)
            step_o0(49, None)
            run(act, 50, AB1 - 2, step_o0)
            step_o0(AB1 - 2, None)
            hi(AB1 + 1, None, (0,))
            square_new(KC - 2, None)
            warm(ACT.Sqrt)
            square_new(KC - 1, None)
            root(2, QT)
            hi(AB1 + 1, None, (1,))
            upper_h(1, range(0, 8))
            for w in (66, 67):
                hi(w, None)
            upper_h(1, range(8, 12))
            for w in (68, 69):
                hi(w, None)
            upper_h(1, range(12, 14))
            hi(70, None)
            upper_h(1, range(14, 16))

            def step_ab(w, t):
                hi(w + AHEAD, t)
                product(w, t)
                pair = (w - AB1) // 2
                if w % 2 == 0:
                    if t is not None or pair > 0:
                        act.wait_ge(u_done, pair if t is None else pair + t)
                    act.activation(T[:, 0, :], Z[0][:, 0:SEQ], ACT.Copy, scale=0.5).then_inc(z_free[0], 1)
                else:
                    act.activation(T[:, 1, :], Z[1][:, 0:SEQ], ACT.Tanh, scale=0.5).then_inc(z_free[1], 1)

            warm(ACT.Tanh)
            for w in (71, 72):
                hi(w, None)
            act.wait_ge(pe_half, 2 * (AB1 + WIDE[1]) + 4)
            for pair in range(4):
                half_a, tanh_b = (T, SG)[pair % 2][:, 0, :], (T, SG)[pair % 2][:, 1, :]
                if pair >= 2:
                    act.wait_ge(u_done, pair - 1)
                for out, s, func in ((half_a, 2 * pair, ACT.Copy), (tanh_b, 2 * pair + 1, ACT.Tanh)):
                    read = act.activation(out, wide(s), func, scale=0.5)
                    if pair < 2:
                        read.then_inc(z_free[pair], 2)
                    else:
                        read.then_inc(s_read, 1)
            hi(73, None)
            step_ab(72, None)
            step_ab(73, None)
            run(act, 74, QI1, step_ab)

            def step_qi(w, t):
                hi(w + AHEAD, t)
                product(w, t)
                act.activation(QI[:, bass.ds(now(w, t) - QI1, 1), :].rearrange("p a t -> p (a t)"),
                               Z[w % 2][:, 0:SEQ], ACT.Copy).then_inc(z_free[w % 2], 1)

            run(act, QI1, KW1, step_qi)
            hi(KW1 + AHEAD, None)
            product(KW1, None)
            act.activation(KW[:], Z[KW1 % 2][:, 0:SEQ], ACT.Copy).then_inc(z_free[KW1 % 2], 1)
            step_qk(85, None, Q1, "q", 1)
            for w in range(86, 94):
                step_qk(w, None, Q1, "q" if w < 93 else "k", 1)
                hh = w - 86
                act.wait_ge(logit, hh + 1)
                if hh >= 2:
                    act.wait_ge(score, 2 * (hh - 1))
                act.activation(SP[:, hh % 2, :], S[hh % 2][:, 0:KEYS], ACT.Relu,
                               scale=float(IDX_DIM) ** -0.5).then_inc(relu, 1)
            run(act, 94, V1, lambda w, t: step_qk(w, t, Q1, "k", 1))
            def normed(chunks):
                for j in chunks:
                    act.wait_ge(ln_mul, j + 1)
                    act.activation(U[:, j, 0:SEQ], Y[:, j, :], ACT.Tanh, bias=lnh[:, HC + j:HC + j + 1],
                                   scale=lnh[:, j:j + 1])
                    act.activation(Y[:, j, :], Y[:, j, :], ACT.Identity,
                                   bias=par[:, C_LB + j:C_LB + j + 1],
                                   scale=par[:, C_LG + j:C_LG + j + 1]).then_inc(ln_act, 1)

            for w in range(V1, 117):
                if w == 114:
                    root(4, QT)
                hi(w + AHEAD, None)
                if w < G1:
                    evict_v(w, V1, 1)
                else:
                    tanh_gate(w, None, G1, 1)
                if w == V1:
                    root(3, 2 * KC)
                attend(1, w - V1 - 3)
                if w > G1:
                    round_gated(w - 1, None, G1, 1)
                if w == 111:
                    act.wait_ge(ln_sub, 1)
                    act.activation(U[:, :, 0:SEQ], Y[:], ACT.Square).then_inc(ln_sq, 1)
                if w in (115, 116):
                    normed(range(2 * (w - 115), 2 * (w - 114)))
            for w in (117, 118):
                step_g(w, None, G1, 1)
                normed(range(2 * (w - 115), 2 * (w - 114)))
            run(act, 119, O1, lambda w, t: step_g(w, t, G1, 1))
            round_gated(O1 - 1, None, G1, 1)
            hi(O1 + AHEAD, None)
            run(act, O1 + 1, N_SLABS - AHEAD, lambda w, t: hi(w + AHEAD, t))

        @block.tensor
        def _(pe):
            for b in range(2):
                pe.sem_inc(z_free[b], 1)
            mm = nc.tensor.matmul

            def keep_warm(count, bank=PT):
                for _ in range(count):
                    mm(bank[:, 0:P], ones[:], ident[:], start=True, stop=True)

            def slab(w, t, ahi, alo, gated_last=None, between=None):
                out = Z[w % 2][:, 0:SEQ]
                pe.wait_ge(z_free[w % 2], bank_uses(w, t) + 1)
                for half in range(2):
                    s = half_slot(w, half)
                    pe.wait_ge(lo_done, 2 * now(w, t) + half + 1 + 4)
                    for k in range(8):
                        c = 8 * half + k
                        if gated_last is not None and c >= KC - 2:
                            pe.wait_ge(glo_done, gated_last - KC + c + 1)
                        mm(out, whi[:, s, k, :], ahi[:, c, :], start=(c == 0), stop=False)
                        mm(out, whi[:, s, k, :], alo[:, c, :], start=False, stop=False)
                        last = mm(out, wlo[:, s, k, :], ahi[:, c, :], start=False, stop=(c == KC - 1))
                        if between is not None and c < KC - 1:
                            between(c)
                    last.then_inc(pe_half, 1)

            def wide_chunk(layer, w0, c):
                pe.wait_ge(hlo_done, KC * layer + c + 1)
                count = WIDE[layer]
                for s in range(count):
                    half, k = (count * c + s) // 8, (count * c + s) % 8
                    slot = half_slot(w0, half)
                    if s == 0 or k == 0:
                        pe.wait_ge(lo_done, 2 * w0 + half + 1 + 4)
                    mm(wide(s), whi[:, slot, k, :], hhi[:, c, :], start=(c == 0 and s % 2 == 0), stop=False,
                       skip_group_check=True)
                    mm(wide(s), whi[:, slot, k, :], hlo[:, c, :], start=False, stop=False, skip_group_check=True)
                    last = mm(wide(s), wlo[:, slot, k, :], hhi[:, c, :], start=False, stop=(c == KC - 1),
                              skip_group_check=True)
                    if k == 7:
                        last.then_inc(pe_half, 1)

            def slab_h(w, t):
                slab(w, t, hhi, hlo)

            def slab_g(w, t):
                slab(w, t, ghi, glo)

            def by_token(bank, chunk, first, last):
                for q in range(QT):
                    ins = mm(bank[:, q:q + 1], chunk[:, q * P:(q + 1) * P], ones[:, 0:1],
                             start=(first and q == 0), stop=last, skip_group_check=True)
                return ins

            def x_stat(i, runtime=None):
                pe.wait_ge(sq_done, (i if runtime is None else runtime) + 1)
                by_token(M, T[:, i % 2, :], i % KC == 0, i % KC == KC - 1).then_inc(stat_done, 1)

            def spread_token(i):
                pe.wait_ge(diag_ready, i + 1)
                for q in range(QT):
                    ins = mm(XB[:, q * P:(q + 1) * P], ones[:], KD[:, q, :], start=True, stop=True)
                ins.then_inc(spread, 1)

            def reduce_part(p, j, half=False):
                if j == 0 and not half:
                    pe.wait_ge(ada_done, UNITS * (p + 1) + 4)
                    if p >= 1:
                        pe.wait_ge(mod_done, p)
                    if p >= 6:
                        pe.wait_ge(o_copied, HC if p < 10 else 2 * HC)
                ins = mm(O[:, j:j + 1], acc[:, p % 2, j * P:(j + 1) * P], ones[:, 0:1], start=True, stop=True)
                if j == HC - 1:
                    ins.then_inc(mod_sum, 1)
                return ins

            def reduce_piece(p):
                for j in range(HC):
                    reduce_part(p, j)

            def with_piece(p):
                return lambda c: c < HC and reduce_part(p, c)

            def qk_stats(w, t, q0):
                pe.wait_ge(z_free[w % 2], bank_uses(w, t) + 2)
                for q in range(QT):
                    ins = mm(M[:, bass.ds(q * KC + now(w, t) - q0, 1)], T[:, w % 2, q * P:(q + 1) * P],
                             ones[:, 0:1], start=True, stop=True)
                ins.then_inc(qk_stat, 1)

            def pool_product(g):
                if g == 0:
                    pe.wait_ge(pw_in, 16)
                pe.wait_ge(d_ready, g + 1)
                if g:
                    pe.wait_ge(pool_out, 2 * g)
                for o in range(2):
                    for k in range(2):
                        ins = mm(PT[:, o * SEQ:(o + 1) * SEQ], PW[:, g, k, o * P:(o + 1) * P],
                                 Y[:, 2 * g + k, :], start=(k == 0), stop=(k == 1))
                ins.then_inc(pool_mm, 1)

            def slab_v(w, v0):
                pair, second = (w - v0) // 2, (w - v0) % 2
                b = (v0 + pair) % 2
                bank = Z[b]
                if not second:
                    pe.wait_ge(z_free[b], (v0 + 1 - b) // 2 + 1 + 2 * (pair // 2))
                for half in range(2):
                    s = half_slot(w, half)
                    pe.wait_ge(lo_done, 2 * w + half + 1 + 4)
                    for k in range(4):
                        c = 8 * second + 4 * half + k
                        upper, lower = flat(whi[:, s, 2 * k:2 * k + 2, :]), flat(wlo[:, s, 2 * k:2 * k + 2, :])
                        for q in range(QT):
                            out, tokens = bank[:, q * SEQ:(q + 1) * SEQ], slice(q * P, (q + 1) * P)
                            mm(out, hhi[:, c, tokens], upper, start=(c == 0 and q == 0), stop=False,
                               skip_group_check=True)
                            mm(out, hlo[:, c, tokens], upper, start=False, stop=False, skip_group_check=True)
                            last = mm(out, hhi[:, c, tokens], lower, start=False, stop=(c == KC - 1),
                                      skip_group_check=True)
                    last.then_inc(pe_half, 1)

            def attend(layer, v0, w):
                i = w - v0 - 3
                if 0 <= i + 1 < HC:
                    a = HC * layer + i + 1
                    pe.wait_ge(kdiag, a + 1)
                    if a:
                        pe.wait_ge(kmul, a)
                    for q in range(QT):
                        ins = mm(M[:, q * P:(q + 1) * P], ones[:], KD[:, q, :], start=True, stop=True)
                    ins.then_inc(kb_done, 1)
                if 0 <= i < HC:
                    a = HC * layer + i
                    pe.wait_ge(kmul, a + 1)
                    if i == 0:
                        pe.wait_ge(s_read, 4 * (layer + 1))
                    if a >= 2:
                        pe.wait_ge(s_added, a - 1)
                    mm(S[a % 2][:, 0:P], X[:, i, 0:P], X[:, HC + i, 0:P], start=True, stop=True)
                    mm(S[a % 2][:, P:KEYS], X[:, i, P:SEQ], X[:, HC + i, :], start=True, stop=True)\
                        .then_inc(scored, 1)
                if 0 <= i - 1 < HC:
                    a = HC * layer + i - 1
                    pe.wait_ge(pdiag, a + 1)
                    if a:
                        pe.wait_ge(pt_copied, a)
                    else:
                        pe.wait_ge(pool_out, HC)
                    for out, keys, q in ((0, 0, 0), (P, P, 1), (2 * P, 2 * P, 1)):
                        ins = mm(PT[:, out:out + P], SP[:, a % 2, keys:keys + P], PD[:, a % 2, q, :],
                                 start=True, stop=True)
                    ins.then_inc(pt_done, 1)
                if 0 <= i - 2 < HC:
                    a, h = HC * layer + i - 2, i - 2
                    pe.wait_ge(pt_copied, a + 1)
                    b = (v0 + h // 2) % 2
                    pe.wait_ge(z_free[b], (v0 + 1 - b) // 2 + 1 + 2 * (h // 4 + 1))
                    pe.wait_ge(mod_done, 6 if layer == 0 else 10)
                    if a:
                        pe.wait_ge(o_copied, a)
                    mm(O[:, 0:SEQ], V[:, 0, h * P:(h + 1) * P], PTs[:, a % 2, 0:SEQ], start=True, stop=False)
                    mm(O[:, P:SEQ], V[:, 1, h * P:(h + 1) * P], PTs[:, a % 2, SEQ:KEYS],
                       start=False, stop=True).then_inc(pv_done, 1)

            def logits(hh):
                c, p0 = hh // 2, IDX_DIM * (hh % 2)
                keys = KW if p0 == 0 else KI
                if hh == 0:
                    pe.wait_ge(z_free[KW1 % 2], KW1 // 2 + 2)
                    pe.wait_ge(s_read, 8)
                if hh == 1:
                    pe.wait_ge(ki_in, 16)
                if hh >= 2:
                    pe.wait_ge(relu, hh - 1)
                mm(S[hh % 2][:, 0:P], QI[p0:p0 + IDX_DIM, c, 0:P], keys[p0:p0 + IDX_DIM, 0:P],
                   start=True, stop=True)
                mm(S[hh % 2][:, P:KEYS], QI[p0:p0 + IDX_DIM, c, P:SEQ], keys[p0:p0 + IDX_DIM, :],
                   start=True, stop=True).then_inc(logit, 1)

            pe.wait_ge(const, 3)
            for i in range(KC):
                x_stat(i)
            spread_token(0)
            for p in range(3):
                if p:
                    pe.wait_ge(ada_done, UNITS * p + 12 + 4)
                    keep_warm(24, M)
                reduce_piece(p)
                for c in range(GROUP * p, GROUP * (p + 1)):
                    if c == 11:
                        pe.wait_ge(ada_done, UNITS * 3 + 8 + 4)
                        pe.wait_ge(mod_done, 3)
                        for j in range(4):
                            ins = reduce_part(3, j, half=True)
                        ins.then_inc(half_sum, 1)
                    wide_chunk(0, U0, c)
            wide_chunk(0, U0, 12)
            wide_chunk(0, U0, 13)
            pe.wait_ge(ada_done, UNITS * 4 + 4)
            for j in range(4, HC):
                reduce_part(3, j)
            wide_chunk(0, U0, 14)
            wide_chunk(0, U0, 15)

            def slab_stat(q0):
                def step(w, t):
                    slab_h(w, t)
                    qk_stats(w - 1, t, q0)
                return step

            slab_h(12, None)
            for i in range(4):
                pe.wait_ge(q_read, i + 1)
                for q in range(QT):
                    ins = mm(M[:, q * KC + i:q * KC + i + 1], (T, SG)[i // 2][:, i % 2, q * P:(q + 1) * P],
                             ones[:, 0:1], start=True, stop=True)
                ins.then_inc(qk_stat, 1)
            slab_h(13, None)
            qk_stats(12, None, Q0)
            slab_stat(Q0)(14, None)
            pool_product(0)
            slab_stat(Q0)(15, None)
            slab_stat(Q0)(16, None)
            pool_product(1)
            slab_stat(Q0)(17, None)
            pool_product(2)
            run(pe, 18, 20, slab_stat(Q0))
            slab(20, None, hhi, hlo, between=with_piece(4))
            qk_stats(19, None, Q0)
            run(pe, 21, V0, slab_stat(Q0))
            for w in range(V0, G0 + 5):
                if w == V0 + 4:
                    reduce_piece(5)
                if w < G0:
                    slab_v(w, V0)
                else:
                    slab_h(w, None)
                if w == V0:
                    qk_stats(w - 1, None, Q0)
                    pool_product(3)
                attend(0, V0, w)
            run(pe, 37, 42, slab_h)
            slab(42, None, hhi, hlo, between=with_piece(6))
            run(pe, 43, O0, slab_h)

            pe.wait_ge(glo_done, KC - 2)
            slab(48, None, ghi, glo, KC)
            slab_g(49, None)
            slab(50, None, ghi, glo, between=with_piece(7))
            x_stat(KC)
            slab_g(51, None)
            x_stat(KC + 1)

            def slab_x(w, t):
                slab_g(w, t)
                x_stat(KC + w - O0 - 2, runtime=KC + now(w, t) - O0 - 2)

            run(pe, 52, 56, slab_x)
            slab_x(56, None)
            slab_x(57, None)
            slab(58, None, ghi, glo, between=with_piece(8))
            x_stat(KC + 58 - O0 - 2)
            run(pe, 59, AB1, slab_x)
            x_stat(2 * KC - 2)
            keep_warm(7)
            x_stat(2 * KC - 1)
            keep_warm(9)
            spread_token(1)
            keep_warm(9)

            pe.wait_ge(s_added, HC)
            for c in range(KC):
                if c == 2 * GROUP:
                    reduce_piece(9)
                wide_chunk(1, AB1, c)
            run(pe, AB1 + WIDE[1], KW1, slab_h)
            slab_h(KW1, None)
            slab_h(85, None)
            pe.wait_ge(z_free[KW1 % 2], KW1 // 2 + 2)
            for q in range(QT):
                ins = nc.tensor.transpose(XB[:, q * P:(q + 1) * P], KW[:, q * P:(q + 1) * P], ident[:])
            ins.then_inc(wt_done, 1)
            for w in range(86, 94):
                slab_stat(Q1)(w, None)
                logits(w - 86)
            run(pe, 94, V1, slab_stat(Q1))
            for w in range(V1, 117):
                if w < G1:
                    slab_v(w, V1)
                elif w == 113:
                    pe.wait_ge(ln_sq, 1)
                    slab(w, None, hhi, hlo, between=lambda c: c < HC and
                         by_token(XB, U[:, c, 0:SEQ], c == 0, c == HC - 1))
                    pe.sem_inc(var_mm, 1)
                else:
                    slab_h(w, None)
                if w == V1:
                    qk_stats(w - 1, None, Q1)
                attend(1, V1, w)
                if w == 110:
                    pe.wait_ge(conv_seq, N_TAPS)
                    for j in range(HC):
                        ins = mm(XB[:, 0:SEQ], ones[:], Y[:, j, :], start=(j == 0), stop=(j == HC - 1))
                    ins.then_inc(mean_mm, 1)
                if w == 114:
                    spread_token(2)
            run(pe, 117, 124, slab_h)
            slab(124, None, hhi, hlo, between=with_piece(10))
            pe.wait_ge(glo_done, 2 * KC - 2)
            slab(125, None, ghi, glo, 2 * KC)
            run(pe, 126, 134, slab_g)
            slab(134, None, ghi, glo, between=with_piece(11))
            run(pe, 135, N_SLABS, slab_g)

        @block.vector
        def _(dve):
            n = [0]

            def seq(ins):
                n[0] += 1
                ins.then_inc(dve_seq, 1)

            def settle():
                dve.wait_ge(dve_seq, n[0])

            def lo(w, t, halves=(0, 1)):
                for half in halves:
                    s = half_slot(w, half)
                    dve.wait_ge(hi_done, 2 * now(w, t) + half + 1)
                    dve.tensor_tensor(wlo[:, s], raw[:, s], whi[:, s].bitcast(F32), ALU.subtract)\
                        .then_inc(lo_done, 1)

            def add_units(first, count, t):
                for u in range(count):
                    unit = first + u if t is None else first + u + 4 * t
                    slot, p = (first + u) % 4, first // UNITS
                    uses = (first + u) // 4 + 1
                    k = unit - UNITS * p
                    dve.wait_ge(ada_in[slot], 16 * (uses if t is None else uses + t))
                    dve.wait_ge(ada_done, unit + 4)
                    dve.scalar_tensor_tensor(acc[:, p % 2, :], ada[:, slot, :], cact[:, bass.ds(k, 1)],
                                             acc[:, p % 2, :], ALU.mult, ALU.add).then_inc(ada_done, 1)

            def units(w, t):
                first, count = units_at(w)
                if count:
                    if t is None and first % UNITS == 0:
                        dve.wait_ge(acc_zero, first // UNITS + 1)
                    add_units(first, count, t)

            def half_units(first, count):
                for unit in range(first, first + count):
                    slot, u, p = unit % 4, unit % UNITS, unit // UNITS
                    out = acc[:, p % 2, PIECE // 2 * (u // 8):PIECE // 2 * (u // 8 + 1)]
                    k = 2 * (u % 8)
                    dve.wait_ge(ada_in[slot], 16 * (unit // 4 + 1))
                    dve.wait_ge(ada_done, unit + 4)
                    seq(dve.scalar_tensor_tensor(out, ada[:, slot, 0:PIECE // 2], cact[:, k:k + 1], out,
                                                 ALU.mult, ALU.add))
                    settle()
                    dve.scalar_tensor_tensor(out, ada[:, slot, PIECE // 2:], cact[:, k + 1:k + 2], out,
                                             ALU.mult, ALU.add).then_inc(ada_done, 1)

            def keep_cols(p, c0, c1):
                return dve.tensor_tensor(mod[:, p * HC + c0:p * HC + c1], O[:, c0:c1],
                                         par[:, C_ADAB + p * HC + c0:C_ADAB + p * HC + c1], ALU.add)

            def keep_piece(p, first=0):
                dve.wait_ge(mod_sum, p + 1)
                keep_cols(p, first, HC).then_inc(mod_done, 1)

            def gain_cols(layer, g, h0, h1):
                p, j = H_PIECE[layer][g], GROUP * g + 2 * h0
                col = C_NORM + KC * layer + j
                scales = mod[:, p * HC + 4 * h0:p * HC + 4 * h1].rearrange("p (h c) -> p h c", c=4)[:, :, 0:2]
                out, gain = (a.rearrange("p (h c) -> p h c", c=2) for a in (
                    hgain[:, j:j + 2 * (h1 - h0)], par[:, col:col + 2 * (h1 - h0)]))
                return dve.scalar_tensor_tensor(out, scales, 1.0, gain, ALU.add, ALU.mult)

            def make_gain(layer, g, h0=0):
                dve.wait_ge(mod_done, H_PIECE[layer][g] + 1)
                gain_cols(layer, g, h0, 2).then_inc(gain_ready, 1)

            def rsqrt(i, cols, src, count):
                a, s, r, y = (st[:, k, 0:cols] for k in (0, 1, 2, 3))
                dve.tensor_scalar(a, src, 1.0 / count, EPS, ALU.mult, ALU.add).then_inc(var_ready, 1)
                dve.wait_ge(root_done, i + 1)
                seq(dve.reciprocal(r, s))
                settle()
                seq(dve.tensor_tensor(y, r, r, ALU.mult))
                settle()
                seq(dve.scalar_tensor_tensor(st[:, 4, 0:cols], y, -0.5, a, ALU.mult, ALU.mult))
                settle()
                seq(dve.scalar_tensor_tensor(rr[:, 0:cols], st[:, 4, 0:cols], 1.5, r, ALU.add, ALU.mult))
                settle()

            def token_diag():
                for q in range(QT):
                    ins = dve.tensor_scalar(KD[:, q, :], ident[:], rr[:, q:q + 1], None, ALU.mult)
                ins.then_inc(diag_ready, 1)

            def norm_x(layer, j):
                if layer or j not in (12, 13):
                    dve.wait_ge(gain_ready, 4 * layer + j // GROUP + 1)
                if layer and j % 4 == 0:
                    dve.wait_ge(store[j // 4], 16)
                factors = (DS[:, 0, 0:SEQ], XB[:, 0:SEQ])[layer]
                dve.scalar_tensor_tensor(X[:, j, :], X[:, j, :], hgain[:, j:j + 1], factors,
                                         ALU.mult, ALU.mult).then_inc(xr_done, 1)

            def lower_h(layer, j):
                col = shift_col(layer, j)
                dve.wait_ge(xr_done, KC * layer + j + 1)
                dve.wait_ge(hhi_done, KC * layer + j + 1)
                dve.scalar_tensor_tensor(hlo[:, j, :], X[:, j, :], mod[:, col:col + 1],
                                         hhi[:, j, :].bitcast(F32), ALU.add, ALU.subtract).then_inc(hlo_done, 1)

            def make_h(layer, chunks, lead=2):
                for i in range(len(chunks) + lead):
                    if i < len(chunks):
                        norm_x(layer, chunks[i])
                    if i >= lead:
                        lower_h(layer, chunks[i - lead])

            def gate(w, t, g0, layer):
                i = KC * layer + now(w, t) - g0
                half, j = (w - g0) // HC, now(w, t) - g0 - HC * ((w - g0) // HC)
                src = (Y, X)[half] if layer == 0 else (X, Y)[half]
                factor = 0.25 if (layer == 1 and half == 1) else 0.5
                dve.wait_ge(tanh_done, i + 1)
                dve.scalar_tensor_tensor(SG[:, w % 2, :], T[:, w % 2, :], 1.0, Z[w % 2][:, 0:SEQ],
                                         ALU.add, ALU.mult).then_inc(z_free[w % 2], 1)
                if src is X and t is None:
                    dve.wait_ge(o_copied, i + 1 - HC * (1 + layer) if layer == 0 else HC + (w - g0) + 1)
                dve.wait_ge(z_free[w % 2], bank_uses(w, t) + 2)
                dve.scalar_tensor_tensor(SG[:, w % 2, :], flat(src[:, bass.ds(j, 1), :]), factor,
                                         SG[:, w % 2, :], ALU.mult, ALU.mult).then_inc(gated, 1)

            def split_gated(w, t, g0, layer):
                c = now(w, t) - g0
                dve.wait_ge(ghi_done, KC * layer + c + 1)
                dve.tensor_tensor(flat(glo[:, bass.ds(c, 1), :]), SG[:, w % 2, :],
                                  flat(ghi[:, bass.ds(c, 1), :]).bitcast(F32), ALU.subtract)\
                    .then_inc(glo_done, 1)

            def add_x(w, t, o0, layer):
                j = now(w, t) - o0
                second, seg = (w - o0) // HC, (w - o0) % HC
                dve.wait_ge(pe_half, 2 * now(w, t) + 2 + 4)
                gcol = GATE[layer] * HC
                seg = seg if t is None else seg + 2 * t
                x = VX[:, bass.ds(seg, 1), :] if second else U[:, bass.ds(seg, 1), PAD:PAD + SEQ]
                dve.scalar_tensor_tensor(flat(X[:, bass.ds(j, 1), :]), Z[w % 2][:, 0:SEQ],
                                         mod[:, bass.ds(gcol + j, 1)], flat(x),
                                         ALU.mult, ALU.add).then_inc(z_free[w % 2], 1)

            def pool_branch(g):
                win = 2 ** (g + 1)
                u = U[:, 2 * g:2 * g + 2, PAD - 16:PAD + SEQ]
                src, s, bufs = u, 1, (poolA, poolB)
                for lev in range(g + 1):
                    dst = bufs[lev % 2]
                    seq(dve.tensor_tensor(dst[:, :, s:SEQ + 16] if lev == 0 else dst[:, :, 2 * s - 1:SEQ + 16],
                                          src[:, :, s:SEQ + 16] if lev == 0 else src[:, :, 2 * s - 1:SEQ + 16],
                                          src[:, :, 0:SEQ + 16 - s] if lev == 0 else
                                          src[:, :, s - 1:SEQ + 16 - s], ALU.add))
                    settle()
                    src, s = dst, 2 * s
                d = Y[:, 2 * g:2 * g + 2, :]
                seq(dve.scalar_tensor_tensor(d, src[:, :, 16:], 1.0 / win, u[:, :, 16:], ALU.mult, ALU.subtract))
                settle()
                for c in range(2):
                    seq(dve.tensor_tensor(src[:, c, 16:16 + win], src[:, c, 16:16 + win], rc[:, 0:win], ALU.mult))
                settle()
                for c in range(2):
                    ins = dve.tensor_tensor(d[:, c, 0:win], src[:, c, 16:16 + win], u[:, c, 16:16 + win],
                                            ALU.subtract)
                    if c:
                        ins.then_inc(d_ready, 1)
                    else:
                        seq(ins)

            def attend(layer, i):
                if 0 <= i + 1 < HC:
                    a = HC * layer + i + 1
                    dve.wait_ge(kb_done, a + 1)
                    dve.scalar_tensor_tensor(X[:, HC + i + 1, :], X[:, HC + i + 1, :],
                                             par[:, C_QK + 2 * layer + 1:C_QK + 2 * layer + 2], M[:, 0:SEQ],
                                             ALU.mult, ALU.mult).then_inc(kmul, 1)
                if 0 <= i < HC:
                    a = HC * layer + i
                    dve.wait_ge(scored, a + 1)
                    dve.wait_ge(ds_ready, a + 1)
                    if a >= 2:
                        dve.wait_ge(pt_done, a - 1)
                    for q, (c0, c1) in enumerate(((0, P), (P, KEYS))):
                        ins = dve.scalar_tensor_tensor(SP[:, a % 2, c0:c1], S[a % 2][:, c0:c1],
                                                       rr[:, KC * q + i:KC * q + i + 1], DS[:, a % 2, c0:c1],
                                                       ALU.mult, ALU.add)
                        if q:
                            ins.then_inc(s_added, 1)
                        else:
                            seq(ins)
                if 0 <= i < HC:
                    settle()
                    dve.wait_ge(s_added, a0(layer, i) + 1)
                    for q, (c0, c1) in enumerate(((0, P), (P, KEYS))):
                        ins = dve.tensor_reduce(nm[:, i % 2, q:q + 1], SP[:, i % 2, c0:c1], AX_X, ALU.max,
                                                negate=True)
                        if q:
                            ins.then_inc(max_done, 1)
                        else:
                            seq(ins)

            def a0(layer, i):
                return HC * layer + i

            def divide(layer, i):
                if 0 <= i < HC:
                    a = HC * layer + i
                    dve.wait_ge(exp_done, 2 * (a + 1))
                    seq(dve.reciprocal(rl[:, i % 2, :], ls[:, i % 2, :]))
                    settle()
                    for q in range(QT):
                        ins = dve.tensor_scalar(PD[:, i % 2, q, :], ident[:], rl[:, i % 2, q:q + 1], None, ALU.mult)
                    ins.then_inc(pdiag, 1)

            plan = conv_plan()
            taps = [0]

            def conv(w):
                for j, k in plan.get(w, ()):
                    wcol = C_CW + j * CONV_WIDTH + k
                    if k == 0:
                        dve.wait_ge(u_done, max(4, j + 1))
                        ins = dve.tensor_scalar(Y[:, j, :], U[:, j, 0:SEQ], par[:, wcol:wcol + 1],
                                                par[:, C_CB + j:C_CB + j + 1], ALU.mult, ALU.add)
                    else:
                        dve.wait_ge(conv_seq, taps[0] - 1)
                        ins = dve.scalar_tensor_tensor(Y[:, j, :], U[:, j, k:k + SEQ], par[:, wcol:wcol + 1],
                                                       Y[:, j, :], ALU.mult, ALU.add)
                    ins.then_inc(conv_seq, 1)
                    taps[0] += 1

            dve.wait_ge(cexp, 1)
            seq(dve.tensor_scalar(ctmp[:], ctmp[:], 1.0, None, ALU.add))
            settle()
            seq(dve.reciprocal(ctmp[:], ctmp[:]))
            settle()
            seq(dve.tensor_tensor(cact[:], ctmp[:], par[:, C_C:C_C + KC], ALU.mult))
            dve.wait_ge(const, 5)
            seq(dve.reciprocal(rc[:], rc[:]))
            settle()
            def group_of_h(g):
                keep_piece(g)
                make_gain(0, g)
                make_h(0, range(GROUP * g, GROUP * (g + 1)))

            def first_half():
                dve.wait_ge(half_sum, 1)
                seq(keep_cols(3, 0, 4))
                settle()
                seq(gain_cols(0, 3, 0, 1))
                settle()
                make_h(0, range(12, 14))

            for p in range(3):
                dve.wait_ge(acc_zero, p + 1)
                add_units(UNITS * p, 4, None)
                if p:
                    group_of_h(p - 1)
                add_units(UNITS * p + 4, 4, None)
                if p:
                    lo(3 * p - 1, None)
                add_units(UNITS * p + 8, 4, None)
                lo(3 * p, None)
                add_units(UNITS * p + 12, 2, None)
                lo(3 * p + 1, None)
                add_units(UNITS * p + 14, 2, None)
                if p == 0:
                    dve.wait_ge(stat_done, KC)
                    rsqrt(0, QT, M[:, 0:QT], D_MODEL)
                    token_diag()
                    dve.wait_ge(r_copied, 1)
            dve.wait_ge(acc_zero, 4)
            half_units(48, 4)
            group_of_h(2)
            half_units(52, 4)
            lo(8, None)
            half_units(56, 4)
            lo(9, None)
            first_half()
            half_units(60, 2)
            lo(10, None)
            half_units(62, 2)
            keep_piece(3, first=4)
            make_gain(0, 3, h0=1)
            make_h(0, range(14, 16))
            lo(11, None)

            def plain(w, t):
                lo(w + AHEAD, t, (0,))
                units(w, t)
                lo(w + AHEAD, t, (1,))

            plain(10, None)
            plain(11, None)
            plain(12, None)
            dve.wait_ge(z_free[0], WIDE[0] // 2 + 1)
            pool_branch(0)
            plain(13, None)
            dve.wait_ge(z_free[1], WIDE[0] // 2 + 1)
            pool_branch(1)
            run(dve, 14, 16, plain)
            plain(16, None)
            dve.wait_ge(s_read, 4)
            pool_branch(2)
            plain(17, None)
            pool_branch(3)
            dve.wait_ge(acc_zero, 6)
            run(dve, 18, 20, plain)
            keep_piece(4)
            run(dve, 20, V0, plain)
            def attention_step(w, v0, g0, layer, more=None):
                i = w - v0 - 3
                lo(w + AHEAD, None, (0,))
                divide(layer, i - 1)
                if w == v0:
                    dve.wait_ge(qk_stat, 2 * HC * (layer + 1))
                    rsqrt(2 * layer + 1, 2 * KC, M[:, 0:2 * KC], P)
                    dve.sem_inc(rr_ready, 1)
                attend(layer, i)
                units(w, None)
                lo(w + AHEAD, None, (1,))
                if w > g0:
                    split_gated(w - 1, None, g0, layer)
                if w >= g0:
                    gate(w, None, g0, layer)

            for w in range(V0, G0 + 5):
                if w == V0 + 4:
                    keep_piece(5)
                attention_step(w, V0, G0, 0)

            def step_g(g0, layer):
                def step(w, t):
                    plain(w, t)
                    split_gated(w - 1, t, g0, layer)
                    gate(w, t, g0, layer)
                return step

            for w in range(37, O0):
                if w == 42:
                    keep_piece(6)
                step_g(G0, 0)(w, None)

            def step_o(o0, layer):
                def step(w, t):
                    last = w + AHEAD >= N_SLABS
                    if not last:
                        lo(w + AHEAD, t, (0,))
                    units(w, t)
                    add_x(w, t, o0, layer)
                    if not last:
                        lo(w + AHEAD, t, (1,))
                return step

            split_gated(O0 - 1, None, G0, 0)
            dve.wait_ge(mod_done, GATE[0] + 1)
            dve.wait_ge(xr_in[0], 16)
            step_o(O0, 0)(48, None)
            step_o(O0, 0)(49, None)
            keep_piece(7)
            step_o(O0, 0)(50, None)
            step_o(O0, 0)(51, None)
            dve.wait_ge(xr_in[1], 16)
            run(dve, 52, 56, step_o(O0, 0))
            dve.wait_ge(mod_done, GATE[0] + 2)
            dve.wait_ge(xr_in[2], 16)
            step_o(O0, 0)(56, None)
            step_o(O0, 0)(57, None)
            keep_piece(8)
            step_o(O0, 0)(58, None)
            step_o(O0, 0)(59, None)
            dve.wait_ge(xr_in[3], 16)
            run(dve, 60, 62, step_o(O0, 0))
            step_o(O0, 0)(62, None)
            lo(65, None, (0,))
            for g in range(3):
                make_gain(1, g)
            add_x(63, None, O0, 0)
            dve.wait_ge(stat_done, 2 * KC)
            rsqrt(2, QT, M[:, 0:QT], D_MODEL)
            token_diag()
            dve.wait_ge(spread, 2)
            make_h(1, range(0, 4))
            lo(65, None, (1,))
            units(63, None)
            units(64, None)
            make_h(1, range(4, 8))
            lo(66, None)
            units(65, None)
            lo(67, None)
            units(66, None)
            make_h(1, range(8, 12))
            lo(68, None)
            keep_piece(9)
            make_gain(1, 3)
            units(67, None)
            lo(69, None)
            make_h(1, range(12, 14))
            lo(70, None)
            units(68, None)
            make_h(1, range(14, 16))
            units(69, None)

            def conv_silu(w):
                for j in range(2 * (w - 116), 2 * (w - 115)):
                    dve.wait_ge(ln_act, j + 1)
                    dve.scalar_tensor_tensor(Y[:, j, :], U[:, j, 0:SEQ], 1.0, Y[:, j, :],
                                             ALU.add, ALU.mult).then_inc(ln_out, 1)

            for w in (71, 72):
                lo(w, None)
                units(w - 1, None)
            for pair in range(4):
                half_a, tanh_b = (T, SG)[pair % 2][:, 0, :], (T, SG)[pair % 2][:, 1, :]
                if pair < 2:
                    dve.wait_ge(z_free[pair], (AB1 + WIDE[1]) // 2 + 1)
                else:
                    dve.wait_ge(s_read, 4 + 2 * (pair - 1))
                dve.scalar_tensor_tensor(U[:, pair, PAD:PAD + SEQ], tanh_b, 1.0, half_a,
                                         ALU.add, ALU.mult).then_inc(u_done, 1)
            lo(73, None)

            def second_layer_step(w):
                if w < V1:
                    plain(w, None)
                else:
                    attention_step(w, V1, G1, 1)

            for w in range(AB1 + WIDE[1], 117):
                if w == 111:
                    dve.wait_ge(mean_mm, 1)
                    for j in range(HC):
                        seq(dve.scalar_tensor_tensor(Y[:, j, :], XB[:, 0:SEQ], -1.0 / HALF, Y[:, j, :],
                                                     ALU.mult, ALU.add))
                    settle()
                    dve.sem_inc(ln_sub, 1)
                if w == 114:
                    dve.wait_ge(var_mm, 1)
                    rsqrt(4, QT, XB[:, 0:QT], HALF)
                    token_diag()
                if w == 115:
                    dve.wait_ge(spread, 3)
                    for j in range(HC):
                        dve.tensor_tensor(Y[:, j, :], Y[:, j, :], XB[:, 0:SEQ], ALU.mult).then_inc(ln_mul, 1)
                second_layer_step(w)
                if w == 116:
                    conv_silu(w)
                if w < QI1 and w % 2:
                    j = (w - AB1) // 2
                    dve.wait_ge(z_free[1], w // 2 + 2)
                    dve.wait_ge(z_free[0], w // 2 + 2)
                    dve.scalar_tensor_tensor(U[:, j, PAD:PAD + SEQ], T[:, 1, :], 1.0, T[:, 0, :],
                                             ALU.add, ALU.mult).then_inc(u_done, 1)
                conv(w)
                if w == 85:
                    dve.wait_ge(wt_done, 1)
                    seq(dve.tensor_scalar(wi[:], XB[:, 0:SEQ].rearrange("p (a b) -> p a b", a=QT)
                                          [:, :, IDX_DIM:IDX_DIM + IDX_HEADS],
                                          float(IDX_HEADS) ** -0.5, None, ALU.mult))
                    settle()
                if 86 <= w < 94:
                    hh = w - 86
                    dve.wait_ge(relu, hh + 1)
                    if hh == 0:
                        dve.wait_ge(cm_ready, 2)
                    else:
                        dve.wait_ge(score, 2 * hh)
                    for q, (c0, c1) in enumerate(((0, P), (P, KEYS))):
                        dve.scalar_tensor_tensor(PTs[:, 0, c0:c1], SP[:, hh % 2, c0:c1], wi[:, q, hh:hh + 1],
                                                 PTs[:, 0, c0:c1], ALU.mult, ALU.add).then_inc(score, 1)
                if 94 <= w < 98:
                    if w == 94:
                        dve.wait_ge(score, 2 * IDX_HEADS)
                    for r in range(2):
                        for q, (c0, c1) in enumerate(((0, P), (P, KEYS))):
                            seq(dve.max(m8[:, q, :], PTs[:, r, c0:c1]))
                        settle()
                        for q, (c0, c1) in enumerate(((0, P), (P, KEYS))):
                            seq(dve.match_replace(PTs[:, 1 - r, c0:c1], m8[:, q, :], PTs[:, r, c0:c1], -3e38))
                        settle()
                if w == 98:
                    seq(dve.tensor_scalar(MK[:], PTs[:, 0, :], -2e38, -BIG, ALU.is_ge, ALU.mult))
                    settle()
                    dve.tensor_tensor(MK[:], MK[:], D[:], ALU.add).then_inc(mask_ready, 1)

            for w in range(117, O1):
                if w == 124:
                    keep_piece(10)
                plain(w, None)
                if w < 120:
                    conv_silu(w)
                split_gated(w - 1, None, G1, 1)
                gate(w, None, G1, 1)
            split_gated(O1 - 1, None, G1, 1)
            for half in range(2):
                w0 = O1 + HC * half
                dve.wait_ge(xr_in[2 * half], 32)
                if half:
                    lo(w0 + AHEAD, None)
                    keep_piece(11)
                dve.wait_ge(mod_done, GATE[1] + half + 1)
                if half:
                    add_x(w0, None, O1, 1)
                else:
                    step_o(O1, 1)(w0, None)
                for w in range(w0 + 1, w0 + 4):
                    step_o(O1, 1)(w, None)
                dve.wait_ge(xr_in[2 * half + 1], 32)
                for w in range(w0 + 4, w0 + HC):
                    step_o(O1, 1)(w, None)


def kernel(**inputs):
    import numpy as np
    import concourse.bacc as bacc
    from concourse.bass_utils import run_bass_kernel_spmd

    def slabs(w):
        k, n = w.shape
        return w.reshape(k // P, P, n // P, P).transpose(2, 1, 0, 3)

    def cols(v):
        return v.reshape(-1, P).T

    od = inputs["od_w_in"][0]
    q, k, v = od[:, 0:HALF], od[:, HALF:2 * HALF], od[:, 2 * HALF:3 * HALF]
    at = 3 * HALF
    qi = od[:, at:at + IDX_HEADS * IDX_DIM]
    at += IDX_HEADS * IDX_DIM
    wi, ki = od[:, at:at + IDX_HEADS], od[:, at + IDX_HEADS:at + IDX_HEADS + IDX_DIM]
    at += IDX_HEADS + IDX_DIM
    ga, gb, g = od[:, at:at + HALF], od[:, at + HALF:at + 2 * HALF], od[:, at + 2 * HALF:]
    ab = np.stack([slabs(ga), slabs(gb)], axis=1).reshape(2 * HC, P, KC, P)
    kw = np.concatenate([ki] + [wi] * (IDX_DIM // IDX_HEADS), axis=1)
    w_slabs = np.concatenate([slabs(inputs["ev_w_in"][0]), slabs(inputs["w_out"][0]), ab, slabs(qi), slabs(kw),
                              slabs(q), slabs(k), slabs(v), slabs(g), slabs(inputs["w_out"][1])])
    def by_token(v):
        return v.reshape(HC // 2, 2, P, KC, P).transpose(0, 2, 3, 1, 4).reshape(HC // 2, P, 2, KC, P)\
            .transpose(0, 2, 1, 3, 4).reshape(HC, P, KC, P)

    def wide(first):
        return first.transpose(2, 0, 1, 3).reshape(len(first), KC, P, P).transpose(0, 2, 1, 3)

    w_slabs = np.concatenate([wide(w_slabs[:WIDE[0]]), w_slabs[WIDE[0]:V0], by_token(w_slabs[V0:G0]), w_slabs[G0:AB1],
                              wide(w_slabs[AB1:AB1 + WIDE[1]]), w_slabs[AB1 + WIDE[1]:V1], by_token(w_slabs[V1:G1]),
                              w_slabs[G1:]])

    def piece(a, kind, layer, n):
        if kind == "gate":
            return a[layer][..., 2 * D_MODEL + PIECE * n:2 * D_MODEL + PIECE * (n + 1)]
        parts = []
        for at in (GROUP * P * n, GROUP * P * n + 2 * P):
            parts += [a[layer][..., D_MODEL + at:D_MODEL + at + 2 * P], a[layer][..., at:at + 2 * P]]
        return np.concatenate(parts, axis=-1)

    def two_rows(units):
        return units.reshape(UNITS // 2, 2, P, 2, PIECE // 2).transpose(3, 0, 2, 1, 4).reshape(UNITS, P, PIECE)

    pieces = [piece(inputs["ada_w"], *which).reshape(UNITS, P, PIECE) for which in PIECES]
    pieces[3] = two_rows(pieces[3])
    ada_units = np.concatenate(pieces)
    params = np.concatenate(
        [cols(inputs["c"]), cols(inputs["norm_g"])] + [cols(piece(inputs["ada_b"], *which)) for which in PIECES]
        + [cols(inputs["pool_scale"]), cols(inputs["moba_qn"]), cols(inputs["moba_kn"]),
           cols(inputs["dsa_qn"]), cols(inputs["dsa_kn"]),
           inputs["conv_w"][0].reshape(CONV_WIDTH, HC, P).transpose(2, 1, 0).reshape(P, HC * CONV_WIDTH),
           cols(inputs["conv_b"]), cols(inputs["conv_ln_g"]), cols(inputs["conv_ln_b"])], axis=1)
    arrays = {
        "xT": inputs["x"][0].T.reshape(KC, P, SEQ).transpose(1, 0, 2),
        "params": params,
        "pool_w": inputs["pool_w"][0].reshape(4, 2, P, 2 * P).transpose(2, 0, 1, 3),
        "w_slabs": w_slabs,
        "ada_units": ada_units,
    }
    arrays = {name: np.ascontiguousarray(a) for name, a in arrays.items()}

    nc = bacc.Bacc("TRN2", target_bir_lowering=False, num_devices=1)
    args = [nc.dram_tensor(name, a.shape, F32, kind="ExternalInput").ap() for name, a in arrays.items()]
    args.append(nc.dram_tensor("x1_dram", (P, KC, SEQ), F32, kind="Internal").ap())
    args.append(nc.dram_tensor("outT", (P, KC, SEQ), F32, kind="ExternalOutput").ap())
    build(nc, *args)
    r = run_bass_kernel_spmd(nc, [arrays], core_ids=[0])
    outT = r.results[0]["outT"]
    return np.ascontiguousarray(outT.transpose(1, 0, 2).reshape(D_MODEL, SEQ).T)[None]
```
